# Optimizing a Trainium2 kernel written in Bass

```python
import math
import jax, jax.numpy as jnp
from jax import lax
import numpy as np

D_MODEL = 1024
BATCH = 1
SEQ = 512
DEPTH = 1

N_HEADS = 8
HEAD_DIM = 64
ATTN_WIDTH = N_HEADS * HEAD_DIM
MOBA_BLOCK = 256
MOBA_TOPK = 3
Q_CHUNK = 128
SSM_GROUP = 16
SSM_GROUPS = 32
SSM_WIDTH = SSM_GROUP * SSM_GROUPS
SSM_STATE = 64
DT_MIN = 1e-3
DT_MAX = 1e-1
D_FF = 2816
EPS = 1e-6
IN_WIDTH = 3 * ATTN_WIDTH + SSM_WIDTH + 2 * D_MODEL
SPLIT_POINTS = (ATTN_WIDTH, 2 * ATTN_WIDTH, 3 * ATTN_WIDTH, 3 * ATTN_WIDTH + SSM_WIDTH,
                3 * ATTN_WIDTH + SSM_WIDTH + D_MODEL)

kernel_name = "hybrid_moba_s5_macaron"

def rms_norm(x, g):
    xf = x.astype(jnp.float32)
    y = xf * lax.rsqrt(jnp.mean(xf * xf, axis=-1, keepdims=True) + EPS)
    return (y * g.astype(jnp.float32)).astype(x.dtype)

def swiglu(h, w_gate, w_up, w_down):
    return (jax.nn.silu(h @ w_gate) * (h @ w_up)) @ w_down

def alibi_slopes(n_heads):
    return jnp.asarray(2.0 ** (-8.0 * np.arange(1, n_heads + 1) / n_heads), dtype=jnp.float32)

def moba_attention(q, k, v):
    B, H, S, Dh = q.shape
    nb = -(-S // MOBA_BLOCK)
    pad = nb * MOBA_BLOCK - S
    qf = q.astype(jnp.float32)
    kp = jnp.pad(k.astype(jnp.float32), ((0, 0), (0, 0), (0, pad), (0, 0)))
    vp = jnp.pad(v.astype(jnp.float32), ((0, 0), (0, 0), (0, pad), (0, 0)))
    kb = kp.reshape(B, H, nb, MOBA_BLOCK, Dh)
    vb = vp.reshape(B, H, nb, MOBA_BLOCK, Dh)
    k_mean = jnp.mean(kb, axis=3)
    gate = jnp.einsum('bhsd,bhnd->bhsn', qf, k_mean)
    own_blk = jnp.arange(S) // MOBA_BLOCK
    past = jnp.arange(nb)[None, :] < own_blk[:, None]
    gate = jnp.where(past[None, None], gate, -jnp.inf)
    k_sel = min(MOBA_TOPK, nb)
    _, sel = lax.top_k(gate, k_sel)
    scale = HEAD_DIM ** -0.5
    slopes = alibi_slopes(H)
    bi = jnp.arange(B)[:, None, None, None]
    hi = jnp.arange(H)[None, :, None, None]
    n_chunks = S // Q_CHUNK

    def chunk(c):
        t0 = c * Q_CHUNK
        qc = lax.dynamic_slice_in_dim(qf, t0, Q_CHUNK, axis=2)
        selc = lax.dynamic_slice_in_dim(sel, t0, Q_CHUNK, axis=2)
        tq = t0 + jnp.arange(Q_CHUNK)
        blk = t0 // MOBA_BLOCK
        k_own = lax.dynamic_index_in_dim(kb, blk, axis=2, keepdims=False)
        v_own = lax.dynamic_index_in_dim(vb, blk, axis=2, keepdims=False)
        s_own = blk * MOBA_BLOCK + jnp.arange(MOBA_BLOCK)
        dist_own = (tq[:, None] - s_own[None, :])
        sc_own = jnp.einsum('bhqd,bhkd->bhqk', qc, k_own) * scale
        sc_own = sc_own - slopes[:, None, None] * jnp.abs(dist_own).astype(jnp.float32)
        sc_own = jnp.where((dist_own >= 0)[None, None], sc_own, -jnp.inf)
        k_g = kb[bi, hi, selc]
        v_g = vb[bi, hi, selc]
        sc_sel = jnp.einsum('bhqd,bhqnkd->bhqnk', qc, k_g) * scale
        s_pos = selc[..., None] * MOBA_BLOCK + jnp.arange(MOBA_BLOCK)
        dist_sel = jnp.abs(tq[:, None, None] - s_pos).astype(jnp.float32)
        sc_sel = sc_sel - slopes[:, None, None, None] * dist_sel
        valid = selc < blk
        sc_sel = jnp.where(valid[..., None], sc_sel, -jnp.inf)
        scores = jnp.concatenate(
            [sc_own, sc_sel.reshape(B, H, Q_CHUNK, k_sel * MOBA_BLOCK)], axis=-1)
        p = jax.nn.softmax(scores, axis=-1)
        p_own = p[..., :MOBA_BLOCK]
        p_sel = p[..., MOBA_BLOCK:].reshape(B, H, Q_CHUNK, k_sel, MOBA_BLOCK)
        return (jnp.einsum('bhqk,bhkd->bhqd', p_own, v_own)
                + jnp.einsum('bhqnk,bhqnkd->bhqd', p_sel, v_g))

    outs = lax.map(chunk, jnp.arange(n_chunks))
    out = outs.transpose(1, 2, 0, 3, 4).reshape(B, H, S, Dh)
    return out.astype(q.dtype)

def s5_ssm(u, lam_re, lam_im, log_dt, b_re, b_im, c_re, c_im, d_skip):
    Bt, S, _ = u.shape
    uf = u.astype(jnp.float32).reshape(Bt, S, SSM_GROUPS, SSM_GROUP)
    lam_re = lam_re.astype(jnp.float32)
    lam_im = lam_im.astype(jnp.float32)
    dt = jnp.exp(log_dt.astype(jnp.float32))[:, None]
    mag = jnp.exp(lam_re * dt)
    ab_r = mag * jnp.cos(lam_im * dt)
    ab_i = mag * jnp.sin(lam_im * dt)
    num_r = ab_r - 1.0
    num_i = ab_i
    den = lam_re * lam_re + lam_im * lam_im
    f_r = (num_r * lam_re + num_i * lam_im) / den
    f_i = (num_i * lam_re - num_r * lam_im) / den
    br = b_re.astype(jnp.float32)
    bim = b_im.astype(jnp.float32)
    bb_r = f_r[..., None] * br - f_i[..., None] * bim
    bb_i = f_r[..., None] * bim + f_i[..., None] * br
    xr = jnp.einsum('bsgh,gph->bsgp', uf, bb_r)
    xi = jnp.einsum('bsgh,gph->bsgp', uf, bb_i)
    a_r = jnp.broadcast_to(ab_r, xr.shape)
    a_i = jnp.broadcast_to(ab_i, xr.shape)

    def combine(e1, e2):
        a1r, a1i, b1r, b1i = e1
        a2r, a2i, b2r, b2i = e2
        return (a2r * a1r - a2i * a1i,
                a2r * a1i + a2i * a1r,
                a2r * b1r - a2i * b1i + b2r,
                a2r * b1i + a2i * b1r + b2i)

    _, _, hr, hi = lax.associative_scan(combine, (a_r, a_i, xr, xi), axis=1)
    y = (jnp.einsum('bsgp,ghp->bsgh', hr, c_re.astype(jnp.float32))
         - jnp.einsum('bsgp,ghp->bsgh', hi, c_im.astype(jnp.float32))
         + d_skip.astype(jnp.float32).reshape(SSM_GROUPS, SSM_GROUP) * uf)
    return y.reshape(Bt, S, SSM_WIDTH)

def setup_inputs(seed: int = 0) -> dict:
    key = jax.random.key(seed)
    ks = jax.random.split(key, 32)
    L = DEPTH
    f32 = jnp.float32

    def w(k, shape, fan_in):
        return jax.random.normal(k, shape, f32) * fan_in ** -0.5

    def gain(k, shape):
        return 1.0 + 0.02 * jax.random.normal(k, shape, f32)

    n = jnp.arange(SSM_STATE, dtype=f32)
    lam_re = -0.5 + 0.01 * jax.random.normal(ks[10], (L, SSM_GROUPS, SSM_STATE), f32)
    lam_im = math.pi * n + 0.01 * jax.random.normal(ks[11], (L, SSM_GROUPS, SSM_STATE), f32)
    log_dt = jax.random.uniform(ks[12], (L, SSM_GROUPS), f32, math.log(DT_MIN), math.log(DT_MAX))
    return {
        "x": jax.random.normal(ks[0], (BATCH, SEQ, D_MODEL), f32),
        "ffn1_norm": gain(ks[1], (L, D_MODEL)),
        "ffn1_w_gate": w(ks[2], (L, D_MODEL, D_FF), D_MODEL),
        "ffn1_w_up": w(ks[3], (L, D_MODEL, D_FF), D_MODEL),
        "ffn1_w_down": w(ks[4], (L, D_FF, D_MODEL), D_FF),
        "mix_norm": gain(ks[5], (L, D_MODEL)),
        "w_in": w(ks[6], (L, D_MODEL, IN_WIDTH), D_MODEL),
        "w_attn_up": w(ks[7], (L, ATTN_WIDTH, D_MODEL), ATTN_WIDTH),
        "ssm_lambda_re": lam_re,
        "ssm_lambda_im": lam_im,
        "ssm_log_dt": log_dt,
        "ssm_b_re": w(ks[13], (L, SSM_GROUPS, SSM_STATE, SSM_GROUP), 2 * SSM_GROUP),
        "ssm_b_im": w(ks[14], (L, SSM_GROUPS, SSM_STATE, SSM_GROUP), 2 * SSM_GROUP),
        "ssm_c_re": w(ks[15], (L, SSM_GROUPS, SSM_GROUP, SSM_STATE), 2 * SSM_STATE),
        "ssm_c_im": w(ks[16], (L, SSM_GROUPS, SSM_GROUP, SSM_STATE), 2 * SSM_STATE),
        "ssm_d": jax.random.normal(ks[17], (L, SSM_WIDTH), f32),
        "w_ssm_glu": w(ks[18], (L, SSM_WIDTH, 2 * D_MODEL), SSM_WIDTH),
        "w_out": w(ks[19], (L, D_MODEL, D_MODEL), D_MODEL),
        "ffn2_norm": gain(ks[20], (L, D_MODEL)),
        "ffn2_w_gate": w(ks[21], (L, D_MODEL, D_FF), D_MODEL),
        "ffn2_w_up": w(ks[22], (L, D_MODEL, D_FF), D_MODEL),
        "ffn2_w_down": w(ks[23], (L, D_FF, D_MODEL), D_FF),
        "final_norm": gain(ks[24], (D_MODEL,)),
    }

def reference(x, ffn1_norm, ffn1_w_gate, ffn1_w_up, ffn1_w_down, mix_norm, w_in, w_attn_up,
              ssm_lambda_re, ssm_lambda_im, ssm_log_dt, ssm_b_re, ssm_b_im, ssm_c_re, ssm_c_im,
              ssm_d, w_ssm_glu, w_out, ffn2_norm, ffn2_w_gate, ffn2_w_up, ffn2_w_down,
              final_norm):
    B, S, _ = x.shape
    for l in range(DEPTH):
        h = rms_norm(x, ffn1_norm[l])
        x = x + 0.5 * swiglu(h, ffn1_w_gate[l], ffn1_w_up[l], ffn1_w_down[l])
        h = rms_norm(x, mix_norm[l])
        proj = h @ w_in[l]
        q, k, v, u, g_attn, g_ssm = jnp.split(proj, SPLIT_POINTS, axis=-1)
        q = q.reshape(B, S, N_HEADS, HEAD_DIM).transpose(0, 2, 1, 3)
        k = k.reshape(B, S, N_HEADS, HEAD_DIM).transpose(0, 2, 1, 3)
        v = v.reshape(B, S, N_HEADS, HEAD_DIM).transpose(0, 2, 1, 3)
        attn = moba_attention(q, k, v).transpose(0, 2, 1, 3).reshape(B, S, ATTN_WIDTH)
        attn = attn @ w_attn_up[l]
        y = s5_ssm(u, ssm_lambda_re[l], ssm_lambda_im[l], ssm_log_dt[l], ssm_b_re[l],
                   ssm_b_im[l], ssm_c_re[l], ssm_c_im[l], ssm_d[l]).astype(x.dtype)
        y_val, y_gate = jnp.split(jax.nn.gelu(y) @ w_ssm_glu[l], 2, axis=-1)
        ssm_out = y_val * jax.nn.sigmoid(y_gate)
        merged = jax.nn.sigmoid(g_attn) * attn + jax.nn.sigmoid(g_ssm) * ssm_out
        x = x + merged @ w_out[l]
        h = rms_norm(x, ffn2_norm[l])
        x = x + 0.5 * swiglu(h, ffn2_w_gate[l], ffn2_w_up[l], ffn2_w_down[l])
    return rms_norm(x, final_norm)


_drawn_inputs = setup_inputs


def setup_inputs(seed=0):
    import zlib

    import numpy as np

    out = dict(_drawn_inputs(seed))
    spreads = {}
    factors = {'ffn1_norm': 6.06,
     'mix_norm': 8.0,
     'ssm_lambda_re': 64.0,
     'ssm_lambda_im': 42.76,
     'ssm_log_dt': 44.16,
     'ssm_b_re': 61.216,
     'ssm_b_im': 62.296,
     'ssm_c_re': 60.176,
     'ssm_c_im': 61.352,
     'ffn2_norm': 7.618,
     'final_norm': 8.142}
    for name, (base, spread) in spreads.items():
        noise = np.random.default_rng([zlib.crc32(name.encode()), seed]).standard_normal(out[name].shape)
        drawn = base * np.exp(spread * noise) if base else spread * noise
        out[name] = __import__('jax').numpy.asarray(drawn.astype(out[name].dtype))
    for name, factor in factors.items():
        out[name] = (out[name] * factor).astype(out[name].dtype)
    return out
```

```python
from contextlib import ExitStack

import concourse.bass as bass
from concourse import mybir

ALU = mybir.AluOpType
ACT = mybir.ActivationFunctionType
F32 = mybir.dt.float32
F32R = mybir.dt.float32r

P = 128
D, S, F = 1024, 512, 2816
DT, FT = D // P, F // P
H, HD = 8, 64
AW = H * HD
AT = AW // P
G, GH, NS = 32, 16, 64
T = 8
C = S // T
QT = S // P
EPS = 1e-6

DOWN_PARTS = ((0, 8), (8, 15), (15, 22))
UP0 = (0, 124)
DN0 = (44, 168)
PRJ0, MRG0, OUT0, CHUNKS = 68, 84, 116, 192
RAW = 4
HL = 2

NA, NB = T + 1, 8
NK = NA + 2 * NB
PI = 3.141592653589793
MAGIC = 12582912.0
TWO_PI = (6.28125, 0.0019340515136718750, 1.2556659146e-06)

BASE = 16512
X_AT = BASE
AH_AT = X_AT + DT * S * 4
RAW_AT = AH_AT + 2 * DT * S * 4
HL_AT = RAW_AT + RAW * D * 4
HID_AT = HL_AT + 2 * HL * D * 4
SPARE_AT = HID_AT + 2 * FT * S * 4
SPARE = 18432
WORK_AT = SPARE_AT + SPARE


def hybrid(nc, x, gains, w_up, w_down, w_proj, w_merge, w_out, lam_re, lam_im, log_dt, b_own,
           b_swap, c_own, c_swap, ssm_d, ident_in, multiples_in, signs_in, dist_in, out):
    with ExitStack() as ctx:
        at = [WORK_AT]

        def place(name, shape, offset, dt=F32):
            return nc.alloc_sbuf_tensor_at(name, shape, dt, offset=offset)

        def work(name, shape, dt=F32):
            n = 4
            for s in shape[1:]:
                n *= s
            n = -(-n // 32) * 32
            at[0] += n
            assert at[0] <= 229344, at[0]
            return place(name, shape, at[0] - n, dt)

        def sem(name):
            return ctx.enter_context(nc.semaphore(name))

        xT = place("xT", [P, DT, S], X_AT)
        ah = place("ah", [P, DT, S], AH_AT, F32R)
        al = place("al", [P, DT, S], AH_AT + DT * S * 4, F32R)
        xg = place("xg", [P, DT, S], AH_AT)
        raw = place("raw", [P, RAW, D], RAW_AT)
        wh = place("wh", [P, HL, D], HL_AT, F32R)
        wl = place("wl", [P, HL, D], HL_AT + HL * D * 4, F32R)
        gs = work("gs", [P, 2, S])
        sg = work("sg", [P, 2, S])
        us = work("us", [P, S])
        hid = work("hid", [P, 2, S])
        rstd = work("rstd", [P, S])
        acc = work("acc", [P, S])
        sq = work("sq", [P, S])
        ident = work("ident", [P, P])
        ones = work("ones", [P, P])
        gain = work("gain", [P, 4, DT])
        eps = work("eps", [P, 1])
        signs = work("signs", [P, 2])
        mx = work("mx", [P, QT * H])
        nmx = work("nmx", [P, QT * H])
        sums = work("sums", [P, QT * H])
        rec = work("rec", [P, QT * H])
        mag8 = work("mag8", [P, G])

        hp = place("hp", [P, FT, 2, S], HID_AT, F32R)

        PX = HID_AT + 13 * 2 * S * 4
        PY = PX + G * NA * GH * 4
        winT = place("winT", [P, G, T, GH], PX)
        ce_w = place("ce_w", [P, G, NA, GH], PX)
        tmpW = place("tmpW", [P, G, T, GH], PY)
        tmpC = place("tmpC", [P, G, NA, GH], PY)
        winS = place("winS", [P, G, P], PY)
        cosS = place("cosS", [P, G, NB, NB], PY)
        sinS = place("sinS", [P, G, NB, NB], PY + 8192)
        tmpR = place("tmpR", [P, 8, NB, NB], PY + 16384)
        ktS = place("ktS", [GH, G, NB, GH], PY)
        dB = place("dB", [GH, G, GH], PX)
        ang = place("ang", [P, G, NK], PX)
        tn = place("tn", [P, G * NK], PX + 4 * G * NK)
        mag = place("mag", [P, G, NA], PX + 8 * G * NK)
        expo = place("expo", [P, G, NA], PX + 8 * G * NK + 4 * G * NA)
        mult = place("mult", [P, NK], PX + 8 * G * NK + 8 * G * NA)
        bO = place("bO", [P, G, GH], PY)
        bS = place("bS", [P, G, GH], PY + 2048)
        cR = place("cR", [P, G, GH], PY + 4096)
        tmpB = place("tmpB", [P, G, GH], PY + 6144)
        small = place("small", [P, 24, G], PY + 8192)
        sn = place("sn", [P, G, NK], SPARE_AT)
        cs = place("cs", [P, G, NK], SPARE_AT + 4 * G * NK)
        s2 = SPARE_AT + 8 * G * NK
        er = place("er", [P, G, NA], s2)
        ei = place("ei", [P, G, NA], s2 + 4 * G * NA)
        s3 = s2 + 8 * G * NA
        bb = place("bb", [P, G, GH], s3)
        bbS = place("bbS", [P, G, GH], s3 + 2048)
        cO = place("cO", [P, G, GH], s3 + 4096)
        cA = place("cA", [P, G, GH], s3 + 6144)

        R = HID_AT
        prj = place("prj", [P, 4 * AT, S], R)
        uc = place("uc", [P, G, C], R)
        win = place("win", [P, G, P], R + 32768)
        zg = place("zg", [P, G, C], R + 32768)
        zx = place("zx", [P, G, C], R + 40960)
        y_ = place("y_", [P, 2, T, P], R + 32768)
        ce = place("ce", [P, G, NA, GH], R + 49152)
        yh = place("yh", [P, AT, S], R + 49152, F32R)
        yl = place("yl", [P, AT, S], R + 57344, F32R)
        u_ = place("u_", [C, G, T, GH], R + 67584)
        toep = place("toep", [P, G, P], R + 67584)
        cosT = place("cosT", [P, G, C], R + 83968)
        sinT = place("sinT", [P, G, C], R + 92160)
        hs = place("hs", [P, G, C], R + 100352)
        bias = [place("biasA", [P, 4, S], R + 40960), place("biasB", [P, 4, S], R + 67584)]
        v_ = place("v_", [P, QT, AW], R + 83968)
        sc = place("sc", [P, 3, S], R + 92160)
        pts = [place("pts0", [P, S], R + 98304), place("pts1", [P, S], R + 106496)]
        pr = place("pr", [P, 3, S], R + 100352)
        ao = place("ao", [P, 2, AW], R + 32768)
        th = place("th", [P, AT, S], R, F32R)
        tl = place("tl", [P, AT, S], R + 24576, F32R)
        mh = place("mh", [P, DT, S], R + 8192, F32R)
        ml = place("ml", [P, DT, S], R + 67584, F32R)
        dist = place("dist", [P, S], R + 36864)

        def scratch(name, shape):
            return nc.dram_tensor(name, shape, F32, kind="Internal").ap()

        win_d = scratch("win_d", [P, G * P])
        ce_d = scratch("ce_d", [P, G * NA * GH])
        cos_d = scratch("cos_d", [P, G * C])
        sin_d = scratch("sin_d", [P, G * C])
        kt_d = scratch("kt_d", [GH, G * P])

        bank = [ctx.enter_context(nc.psum_tensor(f"bank{i}", [P, S], F32)) for i in range(8)]

        landed = [sem(f"landed{i}") for i in range(RAW)]
        hi_ready = sem("hi_ready")
        lo_ready = sem("lo_ready")
        chunk_done = sem("chunk_done")
        x_in = [sem(f"x_in{i}") for i in range(4)]
        c_in = sem("c_in")
        s_in = sem("s_in")
        set_up = sem("set_up")
        x_new = sem("x_new")
        sq_ready, acc_ready = sem("sq_ready"), sem("acc_ready")
        ah_ready, al_ready = sem("ah_ready"), sem("al_ready")
        ss_ready, rt_ready, rstd_ready = sem("ss_ready"), sem("rt_ready"), sem("rstd_ready")
        gate_out, up_out = sem("gate_out"), sem("up_out")
        silu_ready, hid_ready = sem("silu_ready"), sem("hid_ready")
        hh_ready, hl_ready = sem("hh_ready"), sem("hl_ready")
        cd = sem("cd")
        ca = sem("ca")
        cp = sem("cp")
        prep_dve = sem("prep_dve")
        prep_act = sem("prep_act")
        winT_ready, winT_turned, win_out = sem("winT_ready"), sem("winT_turned"), sem("win_out")
        ce_ready, kt_done, kt_out = sem("ce_ready"), sem("kt_done"), sem("kt_out")
        stored = sem("stored")
        tab_in = [sem(f"tab_in{i}") for i in range(4)]
        toep_in = sem("toep_in")
        d_in = sem("d_in")
        dist_in_s = sem("dist_in_s")
        prj_out = sem("prj_out")
        tu_done, u_act, u_dve = sem("tu_done"), sem("u_act"), sem("u_dve")
        tc_done, uc_act, uc_dve = sem("tc_done"), sem("uc_act"), sem("uc_dve")
        z_done, zx_ready, zx_sin, zg_ready = sem("z_done"), sem("zx_ready"), sem("zx_sin"), sem("zg_ready")
        scan_ready, gx_ready, gx_sin, hs_ready = sem("scan_ready"), sem("gx_ready"), sem("gx_sin"), sem("hs_ready")
        y_done, gelu_ready = sem("y_done"), sem("gelu_ready")
        tv_done, v_out = sem("tv_done"), sem("v_out")
        ty_done, yh_ready, yl_ready = sem("ty_done"), sem("yh_ready"), sem("yl_ready")
        bias_ready = sem("bias_ready")
        sc_done, nmx_ready, exp_ready = sem("sc_done"), sem("nmx_ready"), sem("exp_ready")
        pt_done, pt_out, pv_done = sem("pt_done"), [sem("pt_out0"), sem("pt_out1")], sem("pv_done")
        ao_ready, at_done, th_ready, tl_ready = sem("ao_ready"), sem("at_done"), sem("th_ready"), sem("tl_ready")
        ga_out, gs_out, sga_ready, sgs_ready, sgy_ready = (sem("ga_out"), sem("gs_out"), sem("sga_ready"),
                                                           sem("sgs_ready"), sem("sgy_ready"))
        me = sem("me")
        ma_ready, mg_ready, mh_ready, ml_ready = sem("ma_ready"), sem("mg_ready"), sem("mh_ready"), sem("ml_ready")
        xg_ready, fin_dve, fin_pool, out_done = sem("xg_ready"), sem("fin_dve"), sem("fin_pool"), sem("out_done")

        class Count:

            def __init__(self, s):
                self.s, self.n = s, 0

            def step(self, ins):
                self.n += 1
                ins.then_inc(self.s, 1)

            def link(self, eng, ins):
                self.step(ins)
                eng.wait_ge(self.s, self.n)

        def split_hi(act, c, slot, kts, first=False):
            act.wait_ge(landed[slot % RAW], 16 * (c // RAW + 1) if isinstance(c, int) else (c - slot % RAW) * (16 // RAW) + 16)
            if not first:
                act.wait_ge(chunk_done, c - 1)
            act.activation(wh[:, slot % HL, 0:kts * P], raw[:, slot % RAW, 0:kts * P], ACT.Copy).then_inc(hi_ready, 1)

        def split_lo(dve, c, slot, kts):
            dve.wait_ge(hi_ready, c + 1)
            dve.tensor_tensor(wl[:, slot % HL, 0:kts * P], raw[:, slot % RAW, 0:kts * P],
                              wh[:, slot % HL, 0:kts * P].bitcast(F32), ALU.subtract).then_inc(lo_ready, 1)

        def w_tile(slot, k):
            return wh[:, slot % HL, k * P:(k + 1) * P], wl[:, slot % HL, k * P:(k + 1) * P]

        def three(pe, ps, slot, k, r_hi, r_lo, first, last):
            w_hi, w_lo = w_tile(slot, k)
            pe.matmul(ps, w_hi, r_hi, start=first, stop=False)
            pe.matmul(ps, w_hi, r_lo, start=False, stop=False)
            return pe.matmul(ps, w_lo, r_hi, start=False, stop=last)

        def norm_act(act, n, i):
            if n == 0:
                act.wait_ge(x_in[i // 2], 16)
            else:
                act.wait_ge(x_new, 8 * (n - 1) + i + 1)
            if n < 3:
                act.activation(ah[:, i, :], xT[:, i, :], ACT.Copy, scale=gain[:, n, i:i + 1]).then_inc(ah_ready, 1)
            if 8 * n + i > 0:
                act.wait_ge(acc_ready, 8 * n + i)
            act.activation(sq[:], xT[:, i, :], ACT.Square).then_inc(sq_ready, 1)
            if n == 3:
                act.activation(xg[:, i, :], xT[:, i, :], ACT.Copy, scale=gain[:, n, i:i + 1]).then_inc(xg_ready, 1)

        def norm_dve(dve, n, i):
            if n < 3:
                dve.wait_ge(ah_ready, 8 * n + i + 1)
                dve.scalar_tensor_tensor(al[:, i, :], xT[:, i, :], gain[:, n, i:i + 1], ah[:, i, :].bitcast(F32),
                                         ALU.mult, ALU.subtract).then_inc(al_ready, 1)
            dve.wait_ge(sq_ready, 8 * n + i + 1)
            if i == 0:
                if n > 0:
                    dve.wait_ge(ss_ready, n)
                dve.tensor_copy(acc[:], sq[:]).then_inc(acc_ready, 1)
            else:
                dve.wait_ge(acc_ready, 8 * n + i)
                dve.tensor_tensor(acc[:], acc[:], sq[:], ALU.add).then_inc(acc_ready, 1)

        def stat_pe(pe, n):
            pe.wait_ge(acc_ready, 8 * (n + 1))
            if n > 0:
                pe.wait_ge(rt_ready, n)
            pe.matmul(bank[7][:], ones[:], acc[:], start=True, stop=True).then_inc(ss_ready, 1)

        def stat_act(act, n):
            act.wait_ge(ss_ready, n + 1)
            act.activation(sq[:], bank[7][:], ACT.Sqrt, scale=1.0 / D, bias=eps[:, 0:1]).then_inc(rt_ready, 1)

        def stat_dve(dve, n):
            dve.wait_ge(rt_ready, n + 1)
            dve.reciprocal(rstd[:], sq[:]).then_inc(rstd_ready, 1)
            dve.wait_ge(rstd_ready, n + 1)

        def gu_pe(pe, n, f, b, known=True, norm=None):
            c0, g0 = UP0[n], FT * n
            for part in (0, 1):
                pe.wait_ge(lo_ready, c0 + 2 * f + part + 1)
                if known:
                    pe.wait_ge(up_out if part else gate_out, g0 + f - 1)
                for k in range(DT):
                    if norm is not None and part == 0:
                        pe.wait_ge(al_ready, 8 * norm + k + 1)
                    mm = three(pe, bank[2 * part + b][:], part, k, ah[:, k, :], al[:, k, :], k == 0, k == DT - 1)
                mm.then_inc(chunk_done, 1)
                if norm is not None and part == 0:
                    stat_pe(pe, norm)

        def gu_up_dve(dve, n, f, b):
            c0, g0 = UP0[n], FT * n
            dve.wait_ge(chunk_done, c0 + 2 * f + 2)
            dve.tensor_tensor(us[:], bank[2 + b][:], rstd[:], ALU.mult).then_inc(up_out, 1)
            dve.wait_ge(up_out, g0 + f + 1)
            dve.wait_ge(silu_ready, g0 + f + 1)
            dve.tensor_tensor(hid[:, b, :], sg[:, b, :], us[:], ALU.mult).then_inc(hid_ready, 1)

        def gu_low_dve(dve, n, f, b):
            dve.wait_ge(hh_ready, FT * n + f + 1)
            dve.tensor_tensor(hp[:, f, 1, :], hid[:, b, :], hp[:, f, 0, :].bitcast(F32), ALU.subtract).then_inc(hl_ready, 1)

        def gu_gate_dve(dve, n, f, b):
            dve.wait_ge(chunk_done, UP0[n] + 2 * f + 1)
            dve.tensor_tensor(gs[:, b, :], bank[b][:], rstd[:], ALU.mult).then_inc(gate_out, 1)

        def gu_hid_act(act, n, f, b):
            act.wait_ge(hid_ready, FT * n + f + 1)
            act.activation(hp[:, f, 0, :], hid[:, b, :], ACT.Copy).then_inc(hh_ready, 1)

        def gu_silu_act(act, n, f, b):
            act.wait_ge(gate_out, FT * n + f + 1)
            act.activation(sg[:, b, :], gs[:, b, :], ACT.Silu).then_inc(silu_ready, 1)

        def gu_dve(dve, n, f, b, c4, first=False, norm=None):
            c = UP0[n] + 2 * f
            split_lo(dve, c + 1, c4 + 1, DT)
            if norm is not None:
                stat_dve(dve, norm)
            if not first:
                gu_up_dve(dve, n, f - 1, 1 - b)
                gu_low_dve(dve, n, f - 1, 1 - b)
            split_lo(dve, c + 2, c4 + 2, DT)
            gu_gate_dve(dve, n, f, b)

        def gu_act(act, n, f, b, c4, first=False, norm=None):
            c = UP0[n] + 2 * f
            split_hi(act, c + 1, c4 + 1, DT, first=(n == 0 and first))
            if norm is not None:
                stat_act(act, norm)
            if not first:
                gu_hid_act(act, n, f - 1, 1 - b)
            split_hi(act, c + 2, c4 + 2, DT)
            gu_silu_act(act, n, f, b)

        def gu_loop(eng, n, one, f0, f1):
            with eng.Fori(f0 // 2, f1 // 2) as j:
                for b in (0, 1):
                    if one is gu_pe:
                        one(eng, n, 2 * j + b, b)
                    else:
                        one(eng, n, 2 * j + b, b, 2 * b)

        def down_pe(pe, n, m, b, slot0, first=False):
            d0 = DN0[n]
            if not first:
                pe.wait_ge(x_new, X_DOWN[n] + m - 1)
            for i, (k0, k1) in enumerate(DOWN_PARTS):
                pe.wait_ge(lo_ready, d0 + 3 * m + i + 1)
                for k in range(k0, k1):
                    if first and b == 0 and k == FT - 1:
                        pe.wait_ge(hl_ready, FT * (n + 1))
                    mm = three(pe, bank[4 + b][:], slot0 + i, k - k0, hp[:, k, 0, :], hp[:, k, 1, :],
                               k == 0, k == FT - 1)
                mm.then_inc(chunk_done, 1)

        X_DOWN = (0, 16)

        def x_dve(dve, done, ps, m, factor):
            dve.wait_ge(chunk_done, done)
            dve.scalar_tensor_tensor(xT[:, m, :], ps[:], factor, xT[:, m, :], ALU.mult, ALU.add).then_inc(x_new, 1)

        def part_len(i):
            return DOWN_PARTS[i % 3][1] - DOWN_PARTS[i % 3][0]

        def win_bank(g):
            return bank[(4, 5, 6, 7)[g // 4 % 4]]

        def out_pe(pe, m, b, first=False):
            pe.wait_ge(lo_ready, OUT0 + m + 1)
            if not first:
                pe.wait_ge(x_new, 8 + m - 1)
            for k in range(DT):
                if first and b == 0:
                    pe.wait_ge(ml_ready, k + 1)
                mm = three(pe, bank[5 + b][:], b, k, mh[:, k, :], ml[:, k, :], k == 0, k == DT - 1)
            mm.then_inc(chunk_done, 1)

        def gu_act_first2(act):
            c = UP0[1]
            split_hi(act, c + 1, 1, DT)
            norm_act(act, 2, DT - 1)
            stat_act(act, 2)
            split_hi(act, c + 2, 2, DT)
            gu_silu_act(act, 1, 0, 0)

        def turned_u(op, n, *a):
            o = u_[:, 8 * (n // 2):8 * (n // 2) + 8, 4 * (n % 2):4 * (n % 2) + 4, :]
            i = bank[2 + n % 4][0:C, :].rearrange("c (t g h) -> c g t h", t=4, g=8)
            return op(o, i, *a)

        def turned_y(dst, n, half):
            gt, q = n // 2, n % 2
            o = dst[:, gt + 2 * half, :].rearrange("p (c t) -> p t c", t=T)[:, 4 * q:4 * q + 4, :]
            i = bank[2 + n][:].rearrange("p (t b c) -> p t b c", t=4, b=2)[:, :, half, :]
            return o, i

        def pt_evac(eng, op, u, *a):
            qt = u // H
            eng.wait_ge(pt_done, u + 1)
            if u >= 2:
                eng.wait_ge(pv_done, u - 1)
            op(pts[u % 2][:, 0:(qt + 1) * P], bank[2 + u % 2][:, 0:(qt + 1) * P], *a).then_inc(pt_out[u % 2], 1)

        def attn_hi(act, qt):
            act.wait_ge(at_done, qt + 1)
            act.activation(th[:, :, qt * P:(qt + 1) * P], bank[7][:].rearrange("p (i q) -> p i q", i=AT),
                           ACT.Copy).then_inc(th_ready, 1)

        def attn_lo(dve, qt):
            dve.wait_ge(th_ready, qt + 1)
            dve.tensor_tensor(tl[:, :, qt * P:(qt + 1) * P], bank[7][:].rearrange("p (i q) -> p i q", i=AT),
                              th[:, :, qt * P:(qt + 1) * P].bitcast(F32), ALU.subtract).then_inc(tl_ready, 1)

        def down_act(act, n):
            for m in range(DT):
                c = DN0[n] + 3 * m
                split_hi(act, c + 1, 3 * m + 1, part_len(1))
                if m == 0:
                    gu_hid_act(act, n, FT - 1, 1)
                split_hi(act, c + 2, 3 * m + 2, part_len(2))
                if m:
                    norm_act(act, 1 if n == 0 else 3, m - 1)
                if c + 3 < CHUNKS:
                    split_hi(act, c + 3, 3 * m + 3, DT)

        def down_dve(dve, n):
            for m in range(DT):
                c = DN0[n] + 3 * m
                split_lo(dve, c + 1, 3 * m + 1, part_len(1))
                if m == 0:
                    gu_up_dve(dve, n, FT - 1, 1)
                    gu_low_dve(dve, n, FT - 1, 1)
                else:
                    x_dve(dve, c, bank[4 + (m - 1) % 2], m - 1, 0.5)
                split_lo(dve, c + 2, 3 * m + 2, part_len(2))
                if m:
                    norm_dve(dve, 1 if n == 0 else 3, m - 1)
                if c + 3 < CHUNKS:
                    split_lo(dve, c + 3, 3 * m + 3, DT)

        def prj_dve(dve, i):
            dve.wait_ge(chunk_done, PRJ0 + i + 1)
            dve.tensor_tensor(prj[:, i, :], bank[i % 2][:], rstd[:], ALU.mult).then_inc(prj_out, 1)

        def attn_norm(dve, link, qt):
            dve.wait_ge(pv_done, (qt + 1) * H)
            link(dve.reciprocal(rec[:, qt * H:(qt + 1) * H], sums[:, qt * H:(qt + 1) * H]))
            dve.tensor_tensor(ao[:, qt % 2, :].rearrange("p (h d) -> p h d", h=H),
                              bank[4 + qt % 2][:].rearrange("p (h d) -> p h d", h=H),
                              rec[:, qt * H:(qt + 1) * H].unsqueeze(2).to_broadcast([P, H, HD]),
                              ALU.mult).then_inc(ao_ready, 1)

        block = ctx.enter_context(nc.Block())

        @block.sync
        def _(sp):
            def load(c, slot, src, n, first=False):
                if not first:
                    sp.wait_ge(lo_ready, c - RAW + 1)
                sp.dma_start(raw[:, slot % RAW, 0:n * P], src).then_inc(landed[slot % RAW], 16)

            def up_loads(n, f0):
                with sp.Fori(f0 // 2, FT // 2) as i:
                    for j in range(4):
                        load(UP0[n] + 4 * i + j, j, w_up[n, 2 * i + j // 2, j % 2], DT)

            def down_loads(n):
                with sp.Fori(0, DT // 4) as i:
                    for j in range(12):
                        k0, k1 = DOWN_PARTS[j % 3]
                        load(DN0[n] + 12 * i + j, j, w_down[n, 4 * i + j // 3, :, k0 * P:k1 * P], k1 - k0)

            for j in range(2):
                sp.dma_start(xT[:, 2 * j:2 * j + 2, :], x[:, 2 * j:2 * j + 2, :]).then_inc(x_in[j], 16)
                load(j, j, w_up[0, 0, j], DT, first=True)
            for j in range(2, 4):
                sp.dma_start(xT[:, 2 * j:2 * j + 2, :], x[:, 2 * j:2 * j + 2, :]).then_inc(x_in[j], 16)
                load(j, j, w_up[0, 1, j % 2], DT, first=True)
            up_loads(0, 2)
            down_loads(0)
            with sp.Fori(0, AT) as i:
                for j in range(4):
                    load(PRJ0 + 4 * i + j, j, w_proj[4 * i + j], DT)
            with sp.Fori(0, DT) as m:
                for j in range(4):
                    n = (8, 8, 8, 4)[j]
                    load(MRG0 + 4 * m + j, j, w_merge[m, :, 8 * j * P:(8 * j + n) * P], n)
            with sp.Fori(0, DT // 4) as i:
                for j in range(4):
                    load(OUT0 + 4 * i + j, j, w_out[4 * i + j], DT)
            up_loads(1, 0)
            down_loads(1)
            for i in range(DT):
                if i < 5:
                    sp.wait_ge(fin_dve, i + 1)
                else:
                    sp.wait_ge(fin_pool, i - 4)
                sp.dma_start(out[:, i, :], xg[:, i, :]).then_inc(out_done, 16)
            sp.wait_ge(out_done, 16 * DT)

        @block.tensor
        def _(pe):
            gu_pe(pe, 0, 0, 0, known=False, norm=0)
            gu_pe(pe, 0, 1, 1, known=False)
            gu_loop(pe, 0, gu_pe, 2, 4)
            pe.wait_ge(winT_ready, 1)
            pe.wait_ge(c_in, 16 * 4)
            for g in range(G):
                if g >= 16 and g % 4 == 0:
                    pe.wait_ge(win_out, g // 4 - 3)
                tr = pe.transpose(win_bank(g)[:, (g % 4) * P:(g % 4 + 1) * P],
                                  winT[:, g, :, :].rearrange("p t h -> p (t h)"), ident[:])
                if g % 4 == 3:
                    tr.then_inc(winT_turned, 1)
            gu_loop(pe, 0, gu_pe, 4, 14)
            pe.wait_ge(ce_ready, 1)
            for g in range(G):
                if g >= 16 and g % 4 == 0:
                    pe.wait_ge(kt_out, g // 4 - 3)
                mm = pe.matmul(win_bank(g)[0:GH, (g % 4) * P:(g % 4 + 1) * P], bb[:, g, :],
                               ce_w[:, g, 0:T, :].rearrange("p k h -> p (k h)"), start=True, stop=True)
                if g % 4 == 3:
                    mm.then_inc(kt_done, 1)
            gu_loop(pe, 0, gu_pe, 14, FT)
            down_pe(pe, 0, 0, 0, 0, first=True)
            down_pe(pe, 0, 1, 1, 1, first=True)
            with pe.Fori(1, DT // 2) as j:
                for b in (0, 1):
                    down_pe(pe, 0, 2 * j + b, b, b)

            def prj_pe(i, b, known=True, norm=None):
                pe.wait_ge(lo_ready, PRJ0 + i + 1)
                if known:
                    pe.wait_ge(prj_out, i - 1)
                for k in range(DT):
                    if norm is not None:
                        pe.wait_ge(al_ready, 8 * norm + k + 1)
                    mm = three(pe, bank[b][:], b, k, ah[:, k, :], al[:, k, :], k == 0, k == DT - 1)
                mm.then_inc(chunk_done, 1)
                if norm is not None:
                    stat_pe(pe, norm)

            def turn_u(r):
                pe.wait_ge(prj_out, AT)
                for ct in (2 * r, 2 * r + 1):
                    for q in (0, 1):
                        n = 2 * ct + q
                        if n >= 4:
                            pe.wait_ge(u_act if n % 2 == 0 else u_dve, (n - 4) // 2 + 1)
                        for j in range(4):
                            t = T - 1 - (4 * q + j)
                            tr = pe.transpose(bank[2 + n % 4][0:C, j * P:(j + 1) * P],
                                              prj[:, ct, t:S:T], ident[:])
                        tr.then_inc(tu_done, 1)

            prj_pe(0, 0, known=False, norm=1)
            prj_pe(1, 1, known=False)
            prj_pe(2, 0)
            prj_pe(3, 1)
            prj_pe(4, 0)
            turn_u(0)
            prj_pe(5, 1)
            turn_u(1)
            prj_pe(6, 0)
            pe.wait_ge(u_act, 4)
            pe.wait_ge(u_dve, 4)
            for g in range(G):
                tr = pe.transpose(bank[2 + g // 8][:, (g % 8) * C:(g % 8 + 1) * C],
                                  u_[:, g, :, :].rearrange("c t h -> c (t h)"), ident[0:C, 0:C])
                if g % 8 == 7:
                    tr.then_inc(tc_done, 1)
            prj_pe(7, 1)
            pe.wait_ge(tab_in[0], 16)
            for g in range(G):
                if g % 8 == 0:
                    pe.wait_ge(uc_act if g // 8 % 2 == 0 else uc_dve, g // 16 + 1)
                mm = pe.matmul(bank[2 + g // 8][:, (g % 8) * C:(g % 8 + 1) * C], win[:, g, :], uc[:, g, :],
                               start=True, stop=True)
                if g % 8 == 7:
                    mm.then_inc(z_done, 1)
            with pe.Fori(4, 2 * AT) as j:
                for b in (0, 1):
                    prj_pe(2 * j + b, b)

            pe.wait_ge(tab_in[3], 16)
            pe.wait_ge(toep_in, 16 * T)
            pe.wait_ge(hs_ready, 1)
            for j in range(G // 2):
                for half in (0, 1):
                    g = j + G // 2 * half
                    ps = bank[2 + j // 4][C * half:C * (half + 1), (j % 4) * P:(j % 4 + 1) * P]
                    pe.matmul(ps, uc[:, g, :], toep[:, g, :], start=True, stop=False)
                    mm = pe.matmul(ps, hs[:, g, :], ce[:, g, 1:NA, :].rearrange("p k h -> p (k h)"),
                                   start=False, stop=True)
                if j % 4 == 3:
                    mm.then_inc(y_done, 1)
            pe.wait_ge(prj_out, 4 * AT)
            for kb in range(QT):
                for i in range(AT):
                    tr = pe.transpose(bank[(6, 7, 0, 1)[kb]][:, i * P:(i + 1) * P],
                                      prj[:, 3 * AT + i, kb * P:(kb + 1) * P], ident[:])
                tr.then_inc(tv_done, 1)
            pe.wait_ge(gelu_ready, 4)
            for n in range(4):
                for j in range(4):
                    tr = pe.transpose(bank[2 + n][:, j * P:(j + 1) * P], y_[:, n // 2, 4 * (n % 2) + j, :], ident[:])
                tr.then_inc(ty_done, 1)

            units = [(qt, h) for qt in range(QT) for h in range(H)]
            s_bank = (0, 1, 6)

            def scores(u):
                qt, h = units[u]
                if u == 0:
                    pe.wait_ge(v_out, QT)
                if u >= 3:
                    pe.wait_ge(nmx_ready, u - 2)
                r, i = HD * (h % 2), h // 2
                pe.matmul(bank[s_bank[u % 3]][:, 0:(qt + 1) * P], prj[r:r + HD, 2 * AT + i, qt * P:(qt + 1) * P],
                          prj[r:r + HD, AT + i, 0:(qt + 1) * P], start=True, stop=True).then_inc(sc_done, 1)

            def turn_p(u):
                qt, h = units[u]
                if u == 0:
                    pe.wait_ge(yl_ready, 8)
                pe.wait_ge(exp_ready, u + 1)
                if u >= 2:
                    pe.wait_ge(pt_out[u % 2], u // 2)
                for kb in range(qt + 1):
                    tr = pe.transpose(bank[2 + u % 2][:, kb * P:(kb + 1) * P], pr[:, u % 3, kb * P:(kb + 1) * P], ident[:])
                tr.then_inc(pt_done, 1)

            def pv(u):
                qt, h = units[u]
                pe.wait_ge(pt_out[u % 2], u // 2 + 1)
                if h == 0 and qt >= 2:
                    pe.wait_ge(ao_ready, qt - 1)
                for kb in range(qt + 1):
                    mm = pe.matmul(bank[4 + qt % 2][:, h * HD:(h + 1) * HD], pts[u % 2][:, kb * P:(kb + 1) * P],
                                   v_[:, kb, h * HD:(h + 1) * HD], start=(kb == 0), stop=(kb == qt))
                mm.then_inc(pv_done, 1)

            def turn_o(qt):
                pe.wait_ge(ao_ready, qt + 1)
                if qt:
                    pe.wait_ge(tl_ready, qt)
                for i in range(AT):
                    tr = pe.transpose(bank[7][:, i * P:(i + 1) * P], ao[:, qt % 2, i * P:(i + 1) * P], ident[:])
                tr.then_inc(at_done, 1)

            n = len(units)
            for u in range(n + 3):
                if u < n:
                    scores(u)
                if 2 <= u < n + 2:
                    turn_p(u - 2)
                if u >= 3:
                    pv(u - 3)
                    if (u - 3) % H == 1 and u - 3 > H:
                        turn_o((u - 3) // H - 1)
            turn_o(QT - 1)

            def merge_pe(m, first=False):
                for part in (0, 1):
                    pe.wait_ge(lo_ready, MRG0 + 4 * m + part + 1)
                    if not first:
                        pe.wait_ge(gs_out if part else ga_out, m)
                    for k in range(DT):
                        mm = three(pe, bank[part][:], part, k, ah[:, k, :], al[:, k, :], k == 0, k == DT - 1)
                    mm.then_inc(chunk_done, 1)
                    if first and part == 0:
                        pe.wait_ge(tl_ready, QT)
                pe.wait_ge(lo_ready, MRG0 + 4 * m + 3)
                if not first:
                    pe.wait_ge(ma_ready, m)
                for k in range(AT):
                    three(pe, bank[2][:], 2, k, th[:, k, :], tl[:, k, :], k == 0, k == AT - 1)
                for k in range(AT):
                    mm = three(pe, bank[3][:], 2, AT + k, yh[:, k, :], yl[:, k, :], k == 0, k == AT - 1)
                mm.then_inc(chunk_done, 1)
                pe.wait_ge(lo_ready, MRG0 + 4 * m + 4)
                if not first:
                    pe.wait_ge(sgy_ready, m)
                for k in range(AT):
                    mm = three(pe, bank[4][:], 3, k, yh[:, k, :], yl[:, k, :], k == 0, k == AT - 1)
                mm.then_inc(chunk_done, 1)

            merge_pe(0, first=True)
            with pe.Fori(1, DT) as m:
                merge_pe(m)

            for m in range(2):
                out_pe(pe, m, m, first=True)
            with pe.Fori(1, DT // 2) as j:
                for b in (0, 1):
                    out_pe(pe, 2 * j + b, b)

            gu_pe(pe, 1, 0, 0, known=False, norm=2)
            gu_pe(pe, 1, 1, 1, known=False)
            gu_loop(pe, 1, gu_pe, 2, FT)
            down_pe(pe, 1, 0, 0, 0, first=True)
            down_pe(pe, 1, 1, 1, 1, first=True)
            with pe.Fori(1, DT // 2) as j:
                for b in (0, 1):
                    down_pe(pe, 1, 2 * j + b, b, b)
            stat_pe(pe, 3)

        @block.scalar
        def _(act):
            A = Count(ca)
            act.wait_ge(set_up, 1)
            act.wait_ge(s_in, 16 * 7)
            act.activation(small[:, 3, :], small[:, 2, :], ACT.Exp).then_inc(prep_act, 1)
            act.wait_ge(c_in, 16 * 4)
            for i in range(DT):
                norm_act(act, 0, i)
                if i == 1:
                    split_hi(act, 0, 0, DT, first=True)
            gu_act(act, 0, 0, 0, 0, first=True, norm=0)
            act.wait_ge(prep_dve, 1)
            act.activation(mag[:, :, :], expo[:, :, :], ACT.Exp)
            act.activation(mag8[:, :], small[:, 22, :], ACT.Exp).then_inc(prep_act, 1)
            act.activation(sn[:, :, :], ang[:, :, :], ACT.Sin)
            act.activation(cs[:, :, :].rearrange("p g k -> p (g k)"), tn[:], ACT.Sin).then_inc(prep_act, 1)
            gu_act(act, 0, 1, 1, 2)
            gu_loop(act, 0, gu_act, 2, 4)
            for n in range(8):
                act.wait_ge(winT_turned, n + 1)
                act.activation(winS[:, 4 * n:4 * n + 4, :].rearrange("p g c -> p (g c)"),
                               bank[4 + n % 4][:], ACT.Copy).then_inc(win_out, 1)
            gu_loop(act, 0, gu_act, 4, 14)
            act.wait_ge(stored, 16 * 5)
            gu_loop(act, 0, gu_act, 14, FT)
            down_act(act, 0)

            zx_v = zx[:, :, :].rearrange("p g c -> p (g c)")
            for i in range(4 * AT):
                split_hi(act, PRJ0 + i + 1, i + 1, DT)
                if i == 0:
                    norm_act(act, 1, DT - 1)
                    stat_act(act, 1)
                if i in (5, 6):
                    for n in range(4 * (i - 5), 4 * (i - 4), 2):
                        act.wait_ge(tu_done, n + 1)
                        turned_u(act.activation, n, ACT.Copy).then_inc(u_act, 1)
                if i == 7:
                    for n in (0, 2):
                        act.wait_ge(tc_done, n + 1)
                        act.activation(uc[:, 8 * n:8 * n + 8, :].rearrange("p g c -> p (g c)"), bank[2 + n][:],
                                       ACT.Copy).then_inc(uc_act, 1)
                if i == 8:
                    act.wait_ge(z_done, 4)
                    for n in range(4):
                        cols = slice(n * S, (n + 1) * S)
                        act.activation(zx_v[0:NS, cols], bank[2 + n][NS:P, :], ACT.Copy)
                        act.activation(zx_v[NS:P, cols], bank[2 + n][0:NS, :], ACT.Copy, scale=-1.0).then_inc(zx_ready, 1)
                if i == 12:
                    act.wait_ge(scan_ready, G)
                    g_v = zg[:, :, :].rearrange("p g c -> p (g c)")
                    act.activation(g_v[0:NS, :], zx_v[NS:P, :], ACT.Copy, scale=-1.0)
                    act.activation(g_v[NS:P, :], zx_v[0:NS, :], ACT.Copy).then_inc(gx_ready, 1)
            for n in range(4):
                act.wait_ge(y_done, n + 1)
                o = y_[:, n // 2, :, 64 * (n % 2):64 * (n % 2) + 64].rearrange("p t (j h) -> p j t h", j=4)
                act.activation(o, bank[2 + n][:].rearrange("p (j t h) -> p j t h", j=4, t=T),
                               ACT.Gelu_apprx_tanh).then_inc(gelu_ready, 1)
            for n in range(4):
                act.wait_ge(ty_done, n + 1)
                for half in (0, 1):
                    o, i_ = turned_y(yh, n, half)
                    act.activation(o, i_, ACT.Copy).then_inc(yh_ready, 1)
            units = [(qt, h) for qt in range(QT) for h in range(H)]
            for u in range(len(units) + 1):
                if u < len(units):
                    qt, h = units[u]
                    w = (qt + 1) * P
                    act.wait_ge(nmx_ready, u + 1)
                    if u >= 3:
                        act.wait_ge(pt_done, u - 2)
                    act.activation(pr[:, u % 3, 0:w], sc[:, u % 3, 0:w], ACT.Exp, bias=nmx[:, u:u + 1],
                                   scale=HD ** -0.5, accum_out=sums[:, u:u + 1]).then_inc(exp_ready, 1)
                if u >= 1 and (u - 1) % 2 == 1:
                    pt_evac(act, act.activation, u - 1, ACT.Copy)
                if u >= H + 4 and (u - 4) % H == 0:
                    attn_hi(act, (u - 4) // H - 1)
            attn_hi(act, QT - 1)
            def merge_act(m, first=False, last=False):
                c = MRG0 + 4 * m
                split_hi(act, c + 1, 1, DT)
                if not first:
                    merge_act_end(m - 1)
                split_hi(act, c + 2, 2, DT)
                act.wait_ge(ga_out, m + 1)
                act.activation(sg[:, 0, :], gs[:, 0, :], ACT.Sigmoid).then_inc(sga_ready, 1)
                split_hi(act, c + 3, 3, AT)
                act.wait_ge(gs_out, m + 1)
                act.activation(sg[:, 1, :], gs[:, 1, :], ACT.Sigmoid).then_inc(sgs_ready, 1)
                split_hi(act, c + 4, 4, DT)

            def merge_act_end(m):
                act.wait_ge(chunk_done, MRG0 + 4 * m + 4)
                act.activation(us[:], bank[4][:], ACT.Sigmoid).then_inc(sgy_ready, 1)
                act.wait_ge(mg_ready, m + 1)
                act.activation(mh[:, m, :], hid[:, 1, :], ACT.Copy).then_inc(mh_ready, 1)

            merge_act(0, first=True)
            with act.Fori(1, DT) as m:
                merge_act(m)
            for m in range(DT):
                split_hi(act, OUT0 + m + 1, m + 1, DT)
                if m == 0:
                    merge_act_end(DT - 1)
                else:
                    norm_act(act, 2, m - 1)
            gu_act_first2(act)
            gu_act(act, 1, 1, 1, 2)
            gu_loop(act, 1, gu_act, 2, FT)
            down_act(act, 1)
            norm_act(act, 3, DT - 1)
            stat_act(act, 3)

        @block.vector
        def _(dve):
            V = Count(cd)

            def link(ins):
                V.link(dve, ins)

            dve.memset(ones[:], 1.0)
            dve.memset(eps[:], EPS).then_inc(set_up, 1)

            def reduce_angle(r, n_, x_in_, consts):
                link(dve.tensor_scalar(n_, x_in_, 1.0 / (2 * PI), MAGIC, ALU.mult, ALU.add))
                link(dve.tensor_scalar(n_, n_, MAGIC, None, ALU.subtract))
                src = x_in_
                for c_ in consts:
                    link(dve.scalar_tensor_tensor(r, n_, -c_, src, ALU.mult, ALU.add))
                    src = r
                link(dve.tensor_scalar(r, r, PI, -PI, ALU.min, ALU.max))

            sm = [small[:, j, :] for j in range(24)]
            lre, lim, _, dt, lr, an, r0, p8, p64, nn = sm[:10]
            tt, ts = dve.tensor_tensor, dve.tensor_scalar
            dve.wait_ge(prep_act, 1)
            link(tt(lr, lre, dt, ALU.mult))
            link(tt(an, lim, dt, ALU.mult))
            reduce_angle(r0, nn, an, TWO_PI)
            link(ts(an, r0, 8.0, None, ALU.mult))
            reduce_angle(p8, nn, an, TWO_PI)
            link(ts(an, p8, 8.0, None, ALU.mult))
            reduce_angle(p64, nn, an, TWO_PI)
            dve.wait_ge(c_in, 16 * 4)

            for i in range(DT):
                norm_dve(dve, 0, i)
                if i == 1:
                    split_lo(dve, 0, 0, DT)
            gu_dve(dve, 0, 0, 0, 0, first=True, norm=0)

            def angles(k0, k1, base):
                k = mult[:, k0:k1].unsqueeze(1).to_broadcast([P, G, k1 - k0])
                return tt(ang[:, :, k0:k1], base.unsqueeze(2).to_broadcast([P, G, k1 - k0]), k, ALU.mult)

            angles(0, NA, r0)
            angles(NA, NA + NB, p8)
            tt(expo[:, :, :], lr.unsqueeze(2).to_broadcast([P, G, NA]),
               mult[:, 0:NA].unsqueeze(1).to_broadcast([P, G, NA]), ALU.mult)
            ts(sm[22], lr, 8.0, None, ALU.mult)
            link(angles(NA + NB, NK, p64))
            ang_v = ang[:, :, :].rearrange("p g k -> p (g k)")
            reduce_angle(ang_v, tn[:], ang_v, TWO_PI[:2])
            link(ts(tn[:], ang_v, PI / 2, -2 * PI, ALU.is_gt, ALU.mult))
            link(dve.scalar_tensor_tensor(tn[:], ang_v, PI / 2, tn[:], ALU.add, ALU.add))
            dve.tensor_scalar(tn[:], tn[:], PI, -PI, ALU.min, ALU.max).then_inc(prep_dve, 1)
            den, t1, t2, fr, fi, num = sm[10:16]
            link(tt(den, lre, lre, ALU.mult))
            link(tt(t1, lim, lim, ALU.mult))
            link(tt(den, den, t1, ALU.add))
            link(dve.reciprocal(den, den))
            gu_dve(dve, 0, 1, 1, 2)
            dve.wait_ge(prep_act, 3)
            link(tt(er[:, :, :], mag[:, :, :], cs[:, :, 0:NA], ALU.mult))
            link(tt(ei[:, :, :], mag[:, :, :], sn[:, :, 0:NA], ALU.mult))
            ar1, ai1 = er[:, :, 1], ei[:, :, 1]
            link(ts(num, ar1, 1.0, None, ALU.subtract))
            link(tt(fr, num, lre, ALU.mult))
            link(tt(t1, ai1, lim, ALU.mult))
            link(tt(fr, fr, t1, ALU.add))
            link(tt(fr, fr, den, ALU.mult))
            link(tt(fi, ai1, lre, ALU.mult))
            link(tt(t2, num, lim, ALU.mult))
            link(tt(fi, fi, t2, ALU.subtract))
            link(tt(fi, fi, den, ALU.mult))
            link(ts(bS[:, :, :], bS[:, :, :], signs[:, 0:1], None, ALU.mult))
            link(ts(cO[:, :, :], cO[:, :, :], signs[:, 1:2], None, ALU.mult))
            link(ts(cA[:, :, :], cR[:, :, :], -1.0, None, ALU.mult))
            frb = fr.unsqueeze(2).to_broadcast([P, G, GH])
            fib = fi.unsqueeze(2).to_broadcast([P, G, GH])
            link(tt(bb[:, :, :], frb, bO[:, :, :], ALU.mult))
            link(tt(tmpB[:, :, :], fib, bS[:, :, :], ALU.mult))
            link(tt(bb[:, :, :], bb[:, :, :], tmpB[:, :, :], ALU.add))
            link(tt(bbS[:, :, :], frb, bS[:, :, :], ALU.mult))
            link(tt(tmpB[:, :, :], fib, bO[:, :, :], ALU.mult))
            tt(bbS[:, :, :], bbS[:, :, :], tmpB[:, :, :], ALU.subtract).then_inc(prep_dve, 1)
            gu_loop(dve, 0, gu_dve, 2, 4)
            gu_loop(dve, 0, gu_dve, 4, 14)
            for n in range(8):
                dve.wait_ge(kt_done, n + 1)
                if n == 0:
                    dve.wait_ge(stored, 16 * 4)
                dve.tensor_copy(ktS[:, 4 * n:4 * n + 4, :, :].rearrange("p g k h -> p (g k h)"),
                                win_bank(4 * n)[0:GH, :]).then_inc(kt_out, 1)
            dve.wait_ge(stored, 16 * 5)
            gu_loop(dve, 0, gu_dve, 14, FT)
            down_dve(dve, 0)

            flat = "p g c -> p (g c)"
            zg_v, zx_v, cos_v = (t[:, :, :].rearrange(flat) for t in (zg, zx, cosT))
            for i in range(4 * AT):
                split_lo(dve, PRJ0 + i + 1, i + 1, DT)
                if i == 0:
                    x_dve(dve, PRJ0, bank[5], DT - 1, 0.5)
                    norm_dve(dve, 1, DT - 1)
                    stat_dve(dve, 1)
                else:
                    prj_dve(dve, i - 1)
                if i in (5, 6):
                    for n in range(4 * (i - 5) + 1, 4 * (i - 4), 2):
                        dve.wait_ge(tu_done, n + 1)
                        turned_u(dve.tensor_copy, n).then_inc(u_dve, 1)
                if i == 7:
                    for n in (1, 3):
                        dve.wait_ge(tc_done, n + 1)
                        dve.tensor_copy(uc[:, 8 * n:8 * n + 8, :].rearrange(flat), bank[2 + n][:]).then_inc(uc_dve, 1)
                if i == 8:
                    dve.wait_ge(z_done, 4)
                    dve.wait_ge(tab_in[1], 16)
                    for n in range(4):
                        dve.wait_ge(zx_ready, n + 1)
                        cols = slice(n * S, (n + 1) * S)
                        ins = tt(zg_v[:, cols], bank[2 + n][:], cos_v[:, cols], ALU.mult)
                    link(ins)
                if i == 10:
                    dve.wait_ge(zx_sin, 1)
                    link(tt(zg_v, zg_v, zx_v, ALU.add))
                if i in (10, 11):
                    for g in range(16 * (i - 10), 16 * (i - 9)):
                        dve.tensor_tensor_scan(zx[:, g, :], mag8[:, g:g + 1].to_broadcast([P, C]), zg[:, g, :],
                                               0.0, ALU.mult, ALU.add).then_inc(scan_ready, 1)
                if i == 13:
                    dve.wait_ge(scan_ready, G)
                    dve.memset(hs[:, :, 0:1], 0.0)
                    link(tt(hs[:, :, 1:C], zx[:, :, 0:C - 1], cosT[:, :, 0:C - 1], ALU.mult))
                if i == 14:
                    dve.wait_ge(gx_sin, 1)
                    tt(hs[:, :, 1:C], hs[:, :, 1:C], zg[:, :, 0:C - 1], ALU.add).then_inc(hs_ready, 1)
            prj_dve(dve, 4 * AT - 1)
            for kb in range(QT):
                dve.wait_ge(tv_done, kb + 1)
                if kb == 0:
                    dve.wait_ge(hs_ready, 1)
                dve.tensor_copy(v_[:, kb, :], bank[(6, 7, 0, 1)[kb]][:]).then_inc(v_out, 1)
            for n in range(4):
                dve.wait_ge(yh_ready, 2 * n + 2)
                for half in (0, 1):
                    o, i_ = turned_y(yl, n, half)
                    oh, _ = turned_y(yh, n, half)
                    tt(o, i_, oh.bitcast(F32), ALU.subtract).then_inc(yl_ready, 1)
            units = [(qt, h) for qt in range(QT) for h in range(H)]
            for u in range(len(units) + 4):
                if u < len(units):
                    qt, h = units[u]
                    w, o = (qt + 1) * P, (QT - 1 - qt) * P
                    dve.wait_ge(sc_done, u + 1)
                    if u < H:
                        dve.wait_ge(bias_ready, u + 1)
                    if u >= 3:
                        dve.wait_ge(exp_ready, u - 2)
                    link(dve.tensor_tensor_reduce(sc[:, u % 3, 0:w], bank[(0, 1, 6)[u % 3]][:, 0:w],
                                                  bias[h // 4][:, h % 4, o:o + w], 1.0, -3.0e38, ALU.add, ALU.max,
                                                  mx[:, u:u + 1]))
                    dve.tensor_scalar(nmx[:, u:u + 1], mx[:, u:u + 1], -(HD ** -0.5), None,
                                      ALU.mult).then_inc(nmx_ready, 1)
                if 2 <= u < len(units) + 2 and (u - 2) % 2 == 0:
                    pt_evac(dve, dve.tensor_copy, u - 2)
                if u >= 3 and (u - 3) % H == H - 1 and u - 3 < len(units):
                    attn_norm(dve, link, (u - 3) // H)
                if u >= H + 5 and (u - 5) % H == 0:
                    attn_lo(dve, (u - 5) // H - 1)
            attn_lo(dve, QT - 1)
            def merge_dve(m, first=False):
                c = MRG0 + 4 * m
                split_lo(dve, c + 1, 1, DT)
                if not first:
                    merge_dve_end(m - 1)
                split_lo(dve, c + 2, 2, DT)
                dve.wait_ge(chunk_done, c + 1)
                tt(gs[:, 0, :], bank[0][:], rstd[:], ALU.mult).then_inc(ga_out, 1)
                split_lo(dve, c + 3, 3, AT)
                dve.wait_ge(chunk_done, c + 2)
                tt(gs[:, 1, :], bank[1][:], rstd[:], ALU.mult).then_inc(gs_out, 1)
                split_lo(dve, c + 4, 4, DT)
                dve.wait_ge(chunk_done, c + 3)
                dve.wait_ge(sga_ready, m + 1)
                tt(hid[:, 0, :], bank[2][:], sg[:, 0, :], ALU.mult)
                dve.wait_ge(sgs_ready, m + 1)
                tt(acc[:], bank[3][:], sg[:, 1, :], ALU.mult).then_inc(ma_ready, 1)

            def merge_dve_end(m):
                dve.wait_ge(sgy_ready, m + 1)
                dve.wait_ge(ma_ready, m + 1)
                tt(acc[:], acc[:], us[:], ALU.mult).then_inc(me, 1)
                dve.wait_ge(me, m + 1)
                tt(hid[:, 1, :], hid[:, 0, :], acc[:], ALU.add).then_inc(mg_ready, 1)
                dve.wait_ge(mh_ready, m + 1)
                tt(ml[:, m, :], hid[:, 1, :], mh[:, m, :].bitcast(F32), ALU.subtract).then_inc(ml_ready, 1)

            merge_dve(0, first=True)
            with dve.Fori(1, DT) as m:
                merge_dve(m)
            for m in range(DT):
                split_lo(dve, OUT0 + m + 1, m + 1, DT)
                if m == 0:
                    merge_dve_end(DT - 1)
                else:
                    x_dve(dve, OUT0 + m, bank[5 + (m - 1) % 2], m - 1, 1.0)
                    norm_dve(dve, 2, m - 1)
            c = UP0[1]
            split_lo(dve, c + 1, 1, DT)
            x_dve(dve, c, bank[6], DT - 1, 1.0)
            norm_dve(dve, 2, DT - 1)
            stat_dve(dve, 2)
            split_lo(dve, c + 2, 2, DT)
            gu_gate_dve(dve, 1, 0, 0)
            gu_dve(dve, 1, 1, 1, 2)
            gu_loop(dve, 1, gu_dve, 2, FT)
            down_dve(dve, 1)
            x_dve(dve, CHUNKS, bank[5], DT - 1, 0.5)
            norm_dve(dve, 3, DT - 1)
            stat_dve(dve, 3)
            for i in range(5):
                dve.wait_ge(xg_ready, i + 1)
                tt(xg[:, i, :], xg[:, i, :], rstd[:], ALU.mult).then_inc(fin_dve, 1)

        @block.gpsimd
        def _(pool):
            K = Count(cp)

            def link(ins):
                K.link(pool, ins)

            for dst, src in ((ident[:], ident_in), (gain[:], gains), (mult[:], multiples_in), (signs[:], signs_in)):
                pool.dma_start(dst, src).then_inc(c_in, 16)
            for dst, src in ((small[:, 2, :], log_dt), (small[:, 0, :], lam_re), (small[:, 1, :], lam_im),
                             (bO[:], b_own), (bS[:], b_swap), (cO[:], c_own), (cR[:], c_swap)):
                pool.dma_start(dst, src).then_inc(s_in, 16)
            tt = pool.tensor_tensor

            def over_h(t, k0, k1):
                return t[:, :, k0:k1].unsqueeze(3).to_broadcast([P, G, k1 - k0, GH])

            def over_k(t, k):
                return t[:, :, :].unsqueeze(2).to_broadcast([P, G, k, GH])

            pool.wait_ge(prep_dve, 2)
            link(tt(winT[:], over_h(er, 0, T), over_k(bb, T), ALU.mult))
            link(tt(tmpW[:], over_h(ei, 0, T), over_k(bbS, T), ALU.mult))
            tt(winT[:], winT[:], tmpW[:], ALU.add).then_inc(winT_ready, 1)
            pool.wait_ge(win_out, 8)
            pool.dma_start(win_d, winS[:].rearrange("p g c -> p (g c)")).then_inc(stored, 16)
            link(tt(ce_w[:], over_h(er, 0, NA), over_k(cO, NA), ALU.mult))
            pool.wait_ge(stored, 16)
            link(tt(tmpC[:], over_h(ei, 0, NA), over_k(cA, NA), ALU.mult))
            tt(ce_w[:], ce_w[:], tmpC[:], ALU.add).then_inc(ce_ready, 1)
            pool.wait_ge(ce_ready, 1)
            pool.dma_start(ce_d, ce_w[:].rearrange("p g k h -> p (g k h)")).then_inc(stored, 16)
            for q in range(4):
                gg = slice(8 * q, 8 * q + 8)

                def outer(a, b):
                    return (a[:, gg, NA + NB:NK].unsqueeze(3).to_broadcast([P, 8, NB, NB]),
                            b[:, gg, NA:NA + NB].unsqueeze(2).to_broadcast([P, 8, NB, NB]))

                link(tt(cosS[:, gg], *outer(cs, cs), ALU.mult))
                link(tt(tmpR[:], *outer(sn, sn), ALU.mult))
                link(tt(cosS[:, gg], cosS[:, gg], tmpR[:], ALU.subtract))
                link(tt(sinS[:, gg], *outer(sn, cs), ALU.mult))
                link(tt(tmpR[:], *outer(cs, sn), ALU.mult))
                link(tt(sinS[:, gg], sinS[:, gg], tmpR[:], ALU.add))
            pool.dma_start(cos_d, cosS[:].rearrange("p g a b -> p (g a b)")).then_inc(stored, 16)
            pool.dma_start(sin_d, sinS[:].rearrange("p g a b -> p (g a b)")).then_inc(stored, 16)
            pool.wait_ge(kt_out, 8)
            pool.dma_start(dB[:].rearrange("p g h -> p (g h)"), ssm_d.partition_broadcast(GH)).then_inc(d_in, 16)
            pool.wait_ge(d_in, 16)
            link(tt(dB[:], dB[:], ident[0:GH, 0:GH].unsqueeze(1).to_broadcast([GH, G, GH]), ALU.mult))
            link(tt(ktS[:, :, 0, :], ktS[:, :, 0, :], dB[:], ALU.add))
            pool.dma_start(kt_d, ktS[:].rearrange("p g k h -> p (g k h)")).then_inc(stored, 16)

            pool.wait_ge(stored, 16 * 5)
            pool.wait_ge(chunk_done, PRJ0)
            pool.dma_start(win[:].rearrange("p g c -> p (g c)"), win_d).then_inc(tab_in[0], 16)
            pool.dma_start(cosT[:].rearrange("p g c -> p (g c)"), cos_d).then_inc(tab_in[1], 16)
            pool.dma_start(sinT[:].rearrange("p g c -> p (g c)"), sin_d).then_inc(tab_in[2], 16)
            pool.dma_start(ce[:].rearrange("p g k h -> p (g k h)"), ce_d).then_inc(tab_in[3], 16)
            pool.wait_ge(tc_done, 4)
            link(pool.memset(toep[:], 0.0))
            kt_v = kt_d.rearrange("h (g n) -> h g n", g=G)
            for r in range(T):
                n = GH * (r + 1)
                pool.dma_start(toep[GH * r:GH * (r + 1), :, P - n:P], kt_v[:, :, 0:n]).then_inc(toep_in, 16)
            pool.wait_ge(zx_ready, 4)
            pool.wait_ge(tab_in[2], 16)
            tt(zx[:], zx[:], sinT[:], ALU.mult).then_inc(zx_sin, 1)
            pool.wait_ge(gx_ready, 1)
            tt(zg[:], zg[:], sinT[:], ALU.mult).then_inc(gx_sin, 1)
            pool.wait_ge(hs_ready, 1)
            pool.wait_ge(gelu_ready, 4)
            pool.wait_ge(ty_done, 4)
            pool.dma_start(dist[:], dist_in).then_inc(dist_in_s, 16)
            pool.wait_ge(dist_in_s, 16)
            for h in range(H):
                slope = 2.0 ** (-8.0 * (h + 1) / H)
                pool.tensor_scalar(bias[h // 4][:, h % 4, :], dist[:], -slope * HD ** 0.5, None,
                                   ALU.mult).then_inc(bias_ready, 1)
            pool.wait_ge(rstd_ready, 4)
            for i in range(5, DT):
                pool.wait_ge(xg_ready, i + 1)
                tt(xg[:, i, :], xg[:, i, :], rstd[:], ALU.mult).then_inc(fin_pool, 1)


def kernel(**inputs):
    import numpy as np
    import concourse.bacc as bacc
    from concourse.bass_utils import run_bass_kernel_spmd

    a = {k: np.asarray(v) for k, v in inputs.items()}

    def tiles(w):
        k, m = w.shape
        return w.reshape(k // P, P, m // P, P).transpose(2, 1, 0, 3).reshape(m // P, P, k)

    def column(v):
        return v.reshape(-1, P).T

    def states(re, im):
        return np.concatenate([np.moveaxis(re, 1, 0), np.moveaxis(im, 1, 0)])

    ffns = ("ffn1", "ffn2")
    w_in = tiles(a["w_in"][0])
    glu = tiles(a["w_ssm_glu"][0])
    q, k, v, u = (w_in[AT * i:AT * (i + 1)] for i in range(4))
    br, bi = a["ssm_b_re"][0], a["ssm_b_im"][0]
    cr, ci = (a[n][0].transpose(0, 2, 1) for n in ("ssm_c_re", "ssm_c_im"))
    lre, lim = a["ssm_lambda_re"][0], a["ssm_lambda_im"][0]
    multiples = np.concatenate([np.arange(NA), np.arange(NB), np.arange(NB)]).astype(np.float32)
    signs = np.ones((P, 2), np.float32)
    signs[:NS, 0] = signs[NS:, 1] = -1
    rows, cols = np.arange(P)[:, None], np.arange(S)[None, :]
    dist = (rows + S - P - cols).astype(np.float32)
    dist[dist < 0] = 1e30
    arrays = {
        "x": a["x"][0].reshape(S, DT, P).transpose(2, 1, 0),
        "gains": np.stack([column(a[n].reshape(-1)) for n in ("ffn1_norm", "mix_norm", "ffn2_norm", "final_norm")], 1),
        "w_up": np.stack([np.stack([tiles(a[f"{f}_w_{n}"][0]) for n in ("gate", "up")], 1) for f in ffns]),
        "w_down": np.stack([tiles(a[f"{f}_w_down"][0]) for f in ffns]),
        "w_proj": np.concatenate([u, k, q, v]),
        "w_merge": np.concatenate([w_in[4 * AT:4 * AT + DT], w_in[4 * AT + DT:], tiles(a["w_attn_up"][0]),
                                   glu[:DT], glu[DT:]], 2),
        "w_out": tiles(a["w_out"][0]),
        "lam_re": states(lre, lre), "lam_im": states(lim, lim),
        "log_dt": np.broadcast_to(a["ssm_log_dt"], (P, G)),
        "b_own": states(br, bi), "b_swap": states(bi, br), "c_own": states(cr, ci), "c_swap": states(ci, cr),
        "ssm_d": a["ssm_d"][0],
        "ident": np.eye(P, dtype=np.float32), "multiples": np.broadcast_to(multiples, (P, NK)),
        "signs": signs, "dist": dist,
    }
    arrays = {n: np.ascontiguousarray(v) for n, v in arrays.items()}
    nc = bacc.Bacc("TRN2", target_bir_lowering=False, num_devices=1)
    args = [nc.dram_tensor(n, v.shape, mybir.dt.float32, kind="ExternalInput").ap() for n, v in arrays.items()]
    out = nc.dram_tensor("out", (P, DT, S), mybir.dt.float32, kind="ExternalOutput").ap()
    hybrid(nc, *args, out)
    r = run_bass_kernel_spmd(nc, [arrays], core_ids=[0])
    y = r.results[0]["out"]
    return y.reshape(P, DT, S).transpose(2, 1, 0).reshape(1, S, D)
```

```python
from contextlib import ExitStack

import concourse.bass as bass
from concourse import mybir

ALU = mybir.AluOpType
ACT = mybir.ActivationFunctionType
F32 = mybir.dt.float32
F32R = mybir.dt.float32r

P = 128
D, S, F = 1024, 512, 2816
DT, FT = D // P, F // P
H, HD = 8, 64
AW = H * HD
AT = AW // P
G, GH, NS = 32, 16, 64
T = 8
C = S // T
QT = S // P
EPS = 1e-6

DOWN_PARTS = ((0, 8), (8, 15), (15, 22))
UP0 = (0, 132)
DN0 = (44, 176)
PRJ0, ATT0, MRG0, OUT0, CHUNKS = 68, 84, 92, 124, 200
MK = 5
RAW = 4
HL = 2

NA, NB = T + 1, 8
NK = NA + 2 * NB
PI = 3.141592653589793
MAGIC = 12582912.0
TWO_PI = (6.28125, 0.0019340515136718750, 1.2556659146e-06)

BASE = 16512
X_AT = BASE
AH_AT = X_AT + DT * S * 4
RAW_AT = AH_AT + 2 * DT * S * 4
HL_AT = RAW_AT + RAW * D * 4
HID_AT = HL_AT + 2 * HL * D * 4
SPARE_AT = HID_AT + 2 * FT * S * 4
SPARE = 18432
WORK_AT = SPARE_AT + SPARE


def hybrid(nc, x, gains, w_up, w_down, w_proj, w_gate, w_merge, w_out, lam_re, lam_im, log_dt, b_own,
           b_swap, c_own, c_swap, ssm_d, ident_in, multiples_in, signs_in, dist_in, out):
    with ExitStack() as ctx:
        at = [WORK_AT]

        def place(name, shape, offset, dt=F32):
            return nc.alloc_sbuf_tensor_at(name, shape, dt, offset=offset)

        def work(name, shape, dt=F32):
            n = 4
            for s in shape[1:]:
                n *= s
            n = -(-n // 32) * 32
            at[0] += n
            assert at[0] <= 229344, at[0]
            return place(name, shape, at[0] - n, dt)

        def sem(name):
            return ctx.enter_context(nc.semaphore(name))

        xT = place("xT", [P, DT, S], X_AT)
        ah = place("ah", [P, DT, S], AH_AT, F32R)
        al = place("al", [P, DT, S], AH_AT + DT * S * 4, F32R)
        xg = place("xg", [P, DT, S], AH_AT)
        raw = place("raw", [P, RAW, D], RAW_AT)
        wh = place("wh", [P, HL, D], HL_AT, F32R)
        wl = place("wl", [P, HL, D], HL_AT + HL * D * 4, F32R)
        gs = work("gs", [P, 2, S])
        sg = work("sg", [P, 2, S])
        us = work("us", [P, S])
        hid = work("hid", [P, 2, S])
        rstd = work("rstd", [P, S])
        acc = work("acc", [P, S])
        sq = work("sq", [P, S])
        ident = work("ident", [P, P])
        ones = work("ones", [P, P])
        gain = work("gain", [P, 4, DT])
        eps = work("eps", [P, 1])
        signs = work("signs", [P, 2])
        mx = work("mx", [P, QT * H])
        nmx = work("nmx", [P, QT * H])
        sums = work("sums", [P, QT * H])
        rec = work("rec", [P, QT * H])
        mag8 = work("mag8", [P, G])

        hp = place("hp", [P, FT, 2, S], HID_AT, F32R)

        PX = HID_AT + 13 * 2 * S * 4
        PY = PX + G * NA * GH * 4
        winT = place("winT", [P, G, T, GH], PX)
        ce_w = place("ce_w", [P, G, NA, GH], PX)
        tmpW = place("tmpW", [P, G, T, GH], PY)
        tmpC = place("tmpC", [P, G, NA, GH], PY)
        winS = place("winS", [P, G, P], PY)
        cosS = place("cosS", [P, G, NB, NB], PY)
        sinS = place("sinS", [P, G, NB, NB], PY + 8192)
        tmpR = place("tmpR", [P, 8, NB, NB], PY + 16384)
        ktS = place("ktS", [GH, G, NB, GH], PY)
        dB = place("dB", [GH, G, GH], PX)
        ang = place("ang", [P, G, NK], PX)
        tn = place("tn", [P, G * NK], PX + 4 * G * NK)
        mag = place("mag", [P, G, NA], PX + 8 * G * NK)
        expo = place("expo", [P, G, NA], PX + 8 * G * NK + 4 * G * NA)
        mult = place("mult", [P, NK], PX + 8 * G * NK + 8 * G * NA)
        bO = place("bO", [P, G, GH], PY)
        bS = place("bS", [P, G, GH], PY + 2048)
        cR = place("cR", [P, G, GH], PY + 4096)
        tmpB = place("tmpB", [P, G, GH], PY + 6144)
        small = place("small", [P, 24, G], PY + 8192)
        sn = place("sn", [P, G, NK], SPARE_AT)
        cs = place("cs", [P, G, NK], SPARE_AT + 4 * G * NK)
        s2 = SPARE_AT + 8 * G * NK
        er = place("er", [P, G, NA], s2)
        ei = place("ei", [P, G, NA], s2 + 4 * G * NA)
        s3 = s2 + 8 * G * NA
        bb = place("bb", [P, G, GH], s3)
        bbS = place("bbS", [P, G, GH], s3 + 2048)
        cO = place("cO", [P, G, GH], s3 + 4096)
        cA = place("cA", [P, G, GH], s3 + 6144)

        R = HID_AT
        prj = place("prj", [P, 4 * AT, S], R)
        uc = place("uc", [P, G, C], R)
        win = place("win", [P, G, P], R + 32768)
        zg = place("zg", [P, G, C], R + 32768)
        zx = place("zx", [P, G, C], R + 40960)
        y_ = place("y_", [P, 2, T, P], R + 32768)
        ce = place("ce", [P, G, NA, GH], R + 49152)
        yh = place("yh", [P, AT, S], R + 49152, F32R)
        yl = place("yl", [P, AT, S], R + 57344, F32R)
        u_ = place("u_", [C, G, T, GH], R + 67584)
        toep = place("toep", [P, G, P], R + 67584)
        cosT = place("cosT", [P, G, C], R + 83968)
        sinT = place("sinT", [P, G, C], R + 92160)
        hs = place("hs", [P, G, C], R + 100352)
        bias = place("bias", [P, 4, S], R + 40960)
        v_ = place("v_", [P, QT, AW], R + 83968)
        ga = place("ga", [P, DT, S], R + 67584)
        sc = place("sc", [P, 2, S], R + 92160)
        pr = place("pr", [P, 4, S], R + 96256)
        pts = place("pts", [P, 2, S], R + 104448)
        ao = place("ao", [P, 2, S], R + 32768)
        th = place("th", [P, AT, S], R, F32R)
        tl = place("tl", [P, AT, S], R + 24576, F32R)
        mh = place("mh", [P, DT, S], R + 8192, F32R)
        ml = place("ml", [P, DT, S], R + 67584, F32R)

        dist = hid[:, 0, :]

        def scratch(name, shape):
            return nc.dram_tensor(name, shape, F32, kind="Internal").ap()

        win_d = scratch("win_d", [P, G * P])
        ce_d = scratch("ce_d", [P, G * NA * GH])
        cos_d = scratch("cos_d", [P, G * C])
        sin_d = scratch("sin_d", [P, G * C])
        kt_d = scratch("kt_d", [GH, G * P])

        bank = [ctx.enter_context(nc.psum_tensor(f"bank{i}", [P, S], F32)) for i in range(8)]

        landed = [sem(f"landed{i}") for i in range(RAW)]
        hi_ready = sem("hi_ready")
        lo_ready = sem("lo_ready")
        chunk_done = sem("chunk_done")
        x_in = [sem(f"x_in{i}") for i in range(4)]
        c_in = sem("c_in")
        s_in = sem("s_in")
        set_up = sem("set_up")
        x_new = sem("x_new")
        sq_ready, acc_ready = sem("sq_ready"), sem("acc_ready")
        ah_ready, al_ready = sem("ah_ready"), sem("al_ready")
        ss_ready, rt_ready, rstd_ready = sem("ss_ready"), sem("rt_ready"), sem("rstd_ready")
        gate_out, up_out = sem("gate_out"), sem("up_out")
        silu_ready, hid_ready = sem("silu_ready"), sem("hid_ready")
        hh_ready, hl_ready = sem("hh_ready"), sem("hl_ready")
        cd = sem("cd")
        ca = sem("ca")
        cp = sem("cp")
        prep_dve = sem("prep_dve")
        prep_act = sem("prep_act")
        winT_ready, winT_turned, win_out = sem("winT_ready"), sem("winT_turned"), sem("win_out")
        ce_ready, kt_done, kt_out = sem("ce_ready"), sem("kt_done"), sem("kt_out")
        stored = sem("stored")
        tab_in = [sem(f"tab_in{i}") for i in range(4)]
        toep_in = sem("toep_in")
        d_in = sem("d_in")
        dist_in_s = sem("dist_in_s")
        prj_out = sem("prj_out")
        tu_done, u_act, u_dve = sem("tu_done"), sem("u_act"), sem("u_dve")
        tc_done, uc_act, uc_dve = sem("tc_done"), sem("uc_act"), sem("uc_dve")
        z_done, zx_ready, zx_sin, zg_ready = sem("z_done"), sem("zx_ready"), sem("zx_sin"), sem("zg_ready")
        scan_ready, gx_ready, gx_sin, hs_ready = sem("scan_ready"), sem("gx_ready"), sem("gx_sin"), sem("hs_ready")
        y_done, gelu_ready = sem("y_done"), sem("gelu_ready")
        tv_done, v_out = sem("tv_done"), sem("v_out")
        ty_done, yh_ready, yl_ready = sem("ty_done"), sem("yh_ready"), sem("yl_ready")
        bias_ready = sem("bias_ready")
        sc_done, nmx_ready, exp_ready = sem("sc_done"), sem("nmx_ready"), sem("exp_ready")
        pt_done, pt_out, pv_done = sem("pt_done"), [sem("pt_out0"), sem("pt_out1")], sem("pv_done")
        ao_ready, at_done, th_ready, tl_ready = sem("ao_ready"), sem("at_done"), sem("th_ready"), sem("tl_ready")
        ga_out, gs_out, sga_ready, sgs_ready, sgy_ready = (sem("ga_out"), sem("gs_out"), sem("sga_ready"),
                                                           sem("sgs_ready"), sem("sgy_ready"))
        me = sem("me")
        au_out, yv_out = sem("au_out"), sem("yv_out")
        mg_ready, mh_ready, ml_ready = sem("mg_ready"), sem("mh_ready"), sem("ml_ready")
        xg_ready, fin_dve, fin_pool, out_done = sem("xg_ready"), sem("fin_dve"), sem("fin_pool"), sem("out_done")

        class Count:

            def __init__(self, s):
                self.s, self.n = s, 0

            def step(self, ins):
                self.n += 1
                ins.then_inc(self.s, 1)

            def link(self, eng, ins):
                self.step(ins)
                eng.wait_ge(self.s, self.n)

        def split_hi(act, c, slot, kts, first=False):
            act.wait_ge(landed[slot % RAW], 16 * (c // RAW + 1) if isinstance(c, int) else (c - slot % RAW) * (16 // RAW) + 16)
            if not first:
                act.wait_ge(chunk_done, c - 1)
            act.activation(wh[:, slot % HL, 0:kts * P], raw[:, slot % RAW, 0:kts * P], ACT.Copy).then_inc(hi_ready, 1)

        def split_lo(dve, c, slot, kts):
            dve.wait_ge(hi_ready, c + 1)
            dve.tensor_tensor(wl[:, slot % HL, 0:kts * P], raw[:, slot % RAW, 0:kts * P],
                              wh[:, slot % HL, 0:kts * P].bitcast(F32), ALU.subtract).then_inc(lo_ready, 1)

        def w_tile(slot, k):
            return wh[:, slot % HL, k * P:(k + 1) * P], wl[:, slot % HL, k * P:(k + 1) * P]

        def three(pe, ps, slot, k, r_hi, r_lo, first, last):
            w_hi, w_lo = w_tile(slot, k)
            pe.matmul(ps, w_hi, r_hi, start=first, stop=False)
            pe.matmul(ps, w_hi, r_lo, start=False, stop=False)
            return pe.matmul(ps, w_lo, r_hi, start=False, stop=last)

        def norm_act(act, n, i):
            if n == 0:
                act.wait_ge(x_in[i // 2], 16)
            else:
                act.wait_ge(x_new, 8 * (n - 1) + i + 1)
            if n < 3:
                act.activation(ah[:, i, :], xT[:, i, :], ACT.Copy, scale=gain[:, n, i:i + 1]).then_inc(ah_ready, 1)
            if 8 * n + i > 0:
                act.wait_ge(acc_ready, 8 * n + i)
            act.activation(sq[:], xT[:, i, :], ACT.Square).then_inc(sq_ready, 1)
            if n == 3:
                act.activation(xg[:, i, :], xT[:, i, :], ACT.Copy, scale=gain[:, n, i:i + 1]).then_inc(xg_ready, 1)

        def norm_dve(dve, n, i):
            if n < 3:
                dve.wait_ge(ah_ready, 8 * n + i + 1)
                dve.scalar_tensor_tensor(al[:, i, :], xT[:, i, :], gain[:, n, i:i + 1], ah[:, i, :].bitcast(F32),
                                         ALU.mult, ALU.subtract).then_inc(al_ready, 1)
            dve.wait_ge(sq_ready, 8 * n + i + 1)
            if i == 0:
                if n > 0:
                    dve.wait_ge(ss_ready, n)
                dve.tensor_copy(acc[:], sq[:]).then_inc(acc_ready, 1)
            else:
                dve.wait_ge(acc_ready, 8 * n + i)
                dve.tensor_tensor(acc[:], acc[:], sq[:], ALU.add).then_inc(acc_ready, 1)

        def stat_pe(pe, n):
            pe.wait_ge(acc_ready, 8 * (n + 1))
            if n > 0:
                pe.wait_ge(rt_ready, n)
            pe.matmul(bank[7][:], ones[:], acc[:], start=True, stop=True).then_inc(ss_ready, 1)

        def stat_act(act, n):
            act.wait_ge(ss_ready, n + 1)
            act.activation(sq[:], bank[7][:], ACT.Sqrt, scale=1.0 / D, bias=eps[:, 0:1]).then_inc(rt_ready, 1)

        def stat_dve(dve, n):
            dve.wait_ge(rt_ready, n + 1)
            dve.reciprocal(rstd[:], sq[:]).then_inc(rstd_ready, 1)
            dve.wait_ge(rstd_ready, n + 1)

        def gu_pe(pe, n, f, b, known=True, norm=None):
            c0, g0 = UP0[n], FT * n
            for part in (0, 1):
                pe.wait_ge(lo_ready, c0 + 2 * f + part + 1)
                if known:
                    pe.wait_ge(up_out if part else gate_out, g0 + f - 1)
                for k in range(DT):
                    if norm is not None and part == 0:
                        pe.wait_ge(al_ready, 8 * norm + k + 1)
                    mm = three(pe, bank[2 * part + b][:], part, k, ah[:, k, :], al[:, k, :], k == 0, k == DT - 1)
                mm.then_inc(chunk_done, 1)
                if norm is not None and part == 0:
                    stat_pe(pe, norm)

        def gu_up_dve(dve, n, f, b):
            c0, g0 = UP0[n], FT * n
            dve.wait_ge(chunk_done, c0 + 2 * f + 2)
            dve.tensor_tensor(us[:], bank[2 + b][:], rstd[:], ALU.mult).then_inc(up_out, 1)
            dve.wait_ge(up_out, g0 + f + 1)
            dve.wait_ge(silu_ready, g0 + f + 1)
            dve.tensor_tensor(hid[:, b, :], sg[:, b, :], us[:], ALU.mult).then_inc(hid_ready, 1)

        def gu_low_dve(dve, n, f, b):
            dve.wait_ge(hh_ready, FT * n + f + 1)
            dve.tensor_tensor(hp[:, f, 1, :], hid[:, b, :], hp[:, f, 0, :].bitcast(F32), ALU.subtract).then_inc(hl_ready, 1)

        def gu_gate_dve(dve, n, f, b):
            dve.wait_ge(chunk_done, UP0[n] + 2 * f + 1)
            dve.tensor_tensor(gs[:, b, :], bank[b][:], rstd[:], ALU.mult).then_inc(gate_out, 1)

        def gu_hid_act(act, n, f, b):
            act.wait_ge(hid_ready, FT * n + f + 1)
            act.activation(hp[:, f, 0, :], hid[:, b, :], ACT.Copy).then_inc(hh_ready, 1)

        def gu_silu_act(act, n, f, b):
            act.wait_ge(gate_out, FT * n + f + 1)
            act.activation(sg[:, b, :], gs[:, b, :], ACT.Silu).then_inc(silu_ready, 1)

        def gu_dve(dve, n, f, b, c4, first=False, norm=None):
            c = UP0[n] + 2 * f
            split_lo(dve, c + 1, c4 + 1, DT)
            if norm is not None:
                stat_dve(dve, norm)
            if not first:
                gu_up_dve(dve, n, f - 1, 1 - b)
                gu_low_dve(dve, n, f - 1, 1 - b)
            split_lo(dve, c + 2, c4 + 2, DT)
            gu_gate_dve(dve, n, f, b)

        def gu_act(act, n, f, b, c4, first=False, norm=None):
            c = UP0[n] + 2 * f
            split_hi(act, c + 1, c4 + 1, DT, first=(n == 0 and first))
            if norm is not None:
                stat_act(act, norm)
            if not first:
                gu_hid_act(act, n, f - 1, 1 - b)
            split_hi(act, c + 2, c4 + 2, DT)
            gu_silu_act(act, n, f, b)

        def gu_loop(eng, n, one, f0, f1):
            with eng.Fori(f0 // 2, f1 // 2) as j:
                for b in (0, 1):
                    if one is gu_pe:
                        one(eng, n, 2 * j + b, b)
                    else:
                        one(eng, n, 2 * j + b, b, 2 * b)

        def down_pe(pe, n, m, b, slot0, first=False):
            d0 = DN0[n]
            if not first:
                pe.wait_ge(x_new, X_DOWN[n] + m - 1)
            for i, (k0, k1) in enumerate(DOWN_PARTS):
                pe.wait_ge(lo_ready, d0 + 3 * m + i + 1)
                for k in range(k0, k1):
                    if first and b == 0 and k == FT - 1:
                        pe.wait_ge(hl_ready, FT * (n + 1))
                    mm = three(pe, bank[4 + b][:], slot0 + i, k - k0, hp[:, k, 0, :], hp[:, k, 1, :],
                               k == 0, k == FT - 1)
                mm.then_inc(chunk_done, 1)

        X_DOWN = (0, 16)

        def x_dve(dve, done, ps, m, factor):
            dve.wait_ge(chunk_done, done)
            dve.scalar_tensor_tensor(xT[:, m, :], ps[:], factor, xT[:, m, :], ALU.mult, ALU.add).then_inc(x_new, 1)

        def part_len(i):
            return DOWN_PARTS[i % 3][1] - DOWN_PARTS[i % 3][0]

        def win_bank(g):
            return bank[(4, 5, 6, 7)[g // 4 % 4]]

        def out_pe(pe, m, b, first=False):
            pe.wait_ge(lo_ready, OUT0 + m + 1)
            if not first:
                pe.wait_ge(x_new, 8 + m - 1)
            for k in range(DT):
                if first and b == 0:
                    pe.wait_ge(ml_ready, k + 1)
                mm = three(pe, bank[5 + b][:], b, k, mh[:, k, :], ml[:, k, :], k == 0, k == DT - 1)
            mm.then_inc(chunk_done, 1)

        def gu_act_first2(act):
            c = UP0[1]
            split_hi(act, c + 1, 1, DT)
            norm_act(act, 2, DT - 1)
            stat_act(act, 2)
            split_hi(act, c + 2, 2, DT)
            gu_silu_act(act, 1, 0, 0)

        def turned_u(op, n, *a):
            o = u_[:, 8 * (n // 2):8 * (n // 2) + 8, 4 * (n % 2):4 * (n % 2) + 4, :]
            i = bank[2 + n % 4][0:C, :].rearrange("c (t g h) -> c g t h", t=4, g=8)
            return op(o, i, *a)

        def turned_y(dst, n, half):
            gt, q = n // 2, n % 2
            o = dst[:, gt + 2 * half, :].rearrange("p (c t) -> p t c", t=T)[:, 4 * q:4 * q + 4, :]
            i = bank[4 + n][:].rearrange("p (t b c) -> p t b c", t=4, b=2)[:, :, half, :]
            return o, i

        UNITS = AT * QT

        def pt_evac(eng, op, u, head, *a):
            w = (u % QT + 1) * P
            eng.wait_ge(pt_done, 2 * u + head + 1)
            op(pts[:, head, 0:w], bank[4 + head][:, 0:w], *a).then_inc(pt_out[head], 1)

        def attn_hi(act, i):
            act.wait_ge(at_done, i + 1)
            act.activation(th[:, i, :], bank[7][:], ACT.Copy).then_inc(th_ready, 1)

        def attn_lo(dve, i):
            dve.wait_ge(th_ready, i + 1)
            dve.tensor_tensor(tl[:, i, :], bank[7][:], th[:, i, :].bitcast(F32), ALU.subtract).then_inc(tl_ready, 1)

        def down_act(act, n):
            for m in range(DT):
                c = DN0[n] + 3 * m
                split_hi(act, c + 1, 3 * m + 1, part_len(1))
                if m == 0:
                    gu_hid_act(act, n, FT - 1, 1)
                split_hi(act, c + 2, 3 * m + 2, part_len(2))
                if m:
                    norm_act(act, 1 if n == 0 else 3, m - 1)
                if c + 3 < CHUNKS:
                    split_hi(act, c + 3, 3 * m + 3, DT)

        def down_dve(dve, n):
            for m in range(DT):
                c = DN0[n] + 3 * m
                split_lo(dve, c + 1, 3 * m + 1, part_len(1))
                if m == 0:
                    gu_up_dve(dve, n, FT - 1, 1)
                    gu_low_dve(dve, n, FT - 1, 1)
                else:
                    x_dve(dve, c, bank[4 + (m - 1) % 2], m - 1, 0.5)
                split_lo(dve, c + 2, 3 * m + 2, part_len(2))
                if m:
                    norm_dve(dve, 1 if n == 0 else 3, m - 1)
                if c + 3 < CHUNKS:
                    split_lo(dve, c + 3, 3 * m + 3, DT)

        def prj_dve(dve, i):
            dve.wait_ge(chunk_done, PRJ0 + i + 1)
            dve.tensor_tensor(prj[:, i, :], bank[i % 2][:], rstd[:], ALU.mult).then_inc(prj_out, 1)

        def attn_norm(dve, link, i):
            n = 2 * QT
            dve.wait_ge(pv_done, (i + 1) * QT)
            link(dve.reciprocal(rec[:, i * n:(i + 1) * n], sums[:, i * n:(i + 1) * n]))
            dve.tensor_tensor(ao[:, i % 2, :].rearrange("p (n d) -> p n d", n=n),
                              bank[6][:].rearrange("p (n d) -> p n d", n=n),
                              rec[:, i * n:(i + 1) * n].unsqueeze(2).to_broadcast([P, n, HD]),
                              ALU.mult).then_inc(ao_ready, 1)

        block = ctx.enter_context(nc.Block())

        @block.sync
        def _(sp):
            def load(c, slot, src, n, first=False):
                if not first:
                    sp.wait_ge(lo_ready, c - RAW + 1)
                sp.dma_start(raw[:, slot % RAW, 0:n * P], src).then_inc(landed[slot % RAW], 16)

            def up_loads(n, f0):
                with sp.Fori(f0 // 2, FT // 2) as i:
                    for j in range(4):
                        load(UP0[n] + 4 * i + j, j, w_up[n, 2 * i + j // 2, j % 2], DT)

            def down_loads(n):
                with sp.Fori(0, DT // 4) as i:
                    for j in range(12):
                        k0, k1 = DOWN_PARTS[j % 3]
                        load(DN0[n] + 12 * i + j, j, w_down[n, 4 * i + j // 3, :, k0 * P:k1 * P], k1 - k0)

            for j in range(2):
                sp.dma_start(xT[:, 2 * j:2 * j + 2, :], x[:, 2 * j:2 * j + 2, :]).then_inc(x_in[j], 16)
                load(j, j, w_up[0, 0, j], DT, first=True)
            for j in range(2, 4):
                sp.dma_start(xT[:, 2 * j:2 * j + 2, :], x[:, 2 * j:2 * j + 2, :]).then_inc(x_in[j], 16)
                load(j, j, w_up[0, 1, j % 2], DT, first=True)
            up_loads(0, 2)
            down_loads(0)
            with sp.Fori(0, AT) as i:
                for j in range(4):
                    load(PRJ0 + 4 * i + j, j, w_proj[4 * i + j], DT)
            with sp.Fori(0, DT // 4) as i:
                for j in range(4):
                    load(ATT0 + 4 * i + j, j, w_gate[4 * i + j], DT)
            with sp.Fori(0, DT) as m:
                for j in range(4):
                    load(MRG0 + 4 * m + j, j, w_merge[m, :, MK * j * P:MK * (j + 1) * P], MK)
            with sp.Fori(0, DT // 4) as i:
                for j in range(4):
                    load(OUT0 + 4 * i + j, j, w_out[4 * i + j], DT)
            up_loads(1, 0)
            down_loads(1)
            for i in range(DT):
                if i < 5:
                    sp.wait_ge(fin_dve, i + 1)
                else:
                    sp.wait_ge(fin_pool, i - 4)
                sp.dma_start(out[:, i, :], xg[:, i, :]).then_inc(out_done, 16)
            sp.wait_ge(out_done, 16 * DT)

        @block.tensor
        def _(pe):
            gu_pe(pe, 0, 0, 0, known=False, norm=0)
            gu_pe(pe, 0, 1, 1, known=False)
            gu_loop(pe, 0, gu_pe, 2, 4)
            pe.wait_ge(winT_ready, 1)
            pe.wait_ge(c_in, 16 * 4)
            for g in range(G):
                if g >= 16 and g % 4 == 0:
                    pe.wait_ge(win_out, g // 4 - 3)
                tr = pe.transpose(win_bank(g)[:, (g % 4) * P:(g % 4 + 1) * P],
                                  winT[:, g, :, :].rearrange("p t h -> p (t h)"), ident[:])
                if g % 4 == 3:
                    tr.then_inc(winT_turned, 1)
            gu_loop(pe, 0, gu_pe, 4, 14)
            pe.wait_ge(ce_ready, 1)
            for g in range(G):
                if g >= 16 and g % 4 == 0:
                    pe.wait_ge(kt_out, g // 4 - 3)
                mm = pe.matmul(win_bank(g)[0:GH, (g % 4) * P:(g % 4 + 1) * P], bb[:, g, :],
                               ce_w[:, g, 0:T, :].rearrange("p k h -> p (k h)"), start=True, stop=True)
                if g % 4 == 3:
                    mm.then_inc(kt_done, 1)
            gu_loop(pe, 0, gu_pe, 14, FT)
            down_pe(pe, 0, 0, 0, 0, first=True)
            down_pe(pe, 0, 1, 1, 1, first=True)
            with pe.Fori(1, DT // 2) as j:
                for b in (0, 1):
                    down_pe(pe, 0, 2 * j + b, b, b)

            def prj_pe(i, b, known=True, norm=None):
                pe.wait_ge(lo_ready, PRJ0 + i + 1)
                if known:
                    pe.wait_ge(prj_out, i - 1)
                for k in range(DT):
                    if norm is not None:
                        pe.wait_ge(al_ready, 8 * norm + k + 1)
                    mm = three(pe, bank[b][:], b, k, ah[:, k, :], al[:, k, :], k == 0, k == DT - 1)
                mm.then_inc(chunk_done, 1)
                if norm is not None:
                    stat_pe(pe, norm)

            def turn_u(r):
                pe.wait_ge(prj_out, AT)
                for ct in (2 * r, 2 * r + 1):
                    for q in (0, 1):
                        n = 2 * ct + q
                        if n >= 4:
                            pe.wait_ge(u_act if n % 2 == 0 else u_dve, (n - 4) // 2 + 1)
                        for j in range(4):
                            t = T - 1 - (4 * q + j)
                            tr = pe.transpose(bank[2 + n % 4][0:C, j * P:(j + 1) * P],
                                              prj[:, ct, t:S:T], ident[:])
                        tr.then_inc(tu_done, 1)

            prj_pe(0, 0, known=False, norm=1)
            prj_pe(1, 1, known=False)
            prj_pe(2, 0)
            prj_pe(3, 1)
            prj_pe(4, 0)
            turn_u(0)
            prj_pe(5, 1)
            turn_u(1)
            prj_pe(6, 0)
            pe.wait_ge(u_act, 4)
            pe.wait_ge(u_dve, 4)
            for g in range(G):
                tr = pe.transpose(bank[2 + g // 8][:, (g % 8) * C:(g % 8 + 1) * C],
                                  u_[:, g, :, :].rearrange("c t h -> c (t h)"), ident[0:C, 0:C])
                if g % 8 == 7:
                    tr.then_inc(tc_done, 1)
            prj_pe(7, 1)
            pe.wait_ge(tab_in[0], 16)
            for g in range(G):
                if g % 8 == 0:
                    pe.wait_ge(uc_act if g // 8 % 2 == 0 else uc_dve, g // 16 + 1)
                mm = pe.matmul(bank[2 + g // 8][:, (g % 8) * C:(g % 8 + 1) * C], win[:, g, :], uc[:, g, :],
                               start=True, stop=True)
                if g % 8 == 7:
                    mm.then_inc(z_done, 1)
            with pe.Fori(4, 2 * AT) as j:
                for b in (0, 1):
                    prj_pe(2 * j + b, b)

            pe.wait_ge(tab_in[3], 16)
            pe.wait_ge(toep_in, 16 * T)
            pe.wait_ge(hs_ready, 1)
            for j in range(G // 2):
                for half in (0, 1):
                    g = j + G // 2 * half
                    ps = bank[2 + j // 4][C * half:C * (half + 1), (j % 4) * P:(j % 4 + 1) * P]
                    pe.matmul(ps, uc[:, g, :], toep[:, g, :], start=True, stop=False)
                    mm = pe.matmul(ps, hs[:, g, :], ce[:, g, 1:NA, :].rearrange("p k h -> p (k h)"),
                                   start=False, stop=True)
                if j % 4 == 3:
                    mm.then_inc(y_done, 1)
            pe.wait_ge(prj_out, 4 * AT)
            for kb in range(QT):
                for i in range(AT):
                    tr = pe.transpose(bank[(0, 1, 6, 7)[kb]][:, i * P:(i + 1) * P],
                                      prj[:, 3 * AT + i, kb * P:(kb + 1) * P], ident[:])
                tr.then_inc(tv_done, 1)

            def scores(u):
                i, qt = u // QT, u % QT
                if u == 0:
                    pe.wait_ge(gelu_ready, 2)
                else:
                    pe.wait_ge(nmx_ready, u)
                for head in (0, 1):
                    rows = slice(HD * head, HD * (head + 1))
                    mm = pe.matmul(bank[2 + head][:, 0:(qt + 1) * P], prj[rows, 2 * AT + i, qt * P:(qt + 1) * P],
                                   prj[rows, AT + i, 0:(qt + 1) * P], start=True, stop=True)
                mm.then_inc(sc_done, 1)

            def turn_p(u):
                qt = u % QT
                if u == 0:
                    pe.wait_ge(yl_ready, 8)
                pe.wait_ge(exp_ready, u + 1)
                for head in (0, 1):
                    for kb in range(qt + 1):
                        tr = pe.transpose(bank[4 + head][:, kb * P:(kb + 1) * P],
                                          pr[:, 2 * (u % 2) + head, kb * P:(kb + 1) * P], ident[:])
                    tr.then_inc(pt_done, 1)

            def pv(u):
                i, qt = u // QT, u % QT
                if qt == 0 and i:
                    pe.wait_ge(ao_ready, i)
                for head in (0, 1):
                    pe.wait_ge(pt_out[head], u + 1)
                    n = 2 * qt + head
                    for kb in range(qt + 1):
                        mm = pe.matmul(bank[6][:, n * HD:(n + 1) * HD], pts[:, head, kb * P:(kb + 1) * P],
                                       v_[:, kb, (2 * i + head) * HD:(2 * i + head + 1) * HD],
                                       start=(kb == 0), stop=(kb == qt))
                mm.then_inc(pv_done, 1)

            def turn_o(i):
                pe.wait_ge(ao_ready, i + 1)
                if i:
                    pe.wait_ge(tl_ready, i)
                for qt in range(QT):
                    tr = pe.transpose(bank[7][:, qt * P:(qt + 1) * P], ao[:, i % 2, qt * P:(qt + 1) * P], ident[:])
                tr.then_inc(at_done, 1)

            def turn_y():
                pe.wait_ge(gelu_ready, 4)
                pe.wait_ge(v_out, QT)
                for n in range(4):
                    for j in range(4):
                        tr = pe.transpose(bank[4 + n][:, j * P:(j + 1) * P], y_[:, n // 2, 4 * (n % 2) + j, :], ident[:])
                    tr.then_inc(ty_done, 1)

            def g_attn(s, k0):
                m = s // 2
                if s % 2 == 0 and k0 == 0:
                    pe.wait_ge(lo_ready, ATT0 + m + 1)
                    if m < 2:
                        pe.wait_ge(v_out, m + 1)
                    else:
                        pe.wait_ge(ga_out, m - 1)
                for k in range(k0 + 4 * (s % 2), k0 + 4 * (s % 2) + 2):
                    mm = three(pe, bank[m % 2][:], m, k, ah[:, k, :], al[:, k, :], k == 0, k == DT - 1)
                if k == DT - 1:
                    mm.then_inc(chunk_done, 1)

            for s in range(UNITS):
                scores(s)
                g_attn(s, 0)
                if s == 0:
                    turn_y()
                else:
                    turn_p(s - 1)
                g_attn(s, 2)
                if s:
                    pv(s - 1)
                if s % QT == 2 and s > QT:
                    turn_o(s // QT - 1)

            def merge_pe(m, first=False):
                def tile(kk):
                    j, k = kk // MK, kk % MK
                    if k == 0:
                        pe.wait_ge(lo_ready, MRG0 + 4 * m + j + 1)
                    if kk < DT:
                        if kk == 0 and not first:
                            pe.wait_ge(gs_out, m)
                        ps, r, rl, i, n = bank[0], ah, al, kk, DT
                    elif kk < DT + AT:
                        if first:
                            if kk == DT:
                                pe.wait_ge(ga_out, DT)
                            pe.wait_ge(tl_ready, kk - DT + 1)
                        elif kk == DT:
                            pe.wait_ge(au_out, m)
                        ps, r, rl, i, n = bank[1], th, tl, kk - DT, AT
                    elif kk < DT + 2 * AT:
                        if kk == DT + AT and not first:
                            pe.wait_ge(yv_out, m)
                        ps, r, rl, i, n = bank[2], yh, yl, kk - DT - AT, AT
                    else:
                        if kk == DT + 2 * AT and not first:
                            pe.wait_ge(sgy_ready, m)
                        ps, r, rl, i, n = bank[3], yh, yl, kk - DT - 2 * AT, AT
                    mm = three(pe, ps[:], j, k, r[:, i, :], rl[:, i, :], i == 0, i == n - 1)
                    if k == MK - 1:
                        mm.then_inc(chunk_done, 1)

                for kk in range(4 * MK):
                    tile(kk)
                    if first and kk == 1:
                        turn_p(UNITS - 1)
                    if first and kk == 4:
                        pv(UNITS - 1)
                    if first and kk == 8:
                        turn_o(AT - 1)

            pe.wait_ge(ga_out, DT - 1)
            merge_pe(0, first=True)
            with pe.Fori(1, DT) as m:
                merge_pe(m)

            for m in range(2):
                out_pe(pe, m, m, first=True)
            with pe.Fori(1, DT // 2) as j:
                for b in (0, 1):
                    out_pe(pe, 2 * j + b, b)

            gu_pe(pe, 1, 0, 0, known=False, norm=2)
            gu_pe(pe, 1, 1, 1, known=False)
            gu_loop(pe, 1, gu_pe, 2, FT)
            down_pe(pe, 1, 0, 0, 0, first=True)
            down_pe(pe, 1, 1, 1, 1, first=True)
            with pe.Fori(1, DT // 2) as j:
                for b in (0, 1):
                    down_pe(pe, 1, 2 * j + b, b, b)
            stat_pe(pe, 3)

        @block.scalar
        def _(act):
            A = Count(ca)
            act.wait_ge(set_up, 1)
            act.wait_ge(s_in, 16 * 7)
            act.activation(small[:, 3, :], small[:, 2, :], ACT.Exp).then_inc(prep_act, 1)
            act.wait_ge(c_in, 16 * 4)
            for i in range(DT):
                norm_act(act, 0, i)
                if i == 1:
                    split_hi(act, 0, 0, DT, first=True)
            gu_act(act, 0, 0, 0, 0, first=True, norm=0)
            act.wait_ge(prep_dve, 1)
            act.activation(mag[:, :, :], expo[:, :, :], ACT.Exp)
            act.activation(mag8[:, :], small[:, 22, :], ACT.Exp).then_inc(prep_act, 1)
            act.activation(sn[:, :, :], ang[:, :, :], ACT.Sin)
            act.activation(cs[:, :, :].rearrange("p g k -> p (g k)"), tn[:], ACT.Sin).then_inc(prep_act, 1)
            gu_act(act, 0, 1, 1, 2)
            gu_loop(act, 0, gu_act, 2, 4)
            for n in range(8):
                act.wait_ge(winT_turned, n + 1)
                act.activation(winS[:, 4 * n:4 * n + 4, :].rearrange("p g c -> p (g c)"),
                               bank[4 + n % 4][:], ACT.Copy).then_inc(win_out, 1)
            gu_loop(act, 0, gu_act, 4, 14)
            act.wait_ge(stored, 16 * 5)
            gu_loop(act, 0, gu_act, 14, FT)
            down_act(act, 0)

            zx_v = zx[:, :, :].rearrange("p g c -> p (g c)")
            for i in range(4 * AT):
                split_hi(act, PRJ0 + i + 1, i + 1, DT)
                if i == 0:
                    norm_act(act, 1, DT - 1)
                    stat_act(act, 1)
                if i in (5, 6):
                    for n in range(4 * (i - 5), 4 * (i - 4), 2):
                        act.wait_ge(tu_done, n + 1)
                        turned_u(act.activation, n, ACT.Copy).then_inc(u_act, 1)
                if i == 7:
                    for n in (0, 2):
                        act.wait_ge(tc_done, n + 1)
                        act.activation(uc[:, 8 * n:8 * n + 8, :].rearrange("p g c -> p (g c)"), bank[2 + n][:],
                                       ACT.Copy).then_inc(uc_act, 1)
                if i == 8:
                    act.wait_ge(z_done, 4)
                    for n in range(4):
                        cols = slice(n * S, (n + 1) * S)
                        act.activation(zx_v[0:NS, cols], bank[2 + n][NS:P, :], ACT.Copy)
                        act.activation(zx_v[NS:P, cols], bank[2 + n][0:NS, :], ACT.Copy, scale=-1.0).then_inc(zx_ready, 1)
                if i == 12:
                    act.wait_ge(scan_ready, G)
                    g_v = zg[:, :, :].rearrange("p g c -> p (g c)")
                    act.activation(g_v[0:NS, :], zx_v[NS:P, :], ACT.Copy, scale=-1.0)
                    act.activation(g_v[NS:P, :], zx_v[0:NS, :], ACT.Copy).then_inc(gx_ready, 1)
            for n in range(4):
                act.wait_ge(y_done, n + 1)
                o = y_[:, n // 2, :, 64 * (n % 2):64 * (n % 2) + 64].rearrange("p t (j h) -> p j t h", j=4)
                act.activation(o, bank[2 + n][:].rearrange("p (j t h) -> p j t h", j=4, t=T),
                               ACT.Gelu_apprx_tanh).then_inc(gelu_ready, 1)
            def act_slot(s):
                if s >= 1:
                    pt_evac(act, act.activation, s - 1, 0, ACT.Copy)
                if s == UNITS:
                    return
                w = (s % QT + 1) * P
                act.wait_ge(nmx_ready, s + 1)
                if s >= 2:
                    act.wait_ge(pt_done, 2 * (s - 1))
                for head in (0, 1):
                    u = 2 * s + head
                    exp = act.activation(pr[:, 2 * (s % 2) + head, 0:w], sc[:, head, 0:w], ACT.Exp, bias=nmx[:, u:u + 1],
                                         scale=HD ** -0.5, accum_out=sums[:, u:u + 1])
                exp.then_inc(exp_ready, 1)

            for s in range(UNITS):
                if s % 2 == 0:
                    split_hi(act, ATT0 + s // 2 + 1, s // 2 + 1, DT if s < UNITS - 2 else MK)
                if s == 0:
                    for n in range(4):
                        act.wait_ge(ty_done, n + 1)
                        for half in (0, 1):
                            o, i_ = turned_y(yh, n, half)
                            act.activation(o, i_, ACT.Copy).then_inc(yh_ready, 1)
                if s % QT == 3 and s > QT:
                    attn_hi(act, s // QT - 1)
                act_slot(s)

            def merge_act(m, first=False, last=False):
                c = MRG0 + 4 * m
                if first:
                    act_slot(UNITS)
                split_hi(act, c + 1, 1, MK)
                if not first:
                    merge_act_end(m - 1)
                split_hi(act, c + 2, 2, MK)
                if first:
                    act.wait_ge(ga_out, DT)
                else:
                    act.wait_ge(au_out, m)
                act.activation(sg[:, 0, :], ga[:, m, :], ACT.Sigmoid).then_inc(sga_ready, 1)
                if first:
                    attn_hi(act, AT - 1)
                split_hi(act, c + 3, 3, MK)
                act.wait_ge(gs_out, m + 1)
                act.activation(sg[:, 1, :], gs[:, 1, :], ACT.Sigmoid).then_inc(sgs_ready, 1)
                split_hi(act, c + 4, 4, DT if last else MK)

            def merge_act_end(m):
                act.wait_ge(chunk_done, MRG0 + 4 * m + 4)
                act.activation(us[:], bank[3][:], ACT.Sigmoid).then_inc(sgy_ready, 1)
                act.wait_ge(mg_ready, m + 1)
                act.activation(mh[:, m, :], hid[:, 1, :], ACT.Copy).then_inc(mh_ready, 1)

            merge_act(0, first=True)
            with act.Fori(1, DT - 1) as m:
                merge_act(m)
            merge_act(DT - 1, last=True)
            for m in range(DT):
                split_hi(act, OUT0 + m + 1, m + 1, DT)
                if m == 0:
                    merge_act_end(DT - 1)
                else:
                    norm_act(act, 2, m - 1)
            gu_act_first2(act)
            gu_act(act, 1, 1, 1, 2)
            gu_loop(act, 1, gu_act, 2, FT)
            down_act(act, 1)
            norm_act(act, 3, DT - 1)
            stat_act(act, 3)

        @block.vector
        def _(dve):
            V = Count(cd)

            def link(ins):
                V.link(dve, ins)

            dve.memset(ones[:], 1.0)
            dve.memset(eps[:], EPS).then_inc(set_up, 1)

            def reduce_angle(r, n_, x_in_, consts):
                link(dve.tensor_scalar(n_, x_in_, 1.0 / (2 * PI), MAGIC, ALU.mult, ALU.add))
                link(dve.tensor_scalar(n_, n_, MAGIC, None, ALU.subtract))
                src = x_in_
                for c_ in consts:
                    link(dve.scalar_tensor_tensor(r, n_, -c_, src, ALU.mult, ALU.add))
                    src = r
                link(dve.tensor_scalar(r, r, PI, -PI, ALU.min, ALU.max))

            sm = [small[:, j, :] for j in range(24)]
            lre, lim, _, dt, lr, an, r0, p8, p64, nn = sm[:10]
            tt, ts = dve.tensor_tensor, dve.tensor_scalar
            dve.wait_ge(prep_act, 1)
            link(tt(lr, lre, dt, ALU.mult))
            link(tt(an, lim, dt, ALU.mult))
            reduce_angle(r0, nn, an, TWO_PI)
            link(ts(an, r0, 8.0, None, ALU.mult))
            reduce_angle(p8, nn, an, TWO_PI)
            link(ts(an, p8, 8.0, None, ALU.mult))
            reduce_angle(p64, nn, an, TWO_PI)
            dve.wait_ge(c_in, 16 * 4)

            for i in range(DT):
                norm_dve(dve, 0, i)
                if i == 1:
                    split_lo(dve, 0, 0, DT)
            gu_dve(dve, 0, 0, 0, 0, first=True, norm=0)

            def angles(k0, k1, base):
                k = mult[:, k0:k1].unsqueeze(1).to_broadcast([P, G, k1 - k0])
                return tt(ang[:, :, k0:k1], base.unsqueeze(2).to_broadcast([P, G, k1 - k0]), k, ALU.mult)

            angles(0, NA, r0)
            angles(NA, NA + NB, p8)
            tt(expo[:, :, :], lr.unsqueeze(2).to_broadcast([P, G, NA]),
               mult[:, 0:NA].unsqueeze(1).to_broadcast([P, G, NA]), ALU.mult)
            ts(sm[22], lr, 8.0, None, ALU.mult)
            link(angles(NA + NB, NK, p64))
            ang_v = ang[:, :, :].rearrange("p g k -> p (g k)")
            reduce_angle(ang_v, tn[:], ang_v, TWO_PI[:2])
            link(ts(tn[:], ang_v, PI / 2, -2 * PI, ALU.is_gt, ALU.mult))
            link(dve.scalar_tensor_tensor(tn[:], ang_v, PI / 2, tn[:], ALU.add, ALU.add))
            dve.tensor_scalar(tn[:], tn[:], PI, -PI, ALU.min, ALU.max).then_inc(prep_dve, 1)
            den, t1, t2, fr, fi, num = sm[10:16]
            link(tt(den, lre, lre, ALU.mult))
            link(tt(t1, lim, lim, ALU.mult))
            link(tt(den, den, t1, ALU.add))
            link(dve.reciprocal(den, den))
            gu_dve(dve, 0, 1, 1, 2)
            dve.wait_ge(prep_act, 3)
            link(tt(er[:, :, :], mag[:, :, :], cs[:, :, 0:NA], ALU.mult))
            link(tt(ei[:, :, :], mag[:, :, :], sn[:, :, 0:NA], ALU.mult))
            ar1, ai1 = er[:, :, 1], ei[:, :, 1]
            link(ts(num, ar1, 1.0, None, ALU.subtract))
            link(tt(fr, num, lre, ALU.mult))
            link(tt(t1, ai1, lim, ALU.mult))
            link(tt(fr, fr, t1, ALU.add))
            link(tt(fr, fr, den, ALU.mult))
            link(tt(fi, ai1, lre, ALU.mult))
            link(tt(t2, num, lim, ALU.mult))
            link(tt(fi, fi, t2, ALU.subtract))
            link(tt(fi, fi, den, ALU.mult))
            link(ts(bS[:, :, :], bS[:, :, :], signs[:, 0:1], None, ALU.mult))
            link(ts(cO[:, :, :], cO[:, :, :], signs[:, 1:2], None, ALU.mult))
            link(ts(cA[:, :, :], cR[:, :, :], -1.0, None, ALU.mult))
            frb = fr.unsqueeze(2).to_broadcast([P, G, GH])
            fib = fi.unsqueeze(2).to_broadcast([P, G, GH])
            link(tt(bb[:, :, :], frb, bO[:, :, :], ALU.mult))
            link(tt(tmpB[:, :, :], fib, bS[:, :, :], ALU.mult))
            link(tt(bb[:, :, :], bb[:, :, :], tmpB[:, :, :], ALU.add))
            link(tt(bbS[:, :, :], frb, bS[:, :, :], ALU.mult))
            link(tt(tmpB[:, :, :], fib, bO[:, :, :], ALU.mult))
            tt(bbS[:, :, :], bbS[:, :, :], tmpB[:, :, :], ALU.subtract).then_inc(prep_dve, 1)
            gu_loop(dve, 0, gu_dve, 2, 4)
            gu_loop(dve, 0, gu_dve, 4, 14)
            for n in range(8):
                dve.wait_ge(kt_done, n + 1)
                if n == 0:
                    dve.wait_ge(stored, 16 * 4)
                dve.tensor_copy(ktS[:, 4 * n:4 * n + 4, :, :].rearrange("p g k h -> p (g k h)"),
                                win_bank(4 * n)[0:GH, :]).then_inc(kt_out, 1)
            dve.wait_ge(stored, 16 * 5)
            gu_loop(dve, 0, gu_dve, 14, FT)
            down_dve(dve, 0)

            flat = "p g c -> p (g c)"
            zg_v, zx_v, cos_v = (t[:, :, :].rearrange(flat) for t in (zg, zx, cosT))
            for i in range(4 * AT):
                split_lo(dve, PRJ0 + i + 1, i + 1, DT)
                if i == 0:
                    x_dve(dve, PRJ0, bank[5], DT - 1, 0.5)
                    norm_dve(dve, 1, DT - 1)
                    stat_dve(dve, 1)
                else:
                    prj_dve(dve, i - 1)
                if i in (5, 6):
                    for n in range(4 * (i - 5) + 1, 4 * (i - 4), 2):
                        dve.wait_ge(tu_done, n + 1)
                        turned_u(dve.tensor_copy, n).then_inc(u_dve, 1)
                if i == 7:
                    for n in (1, 3):
                        dve.wait_ge(tc_done, n + 1)
                        dve.tensor_copy(uc[:, 8 * n:8 * n + 8, :].rearrange(flat), bank[2 + n][:]).then_inc(uc_dve, 1)
                if i == 8:
                    dve.wait_ge(z_done, 4)
                    dve.wait_ge(tab_in[1], 16)
                    for n in range(4):
                        dve.wait_ge(zx_ready, n + 1)
                        cols = slice(n * S, (n + 1) * S)
                        ins = tt(zg_v[:, cols], bank[2 + n][:], cos_v[:, cols], ALU.mult)
                    link(ins)
                if i == 10:
                    dve.wait_ge(zx_sin, 1)
                    link(tt(zg_v, zg_v, zx_v, ALU.add))
                if i in (10, 11):
                    for g in range(16 * (i - 10), 16 * (i - 9)):
                        dve.tensor_tensor_scan(zx[:, g, :], mag8[:, g:g + 1].to_broadcast([P, C]), zg[:, g, :],
                                               0.0, ALU.mult, ALU.add).then_inc(scan_ready, 1)
                if i == 13:
                    dve.wait_ge(scan_ready, G)
                    dve.memset(hs[:, :, 0:1], 0.0)
                    link(tt(hs[:, :, 1:C], zx[:, :, 0:C - 1], cosT[:, :, 0:C - 1], ALU.mult))
                if i == 14:
                    dve.wait_ge(gx_sin, 1)
                    tt(hs[:, :, 1:C], hs[:, :, 1:C], zg[:, :, 0:C - 1], ALU.add).then_inc(hs_ready, 1)
            prj_dve(dve, 4 * AT - 1)
            for kb in range(QT):
                dve.wait_ge(tv_done, kb + 1)
                if kb == 0:
                    dve.wait_ge(hs_ready, 1)
                dve.tensor_copy(v_[:, kb, :], bank[(0, 1, 6, 7)[kb]][:]).then_inc(v_out, 1)

            def dve_slot(s):
                if s < UNITS:
                    i, qt = s // QT, s % QT
                    w, o = (qt + 1) * P, (QT - 1 - qt) * P
                    dve.wait_ge(sc_done, s + 1)
                    dve.wait_ge(bias_ready, 2 * (i + 1))
                    if s:
                        dve.wait_ge(exp_ready, s)
                    for head in (0, 1):
                        ttr = dve.tensor_tensor_reduce(sc[:, head, 0:w], bank[2 + head][:, 0:w],
                                                       bias[:, (2 * i + head) % 4, o:o + w], 1.0, -3.0e38,
                                                       ALU.add, ALU.max, mx[:, 2 * s + head:2 * s + head + 1])
                    link(ttr)
                    dve.tensor_scalar(nmx[:, 2 * s:2 * s + 2], mx[:, 2 * s:2 * s + 2], -(HD ** -0.5), None,
                                      ALU.mult).then_inc(nmx_ready, 1)
                if s % QT == 1 and s > QT:
                    attn_norm(dve, link, s // QT - 1)
                if s >= 1:
                    pt_evac(dve, dve.tensor_copy, s - 1, 1)

            def ga_dve(m):
                dve.wait_ge(chunk_done, ATT0 + m + 1)
                tt(ga[:, m, :], bank[m % 2][:], rstd[:], ALU.mult).then_inc(ga_out, 1)

            for s in range(UNITS):
                dve_slot(s)
                if s % 2 == 0:
                    split_lo(dve, ATT0 + s // 2 + 1, s // 2 + 1, DT if s < UNITS - 2 else MK)
                    if s:
                        ga_dve(s // 2 - 1)
                if s == 0:
                    for n in range(4):
                        dve.wait_ge(yh_ready, 2 * n + 2)
                        for half in (0, 1):
                            o, i_ = turned_y(yl, n, half)
                            oh, _ = turned_y(yh, n, half)
                            tt(o, i_, oh.bitcast(F32), ALU.subtract).then_inc(yl_ready, 1)
                if s % QT == 3 and s > QT:
                    attn_lo(dve, s // QT - 1)

            def merge_dve(m, first=False, last=False):
                c = MRG0 + 4 * m
                if first:
                    ga_dve(DT - 1)
                    dve_slot(UNITS)
                split_lo(dve, c + 1, 1, MK)
                if first:
                    attn_norm(dve, link, AT - 1)
                else:
                    merge_dve_end(m - 1)
                split_lo(dve, c + 2, 2, MK)
                dve.wait_ge(chunk_done, c + 2)
                tt(gs[:, 1, :], bank[0][:], rstd[:], ALU.mult).then_inc(gs_out, 1)
                if first:
                    attn_lo(dve, AT - 1)
                split_lo(dve, c + 3, 3, MK)
                dve.wait_ge(chunk_done, c + 3)
                dve.wait_ge(sga_ready, m + 1)
                tt(hid[:, 0, :], bank[1][:], sg[:, 0, :], ALU.mult).then_inc(au_out, 1)
                split_lo(dve, c + 4, 4, DT if last else MK)

            def merge_dve_end(m):
                dve.wait_ge(chunk_done, MRG0 + 4 * m + 4)
                dve.wait_ge(sgs_ready, m + 1)
                tt(acc[:], bank[2][:], sg[:, 1, :], ALU.mult).then_inc(yv_out, 1)
                dve.wait_ge(yv_out, m + 1)
                dve.wait_ge(sgy_ready, m + 1)
                tt(acc[:], acc[:], us[:], ALU.mult).then_inc(me, 1)
                dve.wait_ge(me, m + 1)
                dve.wait_ge(au_out, m + 1)
                tt(hid[:, 1, :], hid[:, 0, :], acc[:], ALU.add).then_inc(mg_ready, 1)
                dve.wait_ge(mh_ready, m + 1)
                tt(ml[:, m, :], hid[:, 1, :], mh[:, m, :].bitcast(F32), ALU.subtract).then_inc(ml_ready, 1)

            merge_dve(0, first=True)
            with dve.Fori(1, DT - 1) as m:
                merge_dve(m)
            merge_dve(DT - 1, last=True)
            for m in range(DT):
                split_lo(dve, OUT0 + m + 1, m + 1, DT)
                if m == 0:
                    merge_dve_end(DT - 1)
                else:
                    x_dve(dve, OUT0 + m, bank[5 + (m - 1) % 2], m - 1, 1.0)
                    norm_dve(dve, 2, m - 1)
            c = UP0[1]
            split_lo(dve, c + 1, 1, DT)
            x_dve(dve, c, bank[6], DT - 1, 1.0)
            norm_dve(dve, 2, DT - 1)
            stat_dve(dve, 2)
            split_lo(dve, c + 2, 2, DT)
            gu_gate_dve(dve, 1, 0, 0)
            gu_dve(dve, 1, 1, 1, 2)
            gu_loop(dve, 1, gu_dve, 2, FT)
            down_dve(dve, 1)
            x_dve(dve, CHUNKS, bank[5], DT - 1, 0.5)
            norm_dve(dve, 3, DT - 1)
            stat_dve(dve, 3)
            for i in range(5):
                dve.wait_ge(xg_ready, i + 1)
                tt(xg[:, i, :], xg[:, i, :], rstd[:], ALU.mult).then_inc(fin_dve, 1)

        @block.gpsimd
        def _(pool):
            K = Count(cp)

            def link(ins):
                K.link(pool, ins)

            for dst, src in ((ident[:], ident_in), (gain[:], gains), (mult[:], multiples_in), (signs[:], signs_in)):
                pool.dma_start(dst, src).then_inc(c_in, 16)
            for dst, src in ((small[:, 2, :], log_dt), (small[:, 0, :], lam_re), (small[:, 1, :], lam_im),
                             (bO[:], b_own), (bS[:], b_swap), (cO[:], c_own), (cR[:], c_swap)):
                pool.dma_start(dst, src).then_inc(s_in, 16)
            tt = pool.tensor_tensor

            def over_h(t, k0, k1):
                return t[:, :, k0:k1].unsqueeze(3).to_broadcast([P, G, k1 - k0, GH])

            def over_k(t, k):
                return t[:, :, :].unsqueeze(2).to_broadcast([P, G, k, GH])

            pool.wait_ge(prep_dve, 2)
            link(tt(winT[:], over_h(er, 0, T), over_k(bb, T), ALU.mult))
            link(tt(tmpW[:], over_h(ei, 0, T), over_k(bbS, T), ALU.mult))
            tt(winT[:], winT[:], tmpW[:], ALU.add).then_inc(winT_ready, 1)
            pool.wait_ge(win_out, 8)
            pool.dma_start(win_d, winS[:].rearrange("p g c -> p (g c)")).then_inc(stored, 16)
            link(tt(ce_w[:], over_h(er, 0, NA), over_k(cO, NA), ALU.mult))
            pool.wait_ge(stored, 16)
            link(tt(tmpC[:], over_h(ei, 0, NA), over_k(cA, NA), ALU.mult))
            tt(ce_w[:], ce_w[:], tmpC[:], ALU.add).then_inc(ce_ready, 1)
            pool.wait_ge(ce_ready, 1)
            pool.dma_start(ce_d, ce_w[:].rearrange("p g k h -> p (g k h)")).then_inc(stored, 16)
            for q in range(4):
                gg = slice(8 * q, 8 * q + 8)

                def outer(a, b):
                    return (a[:, gg, NA + NB:NK].unsqueeze(3).to_broadcast([P, 8, NB, NB]),
                            b[:, gg, NA:NA + NB].unsqueeze(2).to_broadcast([P, 8, NB, NB]))

                link(tt(cosS[:, gg], *outer(cs, cs), ALU.mult))
                link(tt(tmpR[:], *outer(sn, sn), ALU.mult))
                link(tt(cosS[:, gg], cosS[:, gg], tmpR[:], ALU.subtract))
                link(tt(sinS[:, gg], *outer(sn, cs), ALU.mult))
                link(tt(tmpR[:], *outer(cs, sn), ALU.mult))
                link(tt(sinS[:, gg], sinS[:, gg], tmpR[:], ALU.add))
            pool.dma_start(cos_d, cosS[:].rearrange("p g a b -> p (g a b)")).then_inc(stored, 16)
            pool.dma_start(sin_d, sinS[:].rearrange("p g a b -> p (g a b)")).then_inc(stored, 16)
            pool.wait_ge(kt_out, 8)
            pool.dma_start(dB[:].rearrange("p g h -> p (g h)"), ssm_d.partition_broadcast(GH)).then_inc(d_in, 16)
            pool.wait_ge(d_in, 16)
            link(tt(dB[:], dB[:], ident[0:GH, 0:GH].unsqueeze(1).to_broadcast([GH, G, GH]), ALU.mult))
            link(tt(ktS[:, :, 0, :], ktS[:, :, 0, :], dB[:], ALU.add))
            pool.dma_start(kt_d, ktS[:].rearrange("p g k h -> p (g k h)")).then_inc(stored, 16)

            pool.wait_ge(stored, 16 * 5)
            pool.wait_ge(chunk_done, PRJ0)
            pool.dma_start(dist, dist_in).then_inc(dist_in_s, 16)
            pool.dma_start(win[:].rearrange("p g c -> p (g c)"), win_d).then_inc(tab_in[0], 16)
            pool.dma_start(cosT[:].rearrange("p g c -> p (g c)"), cos_d).then_inc(tab_in[1], 16)
            pool.dma_start(sinT[:].rearrange("p g c -> p (g c)"), sin_d).then_inc(tab_in[2], 16)
            pool.dma_start(ce[:].rearrange("p g k h -> p (g k h)"), ce_d).then_inc(tab_in[3], 16)
            pool.wait_ge(tc_done, 4)
            link(pool.memset(toep[:], 0.0))
            kt_v = kt_d.rearrange("h (g n) -> h g n", g=G)
            for r in range(T):
                n = GH * (r + 1)
                pool.dma_start(toep[GH * r:GH * (r + 1), :, P - n:P], kt_v[:, :, 0:n]).then_inc(toep_in, 16)
            pool.wait_ge(zx_ready, 4)
            pool.wait_ge(tab_in[2], 16)
            tt(zx[:], zx[:], sinT[:], ALU.mult).then_inc(zx_sin, 1)
            pool.wait_ge(gx_ready, 1)
            tt(zg[:], zg[:], sinT[:], ALU.mult).then_inc(gx_sin, 1)
            pool.wait_ge(dist_in_s, 16)
            for h in range(H):
                if h == 0:
                    pool.wait_ge(hs_ready, 1)
                elif h >= 4 and h % 2 == 0:
                    pool.wait_ge(nmx_ready, QT * (h - 2) // 2)
                slope = 2.0 ** (-8.0 * (h + 1) / H)
                pool.tensor_scalar(bias[:, h % 4, :], dist, -slope * HD ** 0.5, None,
                                   ALU.mult).then_inc(bias_ready, 1)
            pool.wait_ge(rstd_ready, 4)
            for i in range(5, DT):
                pool.wait_ge(xg_ready, i + 1)
                tt(xg[:, i, :], xg[:, i, :], rstd[:], ALU.mult).then_inc(fin_pool, 1)


def kernel(**inputs):
    import numpy as np
    import concourse.bacc as bacc
    from concourse.bass_utils import run_bass_kernel_spmd

    a = {k: np.asarray(v) for k, v in inputs.items()}

    def tiles(w):
        k, m = w.shape
        return w.reshape(k // P, P, m // P, P).transpose(2, 1, 0, 3).reshape(m // P, P, k)

    def column(v):
        return v.reshape(-1, P).T

    def states(re, im):
        return np.concatenate([np.moveaxis(re, 1, 0), np.moveaxis(im, 1, 0)])

    ffns = ("ffn1", "ffn2")
    w_in = tiles(a["w_in"][0])
    glu = tiles(a["w_ssm_glu"][0])
    q, k, v, u = (w_in[AT * i:AT * (i + 1)] for i in range(4))
    br, bi = a["ssm_b_re"][0], a["ssm_b_im"][0]
    cr, ci = (a[n][0].transpose(0, 2, 1) for n in ("ssm_c_re", "ssm_c_im"))
    lre, lim = a["ssm_lambda_re"][0], a["ssm_lambda_im"][0]
    multiples = np.concatenate([np.arange(NA), np.arange(NB), np.arange(NB)]).astype(np.float32)
    signs = np.ones((P, 2), np.float32)
    signs[:NS, 0] = signs[NS:, 1] = -1
    rows, cols = np.arange(P)[:, None], np.arange(S)[None, :]
    dist = (rows + S - P - cols).astype(np.float32)
    dist[dist < 0] = 1e30
    arrays = {
        "x": a["x"][0].reshape(S, DT, P).transpose(2, 1, 0),
        "gains": np.stack([column(a[n].reshape(-1)) for n in ("ffn1_norm", "mix_norm", "ffn2_norm", "final_norm")], 1),
        "w_up": np.stack([np.stack([tiles(a[f"{f}_w_{n}"][0]) for n in ("gate", "up")], 1) for f in ffns]),
        "w_down": np.stack([tiles(a[f"{f}_w_down"][0]) for f in ffns]),
        "w_proj": np.concatenate([u, k, q, v]),
        "w_gate": w_in[4 * AT:4 * AT + DT],
        "w_merge": np.concatenate([w_in[4 * AT + DT:], tiles(a["w_attn_up"][0]),
                                   glu[:DT], glu[DT:]], 2),
        "w_out": tiles(a["w_out"][0]),
        "lam_re": states(lre, lre), "lam_im": states(lim, lim),
        "log_dt": np.broadcast_to(a["ssm_log_dt"], (P, G)),
        "b_own": states(br, bi), "b_swap": states(bi, br), "c_own": states(cr, ci), "c_swap": states(ci, cr),
        "ssm_d": a["ssm_d"][0],
        "ident": np.eye(P, dtype=np.float32), "multiples": np.broadcast_to(multiples, (P, NK)),
        "signs": signs, "dist": dist,
    }
    arrays = {n: np.ascontiguousarray(v) for n, v in arrays.items()}
    nc = bacc.Bacc("TRN2", target_bir_lowering=False, num_devices=1)
    args = [nc.dram_tensor(n, v.shape, mybir.dt.float32, kind="ExternalInput").ap() for n, v in arrays.items()]
    out = nc.dram_tensor("out", (P, DT, S), mybir.dt.float32, kind="ExternalOutput").ap()
    hybrid(nc, *args, out)
    r = run_bass_kernel_spmd(nc, [arrays], core_ids=[0])
    y = r.results[0]["out"]
    return y.reshape(P, DT, S).transpose(2, 1, 0).reshape(1, S, D)
```

```python
from contextlib import ExitStack

import concourse.bass as bass
from concourse import mybir

ALU = mybir.AluOpType
ACT = mybir.ActivationFunctionType
F32 = mybir.dt.float32
F32R = mybir.dt.float32r

P = 128
D, S, F = 1024, 512, 2816
DT, FT = D // P, F // P
H, HD = 8, 64
AW = H * HD
AT = AW // P
G, GH, NS = 32, 16, 64
T = 8
C = S // T
QT = S // P
EPS = 1e-6

DOWN_PARTS = ((0, 8), (8, 15), (15, 22))
UP0 = (0, 132)
DN0 = (44, 176)
PRJ0, ATT0, MRG0, OUT0, CHUNKS = 68, 84, 92, 124, 200
MK = 5
RAW = 4
HL = 2
MID = D // 2

NA, NB = T + 1, 8
NK = NA + 2 * NB
FIN_DVE = 5
WARM = 11
X_AGAIN = 18
PI = 3.141592653589793
MAGIC = 12582912.0
TWO_PI = (6.28125, 0.0019340515136718750, 1.2556659146e-06)

BASE = 16512
X_AT = BASE
AH_AT = X_AT + DT * S * 4
RAW_AT = AH_AT + 2 * DT * S * 4
HL_AT = RAW_AT + RAW * D * 4
HID_AT = HL_AT + 2 * HL * D * 4
SPARE_AT = HID_AT + 2 * FT * S * 4
SPARE = 18432
WORK_AT = SPARE_AT + SPARE


def hybrid(nc, x, gains, w_up, w_down, w_proj, w_gate, w_merge, w_out, lam_re, lam_im, log_dt, b_own,
           b_swap, c_own, c_swap, ssm_d, ident_in, multiples_in, signs_in, dist_in, out):
    with ExitStack() as ctx:
        at = [WORK_AT]

        def place(name, shape, offset, dt=F32):
            return nc.alloc_sbuf_tensor_at(name, shape, dt, offset=offset)

        def work(name, shape, dt=F32):
            n = 4
            for s in shape[1:]:
                n *= s
            n = -(-n // 32) * 32
            at[0] += n
            assert at[0] <= 229344, at[0]
            return place(name, shape, at[0] - n, dt)

        def sem(name):
            return ctx.enter_context(nc.semaphore(name))

        xT = place("xT", [P, DT, S], X_AT)
        ah = place("ah", [P, DT, S], AH_AT, F32R)
        al = place("al", [P, DT, S], AH_AT + DT * S * 4, F32R)
        xg = place("xg", [P, DT, S], AH_AT)
        raw = place("raw", [P, RAW, D], RAW_AT)
        wh = place("wh", [P, HL, D], HL_AT, F32R)
        wl = place("wl", [P, HL, D], HL_AT + HL * D * 4, F32R)
        eh = place("eh", [P, 2, D], AH_AT + DT * S * 4, F32R)
        el = place("el", [P, 2, D], AH_AT + DT * S * 4 + 2 * D * 4, F32R)
        gs = work("gs", [P, 2, S])
        sg = work("sg", [P, 2, S])
        us = work("us", [P, S])
        hid = work("hid", [P, 2, S])
        rstd = work("rstd", [P, S])
        acc = work("acc", [P, S])
        sq = work("sq", [P, S])
        ident = work("ident", [P, P])
        ones = work("ones", [P, P])
        gain = work("gain", [P, 4, DT])
        eps = work("eps", [P, 1])
        signs = work("signs", [P, 2])
        mx = work("mx", [P, QT * H])
        nmx = work("nmx", [P, QT * H])
        sums = work("sums", [P, QT * H])
        rec = work("rec", [P, QT * H])
        root = work("root", [P, 2, QT])
        mag8 = work("mag8", [P, G])

        hp = place("hp", [P, FT, 2, S], HID_AT, F32R)

        PX = HID_AT + 13 * 2 * S * 4
        PY = PX + G * NA * GH * 4
        winT = place("winT", [P, G, T, GH], PX)
        tmpW = place("tmpW", [P, G, T, GH], PY)
        winS = place("winS", [P, G, P], X_AT)
        ce_w = place("ce_w", [P, G, NA, GH], PY)
        tmpC = place("tmpC", [P, 8, NA, GH], PX - 8192)
        cosS = place("cosS", [P, G, NB, NB], PX)
        sinS = place("sinS", [P, G, NB, NB], PX + 8192)
        tmpR = place("tmpR", [P, 8, NB, NB], PX + 16384)
        ktS = place("ktS", [GH, G, NB, GH], X_AT)
        ang = place("ang", [P, G, NK], PX)
        tn = place("tn", [P, G * NK], PX + 4 * G * NK)
        mag = place("mag", [P, G, NA], PX + 8 * G * NK)
        expo = place("expo", [P, G, NA], PX + 8 * G * NK + 4 * G * NA)
        mult = place("mult", [P, NK], PX + 8 * G * NK + 8 * G * NA)
        bO = place("bO", [P, G, GH], PY)
        bS = place("bS", [P, G, GH], PY + 2048)
        cR = place("cR", [P, G, GH], PY + 4096)
        tmpB = place("tmpB", [P, G, GH], PY + 6144)
        small = place("small", [P, 24, G], PY + 8192)
        sn = place("sn", [P, G, NK], SPARE_AT)
        cs = place("cs", [P, G, NK], SPARE_AT + 4 * G * NK)
        s2 = SPARE_AT + 8 * G * NK
        er = place("er", [P, G, NA], s2)
        ei = place("ei", [P, G, NA], s2 + 4 * G * NA)
        s3 = s2 + 8 * G * NA
        bb = place("bb", [P, G, GH], s3)
        bbS = place("bbS", [P, G, GH], s3 + 2048)
        dB = place("dB", [GH, G, GH], s3 + 2048)
        cO = place("cO", [P, G, GH], s3 + 4096)
        cA = place("cA", [P, G, GH], s3 + 6144)

        R = HID_AT
        prj = place("prj", [P, 4 * AT, S], R)
        uc = place("uc", [P, G, C], R)
        win = place("win", [P, G, P], R + 32768)
        zg = place("zg", [P, G, C], R + 32768)
        zx = place("zx", [P, G, C], R + 40960)
        y_ = place("y_", [P, 2, T, P], R + 32768)
        ce = place("ce", [P, G, NA, GH], R + 49152)
        yh = place("yh", [P, AT, S], R + 49152, F32R)
        yl = place("yl", [P, AT, S], R + 57344, F32R)
        u_ = place("u_", [C, G, T, GH], R + 67584)
        toep = place("toep", [P, G, P], R + 67584)
        cosT = place("cosT", [P, G, C], R + 83968)
        sinT = place("sinT", [P, G, C], R + 92160)
        hs = place("hs", [P, G, C], R + 100352)
        bias = place("bias", [P, 4, S], R + 40960)
        v_ = place("v_", [P, QT, AW], R + 83968)
        ga = place("ga", [P, DT, S], R + 67584)
        sc = place("sc", [P, 2, S], R + 92160)
        pr = place("pr", [P, 4, S], R + 96256)
        pts = place("pts", [P, 2, S], R + 104448)
        th = place("th", [P, AT, S], R, F32R)
        tl = place("tl", [P, AT, S], R + 24576, F32R)
        mh = place("mh", [P, DT, S], R + 8192, F32R)
        ml = place("ml", [P, DT, S], R + 67584, F32R)

        dist = hid[:, 0, :]

        def scratch(name, shape):
            return nc.dram_tensor(name, shape, F32, kind="Internal").ap()

        win_d = scratch("win_d", [P, G * P])
        ce_d = scratch("ce_d", [P, G * NA * GH])
        cos_d = scratch("cos_d", [P, G * C])
        sin_d = scratch("sin_d", [P, G * C])
        kt_d = scratch("kt_d", [GH, G * P])

        bank = [ctx.enter_context(nc.psum_tensor(f"bank{i}", [P, S], F32)) for i in range(8)]

        landed = [sem(f"landed{i}") for i in range(RAW)]
        hi_ready = sem("hi_ready")
        lo_ready = sem("lo_ready")
        chunk_done = sem("chunk_done")
        end_done = sem("end_done")
        x_in = [sem(f"x_in{i}") for i in range(4)]
        g_in = sem("g_in")
        s_in = sem("s_in")
        i_in = sem("i_in")
        c_in = sem("c_in")
        set_up = sem("set_up")
        x_new = sem("x_new")
        sq_ready, acc_ready = sem("sq_ready"), sem("acc_ready")
        ah_ready, al_ready = sem("ah_ready"), sem("al_ready")
        ss_ready, rt_ready, dg_ready = sem("ss_ready"), sem("rt_ready"), sem("dg_ready")
        bc_ready, rstd_ready = sem("bc_ready"), sem("rstd_ready")
        x_first = sem("x_first")
        w_first = [sem("w_first0"), sem("w_first1")]
        hi_first, lo_first = sem("hi_first"), sem("lo_first")
        gate_out, up_out = sem("gate_out"), sem("up_out")
        silu_ready, hid_ready = sem("silu_ready"), sem("hid_ready")
        hh_ready, hl_ready = sem("hh_ready"), sem("hl_ready")
        cd = sem("cd")
        ca = sem("ca")
        cp = sem("cp")
        prep_dve = sem("prep_dve")
        prep_act = sem("prep_act")
        winT_ready, winT_turned = sem("winT_ready"), sem("winT_turned")
        win_out = [sem("win_act"), sem("win_dve")]
        ce_ready, kt_done = sem("ce_ready"), sem("kt_done")
        kt_out = [sem("kt_act"), sem("kt_dve")]
        win_stored, kt_stored = sem("win_stored"), sem("kt_stored")
        stored = sem("stored")
        tab_in = [sem(f"tab_in{i}") for i in range(4)]
        toep_in = sem("toep_in")
        d_in = sem("d_in")
        dist_in_s = sem("dist_in_s")
        prj_out = sem("prj_out")
        tu_done, u_act, u_dve = sem("tu_done"), sem("u_act"), sem("u_dve")
        tc_done, uc_act, uc_dve = sem("tc_done"), sem("uc_act"), sem("uc_dve")
        z_done, zx_ready, zx_sin, zg_ready = sem("z_done"), sem("zx_ready"), sem("zx_sin"), sem("zg_ready")
        scan_ready, gx_ready, gx_sin, hs_ready = sem("scan_ready"), sem("gx_ready"), sem("gx_sin"), sem("hs_ready")
        y_done, gelu_ready = sem("y_done"), sem("gelu_ready")
        tv_done, v_out = sem("tv_done"), sem("v_out")
        ty_done, yh_ready, yl_ready = sem("ty_done"), sem("yh_ready"), sem("yl_ready")
        bias_ready = sem("bias_ready")
        sc_done, nmx_ready, exp_ready = sem("sc_done"), sem("nmx_ready"), sem("exp_ready")
        pt_done, pt_out, pv_done = sem("pt_done"), [sem("pt_out0"), sem("pt_out1")], sem("pv_done")
        pn_ready, th_ready, tl_ready = sem("pn_ready"), sem("th_ready"), sem("tl_ready")
        ga_out, gs_out, sga_ready, sgs_ready, sgy_ready = (sem("ga_out"), sem("gs_out"), sem("sga_ready"),
                                                           sem("sgs_ready"), sem("sgy_ready"))
        me = sem("me")
        yg_done = sem("yg_done")
        au_out, yv_out = sem("au_out"), sem("yv_out")
        mg_ready, mh_ready, ml_ready = sem("mg_ready"), sem("mh_ready"), sem("ml_ready")
        xg_ready, fin_dve, fin_pool, out_done = sem("xg_ready"), sem("fin_dve"), sem("fin_pool"), sem("out_done")

        class Count:

            def __init__(self, s):
                self.s, self.n = s, 0

            def step(self, ins):
                self.n += 1
                ins.then_inc(self.s, 1)

            def link(self, eng, ins):
                self.step(ins)
                eng.wait_ge(self.s, self.n)

        def split_hi(act, c, slot, kts, first=False):
            act.wait_ge(landed[slot % RAW], 16 * (c // RAW + 1) if isinstance(c, int) else (c - slot % RAW) * (16 // RAW) + 16)
            if not first:
                act.wait_ge(chunk_done, c - 1)
            act.activation(wh[:, slot % HL, 0:kts * P], raw[:, slot % RAW, 0:kts * P], ACT.Copy).then_inc(hi_ready, 1)

        def split_lo(dve, c, slot, kts):
            dve.wait_ge(hi_ready, c + 1)
            dve.tensor_tensor(wl[:, slot % HL, 0:kts * P], raw[:, slot % RAW, 0:kts * P],
                              wh[:, slot % HL, 0:kts * P].bitcast(F32), ALU.subtract).then_inc(lo_ready, 1)

        def first_hi(act, c, part):
            act.wait_ge(landed[c] if part else w_first[c], 16)
            act.activation(wh[:, c, MID * part:MID * (part + 1)], raw[:, c, MID * part:MID * (part + 1)],
                           ACT.Copy).then_inc(hi_ready if part else hi_first, 1)

        def first_lo(dve, c, part):
            cols = slice(MID * part, MID * (part + 1))
            dve.wait_ge(hi_ready if part else hi_first, c + 1)
            dve.tensor_tensor(wl[:, c, cols], raw[:, c, cols], wh[:, c, cols].bitcast(F32),
                              ALU.subtract).then_inc(lo_ready if part else lo_first, 1)

        def w_tile(slot, k):
            return wh[:, slot % HL, k * P:(k + 1) * P], wl[:, slot % HL, k * P:(k + 1) * P]

        def three(pe, ps, slot, k, r_hi, r_lo, first, last):
            w_hi, w_lo = w_tile(slot, k)
            pe.matmul(ps, w_hi, r_hi, start=first, stop=False)
            pe.matmul(ps, w_hi, r_lo, start=False, stop=False)
            return pe.matmul(ps, w_lo, r_hi, start=False, stop=last)

        def scale_act(act, n, i):
            act.activation(ah[:, i, :], xT[:, i, :], ACT.Copy, scale=gain[:, n, i:i + 1]).then_inc(ah_ready, 1)

        def square_of(n, i):
            return us if n == 0 and i % 2 == 0 else sq

        def square_act(act, n, i):
            if n:
                act.wait_ge(acc_ready, DT * n + i)
            elif i > 1:
                act.wait_ge(acc_ready, i - 1)
            act.activation(square_of(n, i)[:], xT[:, i, :], ACT.Square).then_inc(sq_ready, 1)

        def norm_act(act, n, i):
            act.wait_ge(x_new, 8 * (n - 1) + i + 1)
            if n < 3:
                scale_act(act, n, i)
            square_act(act, n, i)
            if n == 3:
                act.activation(xg[:, i, :], xT[:, i, :], ACT.Copy, scale=gain[:, n, i:i + 1]).then_inc(xg_ready, 1)

        def scale_dve(dve, n, i):
            dve.wait_ge(ah_ready, 8 * n + i + 1)
            dve.scalar_tensor_tensor(al[:, i, :], xT[:, i, :], gain[:, n, i:i + 1], ah[:, i, :].bitcast(F32),
                                     ALU.mult, ALU.subtract).then_inc(al_ready, 1)

        def square_dve(dve, n, i):
            dve.wait_ge(sq_ready, DT * n + i + 1)
            if i == 0:
                if n > 0:
                    dve.wait_ge(ss_ready, n)
                dve.tensor_copy(acc[:], square_of(n, i)[:]).then_inc(acc_ready, 1)
            else:
                dve.wait_ge(acc_ready, DT * n + i)
                dve.tensor_tensor(acc[:], acc[:], square_of(n, i)[:], ALU.add).then_inc(acc_ready, 1)

        def norm_dve(dve, n, i):
            if n < 3:
                scale_dve(dve, n, i)
            square_dve(dve, n, i)

        def stat_pe(pe, n):
            pe.wait_ge(acc_ready, DT * (n + 1))
            if n > 0:
                pe.wait_ge(rstd_ready, n)
            for t in range(QT):
                mm = pe.matmul(bank[7][:, t:t + 1], acc[:, t * P:(t + 1) * P], ones[:, 0:1], start=True, stop=True)
            mm.then_inc(ss_ready, 1)

        def stat_act(act, n):
            act.wait_ge(ss_ready, n + 1)
            act.activation(root[:, 0, :], bank[7][:, 0:QT], ACT.Sqrt, scale=1.0 / D, bias=eps[:, 0:1]).then_inc(rt_ready, 1)

        def stat_dve(dve, link, n):
            dve.wait_ge(rt_ready, n + 1)
            if n == 0:
                dve.wait_ge(i_in, 16)
            link(dve.reciprocal(root[:, 1, :], root[:, 0, :]))
            dve.tensor_tensor(us[:].rearrange("p (t q) -> p t q", t=QT), ident[:].unsqueeze(1).to_broadcast([P, QT, P]),
                              root[:, 1, :].unsqueeze(2).to_broadcast([P, QT, P]), ALU.mult).then_inc(dg_ready, 1)

        def spread_pe(pe, n):
            pe.wait_ge(dg_ready, n + 1)
            pe.matmul(bank[7][:], ones[:], us[:], start=True, stop=True).then_inc(bc_ready, 1)

        def rstd_dve(dve, n):
            dve.wait_ge(bc_ready, n + 1)
            dve.tensor_copy(rstd[:], bank[7][:]).then_inc(rstd_ready, 1)
            dve.wait_ge(rstd_ready, n + 1)

        def gu_pe(pe, n, f, b, known=True, norm=None):
            c0, g0 = UP0[n], FT * n
            for part in (0, 1):
                pe.wait_ge(lo_ready, c0 + 2 * f + part + 1)
                if known:
                    pe.wait_ge(up_out if part else gate_out, g0 + f - 1)
                for k in range(DT):
                    if norm is not None and part == 0:
                        pe.wait_ge(al_ready, 8 * norm + k + 1)
                    mm = three(pe, bank[2 * part + b][:], part, k, ah[:, k, :], al[:, k, :], k == 0, k == DT - 1)
                    if norm is not None and part == 1 and k == DT // 2:
                        spread_pe(pe, norm)
                mm.then_inc(chunk_done, 1)
                if norm is not None and part == 0:
                    stat_pe(pe, norm)

        def gu_up_dve(dve, n, f, b):
            c0, g0 = UP0[n], FT * n
            dve.wait_ge(chunk_done, c0 + 2 * f + 2)
            dve.tensor_tensor(us[:], bank[2 + b][:], rstd[:], ALU.mult).then_inc(up_out, 1)
            dve.wait_ge(up_out, g0 + f + 1)
            dve.wait_ge(silu_ready, g0 + f + 1)
            dve.tensor_tensor(hid[:, b, :], sg[:, b, :], us[:], ALU.mult).then_inc(hid_ready, 1)

        def gu_low_dve(dve, n, f, b):
            dve.wait_ge(hh_ready, FT * n + f + 1)
            dve.tensor_tensor(hp[:, f, 1, :], hid[:, b, :], hp[:, f, 0, :].bitcast(F32), ALU.subtract).then_inc(hl_ready, 1)

        def gu_gate_dve(dve, n, f, b):
            dve.wait_ge(chunk_done, UP0[n] + 2 * f + 1)
            dve.tensor_tensor(gs[:, b, :], bank[b][:], rstd[:], ALU.mult).then_inc(gate_out, 1)

        def gu_hid_act(act, n, f, b):
            act.wait_ge(hid_ready, FT * n + f + 1)
            act.activation(hp[:, f, 0, :], hid[:, b, :], ACT.Copy).then_inc(hh_ready, 1)

        def gu_silu_act(act, n, f, b):
            act.wait_ge(gate_out, FT * n + f + 1)
            act.activation(sg[:, b, :], gs[:, b, :], ACT.Silu).then_inc(silu_ready, 1)

        def gu_dve(dve, n, f, b, c4):
            c = UP0[n] + 2 * f
            split_lo(dve, c + 1, c4 + 1, DT)
            gu_up_dve(dve, n, f - 1, 1 - b)
            gu_low_dve(dve, n, f - 1, 1 - b)
            split_lo(dve, c + 2, c4 + 2, DT)
            gu_gate_dve(dve, n, f, b)

        def gu_act(act, n, f, b, c4):
            c = UP0[n] + 2 * f
            split_hi(act, c + 1, c4 + 1, DT)
            gu_hid_act(act, n, f - 1, 1 - b)
            split_hi(act, c + 2, c4 + 2, DT)
            gu_silu_act(act, n, f, b)

        def gu_loop(eng, n, one, f0, f1):
            with eng.Fori(f0 // 2, f1 // 2) as j:
                for b in (0, 1):
                    if one is gu_pe:
                        one(eng, n, 2 * j + b, b)
                    else:
                        one(eng, n, 2 * j + b, b, 2 * b)

        def down_pe(pe, n, m, b, slot0, first=False):
            d0 = DN0[n]
            if not first:
                pe.wait_ge(x_new, X_DOWN[n] + m - 1)
            for i, (k0, k1) in enumerate(DOWN_PARTS):
                pe.wait_ge(lo_ready, d0 + 3 * m + i + 1)
                for k in range(k0, k1):
                    if first and b == 0 and k == FT - 1:
                        pe.wait_ge(hl_ready, FT * (n + 1))
                    mm = three(pe, bank[4 + b][:], slot0 + i, k - k0, hp[:, k, 0, :], hp[:, k, 1, :],
                               k == 0, k == FT - 1)
                mm.then_inc(chunk_done, 1)

        X_DOWN = (0, 16)

        def x_dve(dve, done, ps, m, factor):
            dve.wait_ge(chunk_done, done)
            dve.scalar_tensor_tensor(xT[:, m, :], ps[:], factor, xT[:, m, :], ALU.mult, ALU.add).then_inc(x_new, 1)

        def part_len(i):
            return DOWN_PARTS[i % 3][1] - DOWN_PARTS[i % 3][0]

        def win_bank(g):
            return bank[4 + g // 4 % 4]

        def win_evac(eng, op, parity, *a):
            for n in range(parity, 8, 2):
                eng.wait_ge(winT_turned, n + 1)
                op(winS[:, 4 * n:4 * n + 4, :].rearrange("p g c -> p (g c)"), bank[4 + n % 4][:],
                   *a).then_inc(win_out[parity], 1)

        def kt_evac(eng, op, parity, *a):
            eng.wait_ge(win_stored, 16)
            eng.wait_ge(kt_done, parity + 1)
            for q in range(4):
                g = 8 * q + 4 * parity
                op(ktS[:, g:g + 4, :, :].rearrange("p g k h -> p (g k h)"), bank[4 + parity][32 * q:32 * q + GH, :],
                   *a).then_inc(kt_out[parity], 1)

        def out_pe(pe, m, b, first=False):
            pe.wait_ge(lo_ready, OUT0 + m + 1)
            if not first:
                pe.wait_ge(x_new, 8 + m - 1)
            for k in range(DT):
                if first and b == 0:
                    pe.wait_ge(ml_ready, k + 1)
                mm = three(pe, bank[5 + b][:], b, k, mh[:, k, :], ml[:, k, :], k == 0, k == DT - 1)
            mm.then_inc(chunk_done, 1)

        def gu_act_first2(act):
            c = UP0[1]
            split_hi(act, c + 1, 1, DT)
            norm_act(act, 2, DT - 1)
            stat_act(act, 2)
            split_hi(act, c + 2, 2, DT)
            gu_silu_act(act, 1, 0, 0)

        def turned_u(op, n, *a):
            o = u_[:, 8 * (n // 2):8 * (n // 2) + 8, 4 * (n % 2):4 * (n % 2) + 4, :]
            i = bank[2 + n % 4][0:C, :].rearrange("c (t g h) -> c g t h", t=4, g=8)
            return op(o, i, *a)

        def turned_y(dst, n, side):
            gt, q = n // 2, n % 2
            o = dst[:, gt + 2 * side, :].rearrange("p (c t) -> p t c", t=T)[:, 4 * q:4 * q + 4, :]
            i = bank[4 + n][:].rearrange("p (t b c) -> p t b c", t=4, b=2)[:, :, side, :]
            return o, i

        UNITS = AT * QT

        def pt_evac(eng, op, u, head, *a):
            w = (u % QT + 1) * P
            eng.wait_ge(pt_done, 2 * u + head + 1)
            op(pts[:, head, 0:w], bank[4 + head][:, 0:w], *a).then_inc(pt_out[head], 1)

        def attn_hi(act, i):
            act.wait_ge(pv_done, QT * (i + 1))
            act.activation(th[:, i, :], bank[6 + i % 2][:], ACT.Copy).then_inc(th_ready, 1)

        def attn_lo(dve, i):
            dve.wait_ge(th_ready, i + 1)
            dve.tensor_tensor(tl[:, i, :], bank[6 + i % 2][:], th[:, i, :].bitcast(F32), ALU.subtract).then_inc(tl_ready, 1)

        END = CHUNKS - 3
        FIN = 3

        def end_place(i):
            return (eh[:, i, :], el[:, i, :]) if i < 2 else (wh[:, 1, :], wl[:, 1, :])

        def end_hi(act, i):
            c, n = END + i, part_len(i) * P
            act.wait_ge(landed[c % RAW], 16 * (c // RAW + 1))
            if i == 2:
                act.wait_ge(chunk_done, END - 1)
            act.activation(end_place(i)[0][:, 0:n], raw[:, c % RAW, 0:n], ACT.Copy).then_inc(hi_ready, 1)

        def end_lo(dve, i):
            c, n = END + i, part_len(i) * P
            hi, lo = end_place(i)
            dve.wait_ge(hi_ready, c + 1)
            dve.tensor_tensor(lo[:, 0:n], raw[:, c % RAW, 0:n], hi[:, 0:n].bitcast(F32), ALU.subtract).then_inc(lo_ready, 1)

        def half(h):
            return slice(h * S // 2, (h + 1) * S // 2)

        def end_tile_pe(pe, h, k):
            i = next(i for i, (k0, k1) in enumerate(DOWN_PARTS) if k < k1)
            k0 = DOWN_PARTS[i][0]
            if h == 0 and k == k0:
                pe.wait_ge(lo_ready, END + i + 1)
            hi, lo = (w[:, (k - k0) * P:(k - k0 + 1) * P] for w in end_place(i))
            ps, r_hi, r_lo = bank[5 * (1 - h)][:, half(h)], hp[:, k, 0, half(h)], hp[:, k, 1, half(h)]
            pe.matmul(ps, hi, r_hi, start=(k == 0), stop=False)
            pe.matmul(ps, hi, r_lo, start=False, stop=False)
            return pe.matmul(ps, lo, r_hi, start=False, stop=(k == FT - 1))

        def end_stat_pe(pe, h):
            pe.wait_ge(acc_ready, DT * FIN + DT + h)
            for t in (2 * h, 2 * h + 1):
                mm = pe.matmul(bank[7 - h][:, t:t + 1], acc[:, t * P:(t + 1) * P], ones[:, 0:1], start=True, stop=True)
            mm.then_inc(ss_ready, 1)

        def end_spread_pe(pe, h):
            pe.wait_ge(dg_ready, FIN + h + 1)
            pe.matmul(bank[7 - h][:, half(h)], ones[:], us[:, half(h)], start=True, stop=True).then_inc(bc_ready, 1)

        def end_act(act, h):
            act.wait_ge(x_new, X_DOWN[1] + DT + h)
            act.wait_ge(acc_ready, DT * FIN + DT - 1)
            act.activation(sq[:, half(h)], xT[:, DT - 1, half(h)], ACT.Square).then_inc(sq_ready, 1)
            act.activation(xg[:, DT - 1, half(h)], xT[:, DT - 1, half(h)], ACT.Copy,
                           scale=gain[:, FIN, DT - 1:DT]).then_inc(xg_ready, 1)
            act.wait_ge(ss_ready, FIN + h + 1)
            act.activation(root[:, 0, 2 * h:2 * h + 2], bank[7 - h][:, 2 * h:2 * h + 2], ACT.Sqrt, scale=1.0 / D,
                           bias=eps[:, 0:1]).then_inc(rt_ready, 1)

        def end_dve(dve, link, h):
            dve.wait_ge(end_done, h + 1)
            dve.scalar_tensor_tensor(xT[:, DT - 1, half(h)], bank[5 * (1 - h)][:, half(h)], 0.5, xT[:, DT - 1, half(h)],
                                     ALU.mult, ALU.add).then_inc(x_new, 1)
            dve.wait_ge(sq_ready, DT * FIN + DT + h)
            dve.tensor_tensor(acc[:, half(h)], acc[:, half(h)], sq[:, half(h)], ALU.add).then_inc(acc_ready, 1)
            dve.wait_ge(rt_ready, FIN + h + 1)
            link(dve.reciprocal(root[:, 1, 2 * h:2 * h + 2], root[:, 0, 2 * h:2 * h + 2]))
            dve.tensor_tensor(us[:, half(h)].rearrange("p (t q) -> p t q", t=2), ident[:].unsqueeze(1).to_broadcast([P, 2, P]),
                              root[:, 1, 2 * h:2 * h + 2].unsqueeze(2).to_broadcast([P, 2, P]),
                              ALU.mult).then_inc(dg_ready, 1)
            dve.wait_ge(bc_ready, FIN + h + 1)
            dve.tensor_copy(rstd[:, half(h)], bank[7 - h][:, half(h)]).then_inc(rstd_ready, 1)
            dve.wait_ge(rstd_ready, FIN + h + 1)
            for i in range(FIN_DVE):
                dve.wait_ge(xg_ready, i + 1)
                dve.tensor_tensor(xg[:, i, half(h)], xg[:, i, half(h)], rstd[:, half(h)], ALU.mult).then_inc(fin_dve, 1)

        def down_act(act, n):
            for m in range(DT):
                c, end = DN0[n] + 3 * m, n == 1 and m == DT - 1
                if end:
                    end_hi(act, 1)
                else:
                    split_hi(act, c + 1, 3 * m + 1, part_len(1))
                if m == 0:
                    gu_hid_act(act, n, FT - 1, 1)
                if end:
                    end_hi(act, 2)
                else:
                    split_hi(act, c + 2, 3 * m + 2, part_len(2))
                if m:
                    norm_act(act, 1 if n == 0 else FIN, m - 1)
                if c + 3 == END:
                    end_hi(act, 0)
                elif not end:
                    split_hi(act, c + 3, 3 * m + 3, DT)

        def down_dve(dve, n):
            for m in range(DT):
                c, end = DN0[n] + 3 * m, n == 1 and m == DT - 1
                if end:
                    end_lo(dve, 1)
                else:
                    split_lo(dve, c + 1, 3 * m + 1, part_len(1))
                if m == 0:
                    gu_up_dve(dve, n, FT - 1, 1)
                    gu_low_dve(dve, n, FT - 1, 1)
                else:
                    x_dve(dve, c, bank[4 + (m - 1) % 2], m - 1, 0.5)
                if end:
                    end_lo(dve, 2)
                else:
                    split_lo(dve, c + 2, 3 * m + 2, part_len(2))
                if m:
                    norm_dve(dve, 1 if n == 0 else FIN, m - 1)
                if c + 3 == END:
                    end_lo(dve, 0)
                elif not end:
                    split_lo(dve, c + 3, 3 * m + 3, DT)

        def prj_dve(dve, i):
            dve.wait_ge(chunk_done, PRJ0 + i + 1)
            dve.tensor_tensor(prj[:, i, :], bank[i % 2][:], rstd[:], ALU.mult).then_inc(prj_out, 1)

        def attn_norm(dve, link, s):
            if s:
                dve.wait_ge(pt_out[0], s)
            else:
                dve.wait_ge(yh_ready, 1)
            w = (s % QT + 1) * P
            link(dve.reciprocal(rec[:, 2 * s:2 * s + 2], sums[:, 2 * s:2 * s + 2]))
            for head in (0, 1):
                p = pr[:, 2 * (s % 2) + head, 0:w]
                ins = dve.tensor_scalar(p, p, rec[:, 2 * s + head:2 * s + head + 1], None, ALU.mult)
            ins.then_inc(pn_ready, 1)

        block = ctx.enter_context(nc.Block())

        @block.sync
        def _(sp):
            def load(c, slot, src, n, first=False):
                if not first:
                    sp.wait_ge(lo_ready, c - RAW + 1)
                sp.dma_start(raw[:, slot % RAW, 0:n * P], src).then_inc(landed[slot % RAW], 16)

            def up_loads(n, f0, f1):
                with sp.Fori(f0 // 2, f1 // 2) as i:
                    for j in range(4):
                        load(UP0[n] + 4 * i + j, j, w_up[n, 2 * i + j // 2, j % 2], DT)

            def down_loads(n):
                with sp.Fori(0, DT // 4) as i:
                    for j in range(12):
                        k0, k1 = DOWN_PARTS[j % 3]
                        load(DN0[n] + 12 * i + j, j, w_down[n, 4 * i + j // 3, :, k0 * P:k1 * P], k1 - k0)

            def x_load(j):
                sp.dma_start(xT[:, 2 * j:2 * j + 2, :], x[:, 2 * j:2 * j + 2, :]).then_inc(x_in[j], 16)

            sp.dma_start(gain[:], gains).then_inc(g_in, 16)
            sp.dma_start(xT[:, 0, :], x[:, 0, :]).then_inc(x_first, 16)
            sp.dma_start(raw[:, 0, 0:MID], w_up[0, 0, 0, :, 0:MID]).then_inc(w_first[0], 16)
            sp.dma_start(xT[:, 1, :], x[:, 1, :]).then_inc(x_in[0], 16)
            sp.dma_start(raw[:, 1, 0:MID], w_up[0, 0, 1, :, 0:MID]).then_inc(w_first[1], 16)
            x_load(1)
            sp.dma_start(raw[:, 0, MID:D], w_up[0, 0, 0, :, MID:D]).then_inc(landed[0], 16)
            x_load(2)
            sp.dma_start(raw[:, 1, MID:D], w_up[0, 0, 1, :, MID:D]).then_inc(landed[1], 16)
            x_load(3)
            for j in (2, 3):
                load(j, j, w_up[0, j // 2, j % 2], DT, first=True)
            up_loads(0, 2, X_AGAIN)
            sp.wait_ge(kt_stored, 16)
            for j in range(4):
                x_load(j)
            up_loads(0, X_AGAIN, FT)
            down_loads(0)
            with sp.Fori(0, AT) as i:
                for j in range(4):
                    load(PRJ0 + 4 * i + j, j, w_proj[4 * i + j], DT)
            with sp.Fori(0, DT // 4) as i:
                for j in range(4):
                    load(ATT0 + 4 * i + j, j, w_gate[4 * i + j], DT)
            with sp.Fori(0, DT) as m:
                for j in range(4):
                    load(MRG0 + 4 * m + j, j, w_merge[m, :, MK * j * P:MK * (j + 1) * P], MK)
            with sp.Fori(0, DT // 4) as i:
                for j in range(4):
                    load(OUT0 + 4 * i + j, j, w_out[4 * i + j], DT)
            up_loads(1, 0, FT)
            down_loads(1)
            for h in (0, 1):
                for i0, i1 in ((0, 1), (1, 3), (5, 6), (3, 5), (6, 8)):
                    if i1 <= FIN_DVE:
                        sp.wait_ge(fin_dve, FIN_DVE * h + i1)
                    else:
                        sp.wait_ge(fin_pool, (DT - FIN_DVE) * h + i1 - FIN_DVE)
                    sp.dma_start(out[:, i0:i1, half(h)], xg[:, i0:i1, half(h)]).then_inc(out_done, 16)
            sp.wait_ge(out_done, 16 * 10)

        @block.tensor
        def _(pe):
            pe.wait_ge(set_up, 1)
            for _ in range(WARM):
                pe.matmul(bank[7][:, 0:P], ones[:], ones[:], start=True, stop=True)
            for c, k0, k1 in ((0, 0, 2), (1, 0, 2), (0, 2, 4), (1, 2, 4), (0, 4, 8), (1, 4, 8)):
                pe.wait_ge(lo_ready if k0 >= DT // 2 else lo_first, c + 1)
                for k in range(k0, k1):
                    pe.wait_ge(al_ready, k + 1)
                    mm = three(pe, bank[2 * c][:], c, k, ah[:, k, :], al[:, k, :], k == 0, k == DT - 1)
                if k1 == DT:
                    mm.then_inc(chunk_done, 1)
            for c in (2, 3):
                pe.wait_ge(lo_ready, c + 1)
                for k in range(DT):
                    mm = three(pe, bank[2 * c - 3][:], c, k, ah[:, k, :], al[:, k, :], k == 0, k == DT - 1)
                    if c == 2 and k == 6:
                        stat_pe(pe, 0)
                    if c == 3 and k == 3:
                        spread_pe(pe, 0)
                mm.then_inc(chunk_done, 1)
            gu_loop(pe, 0, gu_pe, 2, 8)
            pe.wait_ge(winT_ready, 1)
            pe.wait_ge(i_in, 16)
            for g in range(G):
                n = g // 4
                if n >= 4 and g % 4 == 0:
                    pe.wait_ge(win_out[n % 2], (n - 4) // 2 + 1)
                tr = pe.transpose(win_bank(g)[:, (g % 4) * P:(g % 4 + 1) * P],
                                  winT[:, g, :, :].rearrange("p t h -> p (t h)"), ident[:])
                if g % 4 == 3:
                    tr.then_inc(winT_turned, 1)
            gu_loop(pe, 0, gu_pe, 8, 12)
            pe.wait_ge(ce_ready, 4)
            for i in range(8):
                for q in range(4):
                    g = 8 * q + i
                    mm = pe.matmul(bank[4 + i // 4][32 * q:32 * q + GH, (i % 4) * P:(i % 4 + 1) * P], bb[:, g, :],
                                   ce_w[:, g, 0:T, :].rearrange("p k h -> p (k h)"), start=True, stop=True)
                if i % 4 == 3:
                    mm.then_inc(kt_done, 1)
            gu_loop(pe, 0, gu_pe, 12, 14)
            gu_loop(pe, 0, gu_pe, 14, FT)
            down_pe(pe, 0, 0, 0, 0, first=True)
            down_pe(pe, 0, 1, 1, 1, first=True)
            with pe.Fori(1, DT // 2) as j:
                for b in (0, 1):
                    down_pe(pe, 0, 2 * j + b, b, b)

            def prj_pe(i, b, known=True, norm=None, spread=None):
                pe.wait_ge(lo_ready, PRJ0 + i + 1)
                if known:
                    pe.wait_ge(prj_out, i - 1)
                for k in range(DT):
                    if norm is not None:
                        pe.wait_ge(al_ready, 8 * norm + k + 1)
                    mm = three(pe, bank[b][:], b, k, ah[:, k, :], al[:, k, :], k == 0, k == DT - 1)
                    if spread is not None and k == DT // 2:
                        spread_pe(pe, spread)
                mm.then_inc(chunk_done, 1)
                if norm is not None:
                    stat_pe(pe, norm)

            def turn_u(r):
                pe.wait_ge(prj_out, AT)
                for ct in (2 * r, 2 * r + 1):
                    for q in (0, 1):
                        n = 2 * ct + q
                        if n >= 4:
                            pe.wait_ge(u_act if n % 2 == 0 else u_dve, (n - 4) // 2 + 1)
                        for j in range(4):
                            t = T - 1 - (4 * q + j)
                            tr = pe.transpose(bank[2 + n % 4][0:C, j * P:(j + 1) * P],
                                              prj[:, ct, t:S:T], ident[:])
                        tr.then_inc(tu_done, 1)

            prj_pe(0, 0, known=False, norm=1)
            prj_pe(1, 1, known=False, spread=1)
            prj_pe(2, 0)
            prj_pe(3, 1)
            prj_pe(4, 0)
            turn_u(0)
            prj_pe(5, 1)
            turn_u(1)
            prj_pe(6, 0)
            pe.wait_ge(u_act, 4)
            pe.wait_ge(u_dve, 4)
            for g in range(G):
                tr = pe.transpose(bank[2 + g // 8][:, (g % 8) * C:(g % 8 + 1) * C],
                                  u_[:, g, :, :].rearrange("c t h -> c (t h)"), ident[0:C, 0:C])
                if g % 8 == 7:
                    tr.then_inc(tc_done, 1)
            prj_pe(7, 1)
            pe.wait_ge(tab_in[0], 16)
            for g in range(G):
                if g % 8 == 0:
                    pe.wait_ge(uc_act if g // 8 % 2 == 0 else uc_dve, g // 16 + 1)
                mm = pe.matmul(bank[2 + g // 8][:, (g % 8) * C:(g % 8 + 1) * C], win[:, g, :], uc[:, g, :],
                               start=True, stop=True)
                if g % 8 == 7:
                    mm.then_inc(z_done, 1)
            with pe.Fori(4, 2 * AT) as j:
                for b in (0, 1):
                    prj_pe(2 * j + b, b)

            pe.wait_ge(tab_in[3], 16)
            pe.wait_ge(toep_in, 16 * T)
            pe.wait_ge(hs_ready, 1)
            for j in range(G // 2):
                for part in (0, 1):
                    for side in (0, 1):
                        g = j + G // 2 * side
                        ps = bank[2 + j // 4][C * side:C * (side + 1), (j % 4) * P:(j % 4 + 1) * P]
                        if part == 0:
                            pe.matmul(ps, uc[:, g, :], toep[:, g, :], start=True, stop=False)
                        else:
                            mm = pe.matmul(ps, hs[:, g, :], ce[:, g, 1:NA, :].rearrange("p k h -> p (k h)"),
                                           start=False, stop=True)
                if j % 4 == 3:
                    mm.then_inc(y_done, 1)
            pe.wait_ge(prj_out, 4 * AT)
            for kb in range(QT):
                for i in range(AT):
                    tr = pe.transpose(bank[(0, 1, 6, 7)[kb]][:, i * P:(i + 1) * P],
                                      prj[:, 3 * AT + i, kb * P:(kb + 1) * P], ident[:])
                tr.then_inc(tv_done, 1)

            def scores(u):
                i, qt = u // QT, u % QT
                if u == 0:
                    pe.wait_ge(gelu_ready, 2)
                else:
                    pe.wait_ge(nmx_ready, u)
                for head in (0, 1):
                    rows = slice(HD * head, HD * (head + 1))
                    mm = pe.matmul(bank[2 + head][:, 0:(qt + 1) * P], prj[rows, 2 * AT + i, qt * P:(qt + 1) * P],
                                   prj[rows, AT + i, 0:(qt + 1) * P], start=True, stop=True)
                mm.then_inc(sc_done, 1)

            def turn_p(u):
                qt = u % QT
                if u == 0:
                    pe.wait_ge(yl_ready, 8)
                pe.wait_ge(pn_ready, u + 1)
                for head in (0, 1):
                    for kb in range(qt + 1):
                        tr = pe.transpose(bank[4 + head][:, kb * P:(kb + 1) * P],
                                          pr[:, 2 * (u % 2) + head, kb * P:(kb + 1) * P], ident[:])
                    tr.then_inc(pt_done, 1)

            def pv(u):
                i, qt = u // QT, u % QT
                if qt == 0 and i >= 2:
                    pe.wait_ge(tl_ready, i - 1)
                pe.wait_ge(pt_out[0], u + 1)
                pe.wait_ge(pt_out[1], u + 1)
                for kb in range(qt + 1):
                    for head in (0, 1):
                        h = 2 * i + head
                        mm = pe.matmul(bank[6 + i % 2][HD * head:HD * (head + 1), qt * P:(qt + 1) * P],
                                       v_[:, kb, h * HD:(h + 1) * HD], pts[:, head, kb * P:(kb + 1) * P],
                                       start=(kb == 0), stop=(kb == qt))
                mm.then_inc(pv_done, 1)

            def turn_y():
                pe.wait_ge(gelu_ready, 4)
                pe.wait_ge(v_out, QT)
                for n in range(4):
                    for j in range(4):
                        tr = pe.transpose(bank[4 + n][:, j * P:(j + 1) * P], y_[:, n // 2, 4 * (n % 2) + j, :], ident[:])
                    tr.then_inc(ty_done, 1)

            def g_attn(s, k0):
                m = s // 2
                if s % 2 == 0 and k0 == 0:
                    pe.wait_ge(lo_ready, ATT0 + m + 1)
                    if m < 2:
                        pe.wait_ge(v_out, m + 1)
                    else:
                        pe.wait_ge(ga_out, m - 1)
                for k in range(k0 + 4 * (s % 2), k0 + 4 * (s % 2) + 2):
                    mm = three(pe, bank[m % 2][:], m, k, ah[:, k, :], al[:, k, :], k == 0, k == DT - 1)
                if k == DT - 1:
                    mm.then_inc(chunk_done, 1)

            for s in range(UNITS):
                scores(s)
                if s >= 2:
                    pv(s - 2)
                g_attn(s, 0)
                if s == 0:
                    turn_y()
                else:
                    turn_p(s - 1)
                g_attn(s, 2)

            def merge_pe(m, first=False):
                def tile(kk):
                    j, k = kk // MK, kk % MK
                    if k == 0:
                        pe.wait_ge(lo_ready, MRG0 + 4 * m + j + 1)
                    if kk < DT:
                        if kk == 0 and not first:
                            pe.wait_ge(gs_out, m)
                        ps, r, rl, i, n = bank[0], ah, al, kk, DT
                    elif kk < DT + AT:
                        if kk == DT and not first:
                            pe.wait_ge(yv_out, m)
                        ps, r, rl, i, n = bank[2], yh, yl, kk - DT, AT
                    elif kk < DT + 2 * AT:
                        if kk == DT + AT and not first:
                            pe.wait_ge(sgy_ready, m)
                        ps, r, rl, i, n = bank[3], yh, yl, kk - DT - AT, AT
                    else:
                        i = kk - DT - 2 * AT
                        if first:
                            if i == 0:
                                pe.wait_ge(ga_out, DT)
                            pe.wait_ge(tl_ready, i + 1)
                        elif i == 0:
                            pe.wait_ge(au_out, m)
                        ps, r, rl, n = bank[1], th, tl, AT
                    mm = three(pe, ps[:], j, k, r[:, i, :], rl[:, i, :], i == 0, i == n - 1)
                    if k == MK - 1:
                        mm.then_inc(chunk_done, 1)
                    elif kk == DT + 2 * AT - 1:
                        mm.then_inc(yg_done, 1)

                for kk in range(4 * MK):
                    tile(kk)
                    if first and kk == 1:
                        turn_p(UNITS - 1)
                    if first and kk == 4:
                        pv(UNITS - 1)

            pv(UNITS - 2)
            pe.wait_ge(ga_out, DT - 1)
            merge_pe(0, first=True)
            with pe.Fori(1, DT) as m:
                merge_pe(m)

            for m in range(2):
                out_pe(pe, m, m, first=True)
            with pe.Fori(1, DT // 2) as j:
                for b in (0, 1):
                    out_pe(pe, 2 * j + b, b)

            gu_pe(pe, 1, 0, 0, known=False, norm=2)
            gu_pe(pe, 1, 1, 1, known=False)
            gu_loop(pe, 1, gu_pe, 2, FT)
            down_pe(pe, 1, 0, 0, 0, first=True)
            down_pe(pe, 1, 1, 1, 1, first=True)
            with pe.Fori(1, DT // 2 - 1) as j:
                for b in (0, 1):
                    down_pe(pe, 1, 2 * j + b, b, b)
            down_pe(pe, 1, DT - 2, 0, 0)
            pe.wait_ge(x_new, X_DOWN[1] + DT - 2)
            for h in (0, 1):
                for k in range(FT):
                    mm = end_tile_pe(pe, h, k)
                    if h and k == 7:
                        end_stat_pe(pe, 0)
                    if h and k == 14:
                        end_spread_pe(pe, 0)
                mm.then_inc(end_done, 1)
            end_stat_pe(pe, 1)
            end_spread_pe(pe, 1)

        @block.scalar
        def _(act):
            A = Count(ca)
            act.wait_ge(set_up, 1)
            act.activation(root[:, 0, 0:1], eps[:], ACT.Square)
            act.wait_ge(g_in, 16)
            act.wait_ge(x_first, 16)
            scale_act(act, 0, 0)
            first_hi(act, 0, 0)
            act.wait_ge(x_in[0], 16)
            scale_act(act, 0, 1)
            first_hi(act, 1, 0)
            for j in range(1, 4):
                act.wait_ge(x_in[j], 16)
                scale_act(act, 0, 2 * j)
                scale_act(act, 0, 2 * j + 1)
                if j < 3:
                    first_hi(act, j - 1, 1)
            square_act(act, 0, 0)
            square_act(act, 0, 1)
            for i in range(2, DT):
                square_act(act, 0, i)
                if i == 2:
                    act.wait_ge(s_in, 16 * 4)
                    act.activation(small[:, 3, :], small[:, 2, :], ACT.Exp).then_inc(prep_act, 1)
                if i in (2, 4):
                    split_hi(act, i // 2 + 1, i // 2 + 1, DT)
            stat_act(act, 0)
            split_hi(act, 4, 4, DT)
            gu_silu_act(act, 0, 0, 0)
            gu_hid_act(act, 0, 0, 0)
            gu_silu_act(act, 0, 1, 1)
            split_hi(act, 5, 5, DT)
            gu_hid_act(act, 0, 1, 1)
            split_hi(act, 6, 6, DT)
            gu_silu_act(act, 0, 2, 0)
            gu_act(act, 0, 3, 1, 6)
            split_hi(act, 9, 9, DT)
            act.wait_ge(prep_dve, 1)
            act.activation(mag[:, :, :], expo[:, :, :], ACT.Exp)
            act.activation(mag8[:, :], small[:, 22, :], ACT.Exp).then_inc(prep_act, 1)
            act.activation(sn[:, :, :], ang[:, :, :], ACT.Sin)
            act.activation(cs[:, :, :].rearrange("p g k -> p (g k)"), tn[:], ACT.Sin).then_inc(prep_act, 1)
            gu_hid_act(act, 0, 3, 1)
            split_hi(act, 10, 10, DT)
            gu_silu_act(act, 0, 4, 0)
            gu_act(act, 0, 5, 1, 10)
            gu_loop(act, 0, gu_act, 6, 8)
            win_evac(act, act.activation, 0, ACT.Copy)
            gu_loop(act, 0, gu_act, 8, 12)
            kt_evac(act, act.activation, 0, ACT.Copy)
            gu_loop(act, 0, gu_act, 12, 14)
            act.wait_ge(stored, 16 * 3)
            gu_loop(act, 0, gu_act, 14, FT)
            down_act(act, 0)

            zx_v = zx[:, :, :].rearrange("p g c -> p (g c)")
            for i in range(4 * AT):
                split_hi(act, PRJ0 + i + 1, i + 1, DT)
                if i == 0:
                    norm_act(act, 1, DT - 1)
                    stat_act(act, 1)
                if i in (5, 6):
                    for n in range(4 * (i - 5), 4 * (i - 4), 2):
                        act.wait_ge(tu_done, n + 1)
                        turned_u(act.activation, n, ACT.Copy).then_inc(u_act, 1)
                if i == 7:
                    for n in (0, 2):
                        act.wait_ge(tc_done, n + 1)
                        act.activation(uc[:, 8 * n:8 * n + 8, :].rearrange("p g c -> p (g c)"), bank[2 + n][:],
                                       ACT.Copy).then_inc(uc_act, 1)
                if i == 8:
                    act.wait_ge(z_done, 4)
                    for n in range(4):
                        cols = slice(n * S, (n + 1) * S)
                        act.activation(zx_v[0:NS, cols], bank[2 + n][NS:P, :], ACT.Copy)
                        act.activation(zx_v[NS:P, cols], bank[2 + n][0:NS, :], ACT.Copy, scale=-1.0).then_inc(zx_ready, 1)
                if i == 12:
                    act.wait_ge(scan_ready, G)
                    g_v = zg[:, :, :].rearrange("p g c -> p (g c)")
                    act.activation(g_v[0:NS, :], zx_v[NS:P, :], ACT.Copy, scale=-1.0)
                    act.activation(g_v[NS:P, :], zx_v[0:NS, :], ACT.Copy).then_inc(gx_ready, 1)
            for n in range(4):
                act.wait_ge(y_done, n + 1)
                o = y_[:, n // 2, :, 64 * (n % 2):64 * (n % 2) + 64].rearrange("p t (j h) -> p j t h", j=4)
                act.activation(o, bank[2 + n][:].rearrange("p (j t h) -> p j t h", j=4, t=T),
                               ACT.Gelu_apprx_tanh).then_inc(gelu_ready, 1)
            def act_slot(s):
                if s < UNITS:
                    w = (s % QT + 1) * P
                    act.wait_ge(nmx_ready, s + 1)
                    if s >= 2:
                        act.wait_ge(pt_done, 2 * (s - 1))
                    for head in (0, 1):
                        u = 2 * s + head
                        exp = act.activation(pr[:, 2 * (s % 2) + head, 0:w], sc[:, head, 0:w], ACT.Exp,
                                             bias=nmx[:, u:u + 1], scale=HD ** -0.5, accum_out=sums[:, u:u + 1])
                    exp.then_inc(exp_ready, 1)
                if s:
                    pt_evac(act, act.activation, s - 1, 0, ACT.Copy)

            for s in range(UNITS):
                if s % 2 == 0:
                    split_hi(act, ATT0 + s // 2 + 1, s // 2 + 1, DT if s < UNITS - 2 else MK)
                act_slot(s)
                if s == 0:
                    for n in range(4):
                        act.wait_ge(ty_done, n + 1)
                        for side in (0, 1):
                            o, i_ = turned_y(yh, n, side)
                            act.activation(o, i_, ACT.Copy).then_inc(yh_ready, 1)
                if s % QT == 1 and s > QT:
                    attn_hi(act, s // QT - 1)

            def merge_act(m, first=False, last=False):
                c = MRG0 + 4 * m
                if first:
                    act_slot(UNITS)
                split_hi(act, c + 1, 1, MK)
                if not first:
                    merge_act_end(m - 1)
                split_hi(act, c + 2, 2, MK)
                if first:
                    act.wait_ge(ga_out, DT)
                else:
                    act.wait_ge(au_out, m)
                act.activation(sg[:, 0, :], ga[:, m, :], ACT.Sigmoid).then_inc(sga_ready, 1)
                if first:
                    attn_hi(act, AT - 1)
                split_hi(act, c + 3, 3, MK)
                act.wait_ge(gs_out, m + 1)
                act.activation(sg[:, 1, :], gs[:, 1, :], ACT.Sigmoid).then_inc(sgs_ready, 1)
                split_hi(act, c + 4, 4, DT if last else MK)
                act.wait_ge(yg_done, m + 1)
                act.activation(us[:], bank[3][:], ACT.Sigmoid).then_inc(sgy_ready, 1)

            def merge_act_end(m):
                act.wait_ge(mg_ready, m + 1)
                act.activation(mh[:, m, :], hid[:, 1, :], ACT.Copy).then_inc(mh_ready, 1)

            merge_act(0, first=True)
            with act.Fori(1, DT - 1) as m:
                merge_act(m)
            merge_act(DT - 1, last=True)
            for m in range(DT):
                split_hi(act, OUT0 + m + 1, m + 1, DT)
                if m == 0:
                    merge_act_end(DT - 1)
                else:
                    norm_act(act, 2, m - 1)
            gu_act_first2(act)
            gu_act(act, 1, 1, 1, 2)
            gu_loop(act, 1, gu_act, 2, FT)
            down_act(act, 1)
            act.activation(root[:, 0, 0:1], eps[:], ACT.Sqrt)
            end_act(act, 0)
            end_act(act, 1)

        @block.vector
        def _(dve):
            V = Count(cd)

            def link(ins):
                V.link(dve, ins)

            dve.memset(ones[:], 1.0)
            dve.memset(eps[:], EPS).then_inc(set_up, 1)

            def reduce_angle(r, n_, x_in_, consts):
                link(dve.tensor_scalar(n_, x_in_, 1.0 / (2 * PI), MAGIC, ALU.mult, ALU.add))
                link(dve.tensor_scalar(n_, n_, MAGIC, None, ALU.subtract))
                src = x_in_
                for c_ in consts:
                    link(dve.scalar_tensor_tensor(r, n_, -c_, src, ALU.mult, ALU.add))
                    src = r
                link(dve.tensor_scalar(r, r, PI, -PI, ALU.min, ALU.max))

            sm = [small[:, j, :] for j in range(24)]
            lre, lim, _, dt, lr, an, r0, p8, p64, nn, den, t1 = sm[:12]
            tt, ts = dve.tensor_tensor, dve.tensor_scalar
            for i in range(DT):
                scale_dve(dve, 0, i)
                if i < 2:
                    first_lo(dve, i, 0)
                elif i in (3, 5):
                    first_lo(dve, i // 2 - 1, 1)
            for i in range(DT):
                square_dve(dve, 0, i)
                if i in (2, 4):
                    split_lo(dve, i // 2 + 1, i // 2 + 1, DT)
            dve.wait_ge(prep_act, 1)
            link(tt(lr, lre, dt, ALU.mult))
            link(tt(an, lim, dt, ALU.mult))
            reduce_angle(r0, nn, an, TWO_PI)
            stat_dve(dve, link, 0)
            split_lo(dve, 4, 4, DT)
            rstd_dve(dve, 0)
            gu_gate_dve(dve, 0, 0, 0)
            gu_up_dve(dve, 0, 0, 0)
            gu_gate_dve(dve, 0, 1, 1)
            gu_low_dve(dve, 0, 0, 0)
            link(ts(an, r0, 8.0, None, ALU.mult))
            reduce_angle(p8, nn, an, TWO_PI)

            def angles(k0, k1, base):
                k = mult[:, k0:k1].unsqueeze(1).to_broadcast([P, G, k1 - k0])
                return tt(ang[:, :, k0:k1], base.unsqueeze(2).to_broadcast([P, G, k1 - k0]), k, ALU.mult)

            split_lo(dve, 5, 5, DT)
            gu_up_dve(dve, 0, 1, 1)
            gu_low_dve(dve, 0, 1, 1)
            link(ts(an, p8, 8.0, None, ALU.mult))
            reduce_angle(p64, nn, an, TWO_PI)
            angles(0, NA, r0)
            angles(NA, NA + NB, p8)
            link(angles(NA + NB, NK, p64))
            split_lo(dve, 6, 6, DT)
            gu_gate_dve(dve, 0, 2, 0)
            ang_v = ang[:, :, :].rearrange("p g k -> p (g k)")
            reduce_angle(ang_v, tn[:], ang_v, TWO_PI[:2])
            split_lo(dve, 7, 7, DT)
            gu_up_dve(dve, 0, 2, 0)
            gu_low_dve(dve, 0, 2, 0)
            link(ts(tn[:], ang_v, PI / 2, -2 * PI, ALU.is_gt, ALU.mult))
            split_lo(dve, 8, 8, DT)
            gu_gate_dve(dve, 0, 3, 1)
            tt(expo[:, :, :], lr.unsqueeze(2).to_broadcast([P, G, NA]),
               mult[:, 0:NA].unsqueeze(1).to_broadcast([P, G, NA]), ALU.mult)
            ts(sm[22], lr, 8.0, None, ALU.mult)
            link(dve.scalar_tensor_tensor(tn[:], ang_v, PI / 2, tn[:], ALU.add, ALU.add))
            dve.tensor_scalar(tn[:], tn[:], PI, -PI, ALU.min, ALU.max).then_inc(prep_dve, 1)
            link(tt(den, lre, lre, ALU.mult))
            link(tt(t1, lim, lim, ALU.mult))
            link(tt(den, den, t1, ALU.add))
            dve.reciprocal(den, den).then_inc(prep_dve, 1)
            gu_loop(dve, 0, gu_dve, 4, 8)
            win_evac(dve, dve.tensor_copy, 1)
            gu_loop(dve, 0, gu_dve, 8, 12)
            kt_evac(dve, dve.tensor_copy, 1)
            gu_loop(dve, 0, gu_dve, 12, 14)
            dve.wait_ge(stored, 16 * 3)
            gu_loop(dve, 0, gu_dve, 14, FT)
            for j in range(4):
                dve.wait_ge(x_in[j], 32)
            down_dve(dve, 0)

            flat = "p g c -> p (g c)"
            zg_v, zx_v, cos_v = (t[:, :, :].rearrange(flat) for t in (zg, zx, cosT))
            for i in range(4 * AT):
                split_lo(dve, PRJ0 + i + 1, i + 1, DT)
                if i == 0:
                    x_dve(dve, PRJ0, bank[5], DT - 1, 0.5)
                    norm_dve(dve, 1, DT - 1)
                    stat_dve(dve, link, 1)
                else:
                    if i == 1:
                        rstd_dve(dve, 1)
                    prj_dve(dve, i - 1)
                if i in (5, 6):
                    for n in range(4 * (i - 5) + 1, 4 * (i - 4), 2):
                        dve.wait_ge(tu_done, n + 1)
                        turned_u(dve.tensor_copy, n).then_inc(u_dve, 1)
                if i == 7:
                    for n in (1, 3):
                        dve.wait_ge(tc_done, n + 1)
                        dve.tensor_copy(uc[:, 8 * n:8 * n + 8, :].rearrange(flat), bank[2 + n][:]).then_inc(uc_dve, 1)
                if i == 8:
                    dve.wait_ge(z_done, 4)
                    dve.wait_ge(tab_in[1], 16)
                    for n in range(4):
                        dve.wait_ge(zx_ready, n + 1)
                        cols = slice(n * S, (n + 1) * S)
                        ins = tt(zg_v[:, cols], bank[2 + n][:], cos_v[:, cols], ALU.mult)
                    link(ins)
                if i == 10:
                    dve.wait_ge(zx_sin, 1)
                    link(tt(zg_v, zg_v, zx_v, ALU.add))
                if i in (10, 11):
                    for g in range(16 * (i - 10), 16 * (i - 9)):
                        dve.tensor_tensor_scan(zx[:, g, :], mag8[:, g:g + 1].to_broadcast([P, C]), zg[:, g, :],
                                               0.0, ALU.mult, ALU.add).then_inc(scan_ready, 1)
                if i == 13:
                    dve.wait_ge(scan_ready, G)
                    dve.memset(hs[:, :, 0:1], 0.0)
                    link(tt(hs[:, :, 1:C], zx[:, :, 0:C - 1], cosT[:, :, 0:C - 1], ALU.mult))
                if i == 14:
                    dve.wait_ge(gx_sin, 1)
                    tt(hs[:, :, 1:C], hs[:, :, 1:C], zg[:, :, 0:C - 1], ALU.add).then_inc(hs_ready, 1)
            prj_dve(dve, 4 * AT - 1)
            for kb in range(QT):
                dve.wait_ge(tv_done, kb + 1)
                if kb == 0:
                    dve.wait_ge(hs_ready, 1)
                dve.tensor_copy(v_[:, kb, :], bank[(0, 1, 6, 7)[kb]][:]).then_inc(v_out, 1)

            def dve_slot(s):
                if s < UNITS:
                    i, qt = s // QT, s % QT
                    w, o = (qt + 1) * P, (QT - 1 - qt) * P
                    dve.wait_ge(sc_done, s + 1)
                    dve.wait_ge(bias_ready, 2 * (i + 1))
                    if s:
                        dve.wait_ge(exp_ready, s)
                    for head in (0, 1):
                        ttr = dve.tensor_tensor_reduce(sc[:, head, 0:w], bank[2 + head][:, 0:w],
                                                       bias[:, (2 * i + head) % 4, o:o + w], 1.0, -3.0e38,
                                                       ALU.add, ALU.max, mx[:, 2 * s + head:2 * s + head + 1])
                    link(ttr)
                    dve.tensor_scalar(nmx[:, 2 * s:2 * s + 2], mx[:, 2 * s:2 * s + 2], -(HD ** -0.5), None,
                                      ALU.mult).then_inc(nmx_ready, 1)
                if s:
                    pt_evac(dve, dve.tensor_copy, s - 1, 1)

            def ga_dve(m):
                dve.wait_ge(chunk_done, ATT0 + m + 1)
                tt(ga[:, m, :], bank[m % 2][:], rstd[:], ALU.mult).then_inc(ga_out, 1)

            for s in range(UNITS):
                dve_slot(s)
                if s % 2 == 0:
                    split_lo(dve, ATT0 + s // 2 + 1, s // 2 + 1, DT if s < UNITS - 2 else MK)
                attn_norm(dve, link, s)
                if s % 2 == 0 and s:
                    ga_dve(s // 2 - 1)
                if s == 0:
                    for n in range(4):
                        dve.wait_ge(yh_ready, 2 * n + 2)
                        for side in (0, 1):
                            o, i_ = turned_y(yl, n, side)
                            oh, _ = turned_y(yh, n, side)
                            tt(o, i_, oh.bitcast(F32), ALU.subtract).then_inc(yl_ready, 1)
                if s % QT == 1 and s > QT:
                    attn_lo(dve, s // QT - 1)

            def merge_dve(m, first=False, last=False):
                c = MRG0 + 4 * m
                if first:
                    ga_dve(DT - 1)
                    dve_slot(UNITS)
                split_lo(dve, c + 1, 1, MK)
                if not first:
                    merge_dve_end(m - 1)
                split_lo(dve, c + 2, 2, MK)
                dve.wait_ge(chunk_done, c + 2)
                tt(gs[:, 1, :], bank[0][:], rstd[:], ALU.mult).then_inc(gs_out, 1)
                if first:
                    attn_lo(dve, AT - 1)
                split_lo(dve, c + 3, 3, MK)
                dve.wait_ge(chunk_done, c + 3)
                dve.wait_ge(sgs_ready, m + 1)
                tt(acc[:], bank[2][:], sg[:, 1, :], ALU.mult).then_inc(yv_out, 1)
                split_lo(dve, c + 4, 4, DT if last else MK)
                dve.wait_ge(sgy_ready, m + 1)
                dve.wait_ge(yv_out, m + 1)
                tt(acc[:], acc[:], us[:], ALU.mult).then_inc(me, 1)

            def merge_dve_end(m):
                dve.wait_ge(chunk_done, MRG0 + 4 * m + 4)
                dve.wait_ge(sga_ready, m + 1)
                tt(hid[:, 0, :], bank[1][:], sg[:, 0, :], ALU.mult).then_inc(au_out, 1)
                dve.wait_ge(me, m + 1)
                dve.wait_ge(au_out, m + 1)
                tt(hid[:, 1, :], hid[:, 0, :], acc[:], ALU.add).then_inc(mg_ready, 1)
                dve.wait_ge(mh_ready, m + 1)
                tt(ml[:, m, :], hid[:, 1, :], mh[:, m, :].bitcast(F32), ALU.subtract).then_inc(ml_ready, 1)

            merge_dve(0, first=True)
            with dve.Fori(1, DT - 1) as m:
                merge_dve(m)
            merge_dve(DT - 1, last=True)
            for m in range(DT):
                if m == 0:
                    merge_dve_end(DT - 1)
                split_lo(dve, OUT0 + m + 1, m + 1, DT)
                if m:
                    x_dve(dve, OUT0 + m, bank[5 + (m - 1) % 2], m - 1, 1.0)
                    norm_dve(dve, 2, m - 1)
            c = UP0[1]
            split_lo(dve, c + 1, 1, DT)
            x_dve(dve, c, bank[6], DT - 1, 1.0)
            norm_dve(dve, 2, DT - 1)
            stat_dve(dve, link, 2)
            split_lo(dve, c + 2, 2, DT)
            rstd_dve(dve, 2)
            gu_gate_dve(dve, 1, 0, 0)
            gu_dve(dve, 1, 1, 1, 2)
            gu_loop(dve, 1, gu_dve, 2, FT)
            down_dve(dve, 1)
            end_dve(dve, link, 0)
            end_dve(dve, link, 1)

        @block.gpsimd
        def _(pool):
            K = Count(cp)

            def link(ins):
                K.link(pool, ins)

            for dst, src in ((small[:, 2, :], log_dt), (small[:, 0, :], lam_re), (small[:, 1, :], lam_im),
                             (mult[:], multiples_in)):
                pool.dma_start(dst, src).then_inc(s_in, 16)
            pool.dma_start(ident[:], ident_in).then_inc(i_in, 16)
            pool.wait_ge(landed[1], 16)
            for dst, src in ((bS[:], b_swap), (signs[:], signs_in), (cO[:], c_own), (cR[:], c_swap),
                             (bO[:], b_own)):
                pool.dma_start(dst, src).then_inc(c_in, 16)
            tt, ts = pool.tensor_tensor, pool.tensor_scalar

            def over_h(t, k0, k1):
                return t[:, :, k0:k1].unsqueeze(3).to_broadcast([P, G, k1 - k0, GH])

            def over_k(t, k):
                return t[:, :, :].unsqueeze(2).to_broadcast([P, G, k, GH])

            pool.wait_ge(c_in, 16 * 5)
            link(ts(bS[:, :, :], bS[:, :, :], signs[:, 0:1], None, ALU.mult))
            link(ts(cO[:, :, :], cO[:, :, :], signs[:, 1:2], None, ALU.mult))
            link(ts(cA[:, :, :], cR[:, :, :], -1.0, None, ALU.mult))
            pool.wait_ge(prep_act, 3)
            pool.wait_ge(prep_dve, 2)
            link(tt(er[:, :, :], mag[:, :, :], cs[:, :, 0:NA], ALU.mult))
            link(tt(ei[:, :, :], mag[:, :, :], sn[:, :, 0:NA], ALU.mult))
            lre, lim, den, t2, fr, fi, num = (small[:, j, :] for j in (0, 1, 10, 12, 13, 14, 15))
            ar1, ai1 = er[:, :, 1], ei[:, :, 1]
            link(ts(num, ar1, 1.0, None, ALU.subtract))
            link(tt(fr, num, lre, ALU.mult))
            link(tt(t2, ai1, lim, ALU.mult))
            link(tt(fr, fr, t2, ALU.add))
            link(tt(fr, fr, den, ALU.mult))
            link(tt(fi, ai1, lre, ALU.mult))
            link(tt(t2, num, lim, ALU.mult))
            link(tt(fi, fi, t2, ALU.subtract))
            link(tt(fi, fi, den, ALU.mult))
            frb = fr.unsqueeze(2).to_broadcast([P, G, GH])
            fib = fi.unsqueeze(2).to_broadcast([P, G, GH])
            link(tt(bb[:, :, :], frb, bO[:, :, :], ALU.mult))
            link(tt(tmpB[:, :, :], fib, bS[:, :, :], ALU.mult))
            link(tt(bb[:, :, :], bb[:, :, :], tmpB[:, :, :], ALU.add))
            link(tt(bbS[:, :, :], frb, bS[:, :, :], ALU.mult))
            link(tt(tmpB[:, :, :], fib, bO[:, :, :], ALU.mult))
            link(tt(bbS[:, :, :], bbS[:, :, :], tmpB[:, :, :], ALU.subtract))
            link(tt(winT[:], over_h(er, 0, T), over_k(bb, T), ALU.mult))
            link(tt(tmpW[:], over_h(ei, 0, T), over_k(bbS, T), ALU.mult))
            tt(winT[:], winT[:], tmpW[:], ALU.add).then_inc(winT_ready, 1)
            pool.wait_ge(winT_ready, 1)
            for q in range(4):
                gg = slice(8 * q, 8 * q + 8)

                def eight(t, c):
                    return (t[:, gg, :].unsqueeze(3).to_broadcast([P, 8, NA, GH]),
                            c[:, gg, :].unsqueeze(2).to_broadcast([P, 8, NA, GH]))

                link(tt(ce_w[:, gg], *eight(er, cO), ALU.mult))
                if q:
                    pool.wait_ge(ce_ready, q)
                link(tt(tmpC[:], *eight(ei, cA), ALU.mult))
                tt(ce_w[:, gg], ce_w[:, gg], tmpC[:], ALU.add).then_inc(ce_ready, 1)
            pool.wait_ge(win_out[0], 4)
            pool.wait_ge(win_out[1], 4)
            pool.dma_start(win_d, winS[:].rearrange("p g c -> p (g c)")).then_inc(win_stored, 16)
            pool.wait_ge(ce_ready, 4)
            pool.dma_start(ce_d, ce_w[:].rearrange("p g k h -> p (g k h)")).then_inc(stored, 16)
            pool.dma_start(dB[:].rearrange("p g h -> p (g h)"), ssm_d.partition_broadcast(GH)).then_inc(d_in, 16)
            for q in range(4):
                gg = slice(8 * q, 8 * q + 8)

                def outer(a, b):
                    return (a[:, gg, NA + NB:NK].unsqueeze(3).to_broadcast([P, 8, NB, NB]),
                            b[:, gg, NA:NA + NB].unsqueeze(2).to_broadcast([P, 8, NB, NB]))

                link(tt(cosS[:, gg], *outer(cs, cs), ALU.mult))
                link(tt(tmpR[:], *outer(sn, sn), ALU.mult))
                link(tt(cosS[:, gg], cosS[:, gg], tmpR[:], ALU.subtract))
                link(tt(sinS[:, gg], *outer(sn, cs), ALU.mult))
                link(tt(tmpR[:], *outer(cs, sn), ALU.mult))
                link(tt(sinS[:, gg], sinS[:, gg], tmpR[:], ALU.add))
            pool.dma_start(cos_d, cosS[:].rearrange("p g a b -> p (g a b)")).then_inc(stored, 16)
            pool.dma_start(sin_d, sinS[:].rearrange("p g a b -> p (g a b)")).then_inc(stored, 16)
            pool.wait_ge(d_in, 16)
            pool.wait_ge(i_in, 16)
            link(tt(dB[:], dB[:], ident[0:GH, 0:GH].unsqueeze(1).to_broadcast([GH, G, GH]), ALU.mult))
            pool.wait_ge(kt_out[0], 4)
            pool.wait_ge(kt_out[1], 4)
            link(tt(ktS[:, :, 0, :], ktS[:, :, 0, :], dB[:], ALU.add))
            pool.dma_start(kt_d, ktS[:].rearrange("p g k h -> p (g k h)")).then_inc(kt_stored, 16)

            pool.wait_ge(stored, 16 * 3)
            pool.wait_ge(win_stored, 16)
            pool.wait_ge(kt_stored, 16)
            pool.wait_ge(chunk_done, PRJ0)
            pool.dma_start(dist, dist_in).then_inc(dist_in_s, 16)
            pool.dma_start(win[:].rearrange("p g c -> p (g c)"), win_d).then_inc(tab_in[0], 16)
            pool.dma_start(cosT[:].rearrange("p g c -> p (g c)"), cos_d).then_inc(tab_in[1], 16)
            pool.dma_start(sinT[:].rearrange("p g c -> p (g c)"), sin_d).then_inc(tab_in[2], 16)
            pool.dma_start(ce[:].rearrange("p g k h -> p (g k h)"), ce_d).then_inc(tab_in[3], 16)
            pool.wait_ge(tc_done, 4)
            link(pool.memset(toep[:], 0.0))
            kt_v = kt_d.rearrange("h (g n) -> h g n", g=G)
            for r in range(T):
                n = GH * (r + 1)
                pool.dma_start(toep[GH * r:GH * (r + 1), :, P - n:P], kt_v[:, :, 0:n]).then_inc(toep_in, 16)
            pool.wait_ge(zx_ready, 4)
            pool.wait_ge(tab_in[2], 16)
            tt(zx[:], zx[:], sinT[:], ALU.mult).then_inc(zx_sin, 1)
            pool.wait_ge(gx_ready, 1)
            tt(zg[:], zg[:], sinT[:], ALU.mult).then_inc(gx_sin, 1)
            pool.wait_ge(dist_in_s, 16)
            for h in range(H):
                if h == 0:
                    pool.wait_ge(hs_ready, 1)
                elif h >= 4 and h % 2 == 0:
                    pool.wait_ge(nmx_ready, QT * (h - 2) // 2)
                slope = 2.0 ** (-8.0 * (h + 1) / H)
                pool.tensor_scalar(bias[:, h % 4, :], dist, -slope * HD ** 0.5, None,
                                   ALU.mult).then_inc(bias_ready, 1)
            for h in (0, 1):
                pool.wait_ge(rstd_ready, FIN + h + 1)
                for i in range(FIN_DVE, DT):
                    pool.wait_ge(xg_ready, i + 1 + (h if i == DT - 1 else 0))
                    tt(xg[:, i, half(h)], xg[:, i, half(h)], rstd[:, half(h)], ALU.mult).then_inc(fin_pool, 1)


def kernel(**inputs):
    import numpy as np
    import concourse.bacc as bacc
    from concourse.bass_utils import run_bass_kernel_spmd

    a = {k: np.asarray(v) for k, v in inputs.items()}

    def tiles(w):
        k, m = w.shape
        return w.reshape(k // P, P, m // P, P).transpose(2, 1, 0, 3).reshape(m // P, P, k)

    def column(v):
        return v.reshape(-1, P).T

    def states(re, im):
        return np.concatenate([np.moveaxis(re, 1, 0), np.moveaxis(im, 1, 0)])

    ffns = ("ffn1", "ffn2")
    w_in = tiles(a["w_in"][0])
    glu = tiles(a["w_ssm_glu"][0])
    q, k, v, u = (w_in[AT * i:AT * (i + 1)] for i in range(4))
    br, bi = a["ssm_b_re"][0], a["ssm_b_im"][0]
    cr, ci = (a[n][0].transpose(0, 2, 1) for n in ("ssm_c_re", "ssm_c_im"))
    lre, lim = a["ssm_lambda_re"][0], a["ssm_lambda_im"][0]
    multiples = np.concatenate([np.arange(NA), np.arange(NB), np.arange(NB)]).astype(np.float32)
    signs = np.ones((P, 2), np.float32)
    signs[:NS, 0] = signs[NS:, 1] = -1
    rows, cols = np.arange(P)[:, None], np.arange(S)[None, :]
    dist = (rows + S - P - cols).astype(np.float32)
    dist[dist < 0] = 1e30
    arrays = {
        "x": a["x"][0].reshape(S, DT, P).transpose(2, 1, 0),
        "gains": np.stack([column(a[n].reshape(-1)) for n in ("ffn1_norm", "mix_norm", "ffn2_norm", "final_norm")], 1),
        "w_up": np.stack([np.stack([tiles(a[f"{f}_w_{n}"][0]) for n in ("gate", "up")], 1) for f in ffns]),
        "w_down": np.stack([tiles(a[f"{f}_w_down"][0]) for f in ffns]),
        "w_proj": np.concatenate([u, k, q, v]),
        "w_gate": w_in[4 * AT:4 * AT + DT],
        "w_merge": np.concatenate([w_in[4 * AT + DT:], glu[:DT], glu[DT:], tiles(a["w_attn_up"][0])], 2),
        "w_out": tiles(a["w_out"][0]),
        "lam_re": states(lre, lre), "lam_im": states(lim, lim),
        "log_dt": np.broadcast_to(a["ssm_log_dt"], (P, G)),
        "b_own": states(br, bi), "b_swap": states(bi, br), "c_own": states(cr, ci), "c_swap": states(ci, cr),
        "ssm_d": a["ssm_d"][0],
        "ident": np.eye(P, dtype=np.float32), "multiples": np.broadcast_to(multiples, (P, NK)),
        "signs": signs, "dist": dist,
    }
    arrays = {n: np.ascontiguousarray(v) for n, v in arrays.items()}
    nc = bacc.Bacc("TRN2", target_bir_lowering=False, num_devices=1)
    args = [nc.dram_tensor(n, v.shape, mybir.dt.float32, kind="ExternalInput").ap() for n, v in arrays.items()]
    out = nc.dram_tensor("out", (P, DT, S), mybir.dt.float32, kind="ExternalOutput").ap()
    hybrid(nc, *args, out)
    r = run_bass_kernel_spmd(nc, [arrays], core_ids=[0])
    y = r.results[0]["out"]
    return y.reshape(P, DT, S).transpose(2, 1, 0).reshape(1, S, D)
```
